# Optimizing a Trainium2 kernel written in Bass

```python
import math
import jax, jax.numpy as jnp
from jax import lax
import numpy as np

D_MODEL = 1024
BATCH = 1
SEQ = 512
DEPTH = 2

N_MEM = 256
D_MIX = D_MODEL
D_DIFF = D_MIX // 2
N_DIFF_HEADS = 4
DIFF_V_DIM = D_DIFF // N_DIFF_HEADS
DIFF_QK_DIM = DIFF_V_DIM // 2
ROPE_DIM = DIFF_QK_DIM // 4
ROPE_THETA = 500000.0
D_GMLP = D_MIX - D_DIFF
N_GMLP_GROUPS = 4
GMLP_GROUP_DIM = D_GMLP // N_GMLP_GROUPS
CHUNK = 128
Q_BLOCK = 128
N_CROSS_HEADS = 4
CROSS_HEAD_DIM = D_MODEL // N_CROSS_HEADS
D_FF = ((8 * D_MODEL // 3 + 255) // 256) * 256
D_IN = 3 * D_DIFF + 2 * D_GMLP
NORM_EPS = 1e-6
NEG_INF = -1e30

kernel_name = 'hybrid_diffattn_gmlp_macaron'

def rms_norm(x, g):
    xf = x.astype(jnp.float32)
    y = xf * lax.rsqrt(jnp.mean(xf * xf, axis=-1, keepdims=True) + NORM_EPS)
    return (y * g.astype(jnp.float32)).astype(x.dtype)

def layer_norm(x, g, b):
    xf = x.astype(jnp.float32)
    mu = jnp.mean(xf, axis=-1, keepdims=True)
    xc = xf - mu
    y = xc * lax.rsqrt(jnp.mean(xc * xc, axis=-1, keepdims=True) + NORM_EPS)
    return (y * g.astype(jnp.float32) + b.astype(jnp.float32)).astype(x.dtype)

def swiglu(x, wgu, wd):
    gate, up = jnp.split(x @ wgu, 2, axis=-1)
    return (jax.nn.silu(gate) * up) @ wd

def rope_tables(positions):
    inv_freq = 1.0 / (ROPE_THETA ** (jnp.arange(0, ROPE_DIM, 2, dtype=jnp.float32) / ROPE_DIM))
    ang = positions.astype(jnp.float32)[..., None] * inv_freq
    return jnp.cos(ang), jnp.sin(ang)

def partial_rope(t, cos, sin):
    c = cos[:, :, None, None, :].astype(t.dtype)
    s = sin[:, :, None, None, :].astype(t.dtype)
    half = ROPE_DIM // 2
    t1 = t[..., :half]
    t2 = t[..., half:ROPE_DIM]
    return jnp.concatenate([t1 * c - t2 * s, t2 * c + t1 * s, t[..., ROPE_DIM:]], axis=-1)

def diff_attention(q, k, v, lam):
    b, s = q.shape[0], q.shape[1]
    nb = s // Q_BLOCK
    k1 = k[..., 0, :].transpose(0, 2, 1, 3)
    k2 = k[..., 1, :].transpose(0, 2, 1, 3)
    vh = v.transpose(0, 2, 1, 3)
    qb = (q * (DIFF_QK_DIM ** -0.5)).reshape(b, nb, Q_BLOCK, N_DIFF_HEADS, 2, DIFF_QK_DIM)
    qb = qb.transpose(1, 0, 3, 4, 2, 5)
    key_pos = jnp.arange(s)
    lam32 = lam.astype(jnp.float32)

    def one_block(args):
        qblk, start = args
        q_pos = start + jnp.arange(Q_BLOCK)
        causal = key_pos[None, :] <= q_pos[:, None]
        s1 = jnp.einsum('bhqd,bhkd->bhqk', qblk[:, :, 0], k1).astype(jnp.float32)
        s2 = jnp.einsum('bhqd,bhkd->bhqk', qblk[:, :, 1], k2).astype(jnp.float32)
        p1 = jax.nn.softmax(jnp.where(causal, s1, NEG_INF), axis=-1)
        p2 = jax.nn.softmax(jnp.where(causal, s2, NEG_INF), axis=-1)
        w = (p1 - lam32 * p2).astype(vh.dtype)
        return jnp.einsum('bhqk,bhkd->bhqd', w, vh)

    out = lax.map(one_block, (qb, jnp.arange(nb) * Q_BLOCK))
    return out.transpose(1, 0, 3, 2, 4).reshape(b, s, N_DIFF_HEADS, DIFF_V_DIM)

def chunked_spatial_gating(u, v, ws, bs, ln_g, ln_b):
    b, s = u.shape[0], u.shape[1]
    vn = layer_norm(v, ln_g, ln_b)
    vc = vn.reshape(b, s // CHUNK, CHUNK, N_GMLP_GROUPS, GMLP_GROUP_DIM)
    causal = jnp.tril(jnp.ones((CHUNK, CHUNK), dtype=bool))
    w = jnp.where(causal[None], ws, 0)
    mixed = jnp.einsum('gts,bnsgc->bntgc', w, vc) + bs.T[None, None, :, :, None]
    return (u * mixed.reshape(b, s, N_GMLP_GROUPS, GMLP_GROUP_DIM)).reshape(b, s, D_GMLP)

def cross_attention(hn, mem_n, wq, wkv, wo):
    b, s = hn.shape[0], hn.shape[1]
    m = mem_n.shape[1]
    q = (hn @ wq).reshape(b, s, N_CROSS_HEADS, CROSS_HEAD_DIM)
    kv = (mem_n @ wkv).reshape(b, m, 2, N_CROSS_HEADS, CROSS_HEAD_DIM)
    sc = jnp.einsum('bshd,bmhd->bhsm', q, kv[:, :, 0]).astype(jnp.float32) * (CROSS_HEAD_DIM ** -0.5)
    p = jax.nn.softmax(sc, axis=-1).astype(hn.dtype)
    o = jnp.einsum('bhsm,bmhd->bshd', p, kv[:, :, 1]).reshape(b, s, D_MODEL)
    return o @ wo

def setup_inputs(seed: int = 0) -> dict:
    key = jax.random.key(seed)
    ks = jax.random.split(key, 32)
    f32 = jnp.float32

    def nrm(k, shape, fan_in):
        return jax.random.normal(k, shape, f32) * (fan_in ** -0.5)

    def gain(k, shape):
        return 1.0 + 0.02 * jax.random.normal(k, shape, f32)

    L = DEPTH
    return {
        'x': jax.random.normal(ks[0], (BATCH, SEQ, D_MODEL), f32),
        'mem': jax.random.normal(ks[1], (BATCH, N_MEM, D_MODEL), f32),
        'positions': jnp.broadcast_to(jnp.arange(SEQ, dtype=jnp.int32)[None, :], (BATCH, SEQ)),
        'ffn1_norm': gain(ks[2], (L, D_MODEL)),
        'ffn1_wgu': nrm(ks[3], (L, D_MODEL, 2 * D_FF), D_MODEL),
        'ffn1_wd': nrm(ks[4], (L, D_FF, D_MODEL), D_FF),
        'mix_norm': gain(ks[5], (L, D_MODEL)),
        'w_in': nrm(ks[6], (L, D_MODEL, D_IN), D_MODEL),
        'lam_q1': 0.1 * jax.random.normal(ks[7], (L, DIFF_QK_DIM), f32),
        'lam_k1': 0.1 * jax.random.normal(ks[8], (L, DIFF_QK_DIM), f32),
        'lam_q2': 0.1 * jax.random.normal(ks[9], (L, DIFF_QK_DIM), f32),
        'lam_k2': 0.1 * jax.random.normal(ks[10], (L, DIFF_QK_DIM), f32),
        'subln': gain(ks[11], (L, DIFF_V_DIM)),
        'gmlp_ln_g': gain(ks[12], (L, N_GMLP_GROUPS, GMLP_GROUP_DIM)),
        'gmlp_ln_b': 0.02 * jax.random.normal(ks[13], (L, N_GMLP_GROUPS, GMLP_GROUP_DIM), f32),
        'gmlp_ws': nrm(ks[14], (L, N_GMLP_GROUPS, CHUNK, CHUNK), CHUNK),
        'gmlp_bs': gain(ks[15], (L, N_GMLP_GROUPS, CHUNK)),
        'w_out': nrm(ks[16], (L, D_MIX, D_MODEL), D_MIX),
        'cross_norm': gain(ks[17], (L, D_MODEL)),
        'mem_norm': gain(ks[18], (L, D_MODEL)),
        'cross_wq': nrm(ks[19], (L, D_MODEL, D_MODEL), D_MODEL),
        'cross_wkv': nrm(ks[20], (L, D_MODEL, 2 * D_MODEL), D_MODEL),
        'cross_wo': nrm(ks[21], (L, D_MODEL, D_MODEL), D_MODEL),
        'ffn2_norm': gain(ks[22], (L, D_MODEL)),
        'ffn2_wgu': nrm(ks[23], (L, D_MODEL, 2 * D_FF), D_MODEL),
        'ffn2_wd': nrm(ks[24], (L, D_FF, D_MODEL), D_FF),
        'final_norm': gain(ks[25], (D_MODEL,)),
    }

def reference(x, mem, positions, ffn1_norm, ffn1_wgu, ffn1_wd, mix_norm, w_in,
              lam_q1, lam_k1, lam_q2, lam_k2, subln, gmlp_ln_g, gmlp_ln_b, gmlp_ws,
              gmlp_bs, w_out, cross_norm, mem_norm, cross_wq, cross_wkv, cross_wo,
              ffn2_norm, ffn2_wgu, ffn2_wd, final_norm):
    b, s = x.shape[0], x.shape[1]
    cos, sin = rope_tables(positions)
    h = x
    for i in range(DEPTH):
        h = h + 0.5 * swiglu(rms_norm(h, ffn1_norm[i]), ffn1_wgu[i], ffn1_wd[i])

        hn = rms_norm(h, mix_norm[i])
        proj = hn @ w_in[i]
        q, k, v, gu, gv = jnp.split(
            proj, [D_DIFF, 2 * D_DIFF, 3 * D_DIFF, 3 * D_DIFF + D_GMLP], axis=-1)
        q = partial_rope(q.reshape(b, s, N_DIFF_HEADS, 2, DIFF_QK_DIM), cos, sin)
        k = partial_rope(k.reshape(b, s, N_DIFF_HEADS, 2, DIFF_QK_DIM), cos, sin)
        v = v.reshape(b, s, N_DIFF_HEADS, DIFF_V_DIM)
        lam_init = 0.8 - 0.6 * math.exp(-0.3 * i)
        lam = (jnp.exp(jnp.sum(lam_q1[i].astype(jnp.float32) * lam_k1[i].astype(jnp.float32)))
               - jnp.exp(jnp.sum(lam_q2[i].astype(jnp.float32) * lam_k2[i].astype(jnp.float32)))
               + lam_init)
        attn = diff_attention(q, k, v, lam)
        attn = (rms_norm(attn, subln[i]) * (1.0 - lam_init)).reshape(b, s, D_DIFF)

        gu = jax.nn.gelu(gu, approximate=False).reshape(b, s, N_GMLP_GROUPS, GMLP_GROUP_DIM)
        gv = jax.nn.gelu(gv, approximate=False).reshape(b, s, N_GMLP_GROUPS, GMLP_GROUP_DIM)
        gm = chunked_spatial_gating(gu, gv, gmlp_ws[i], gmlp_bs[i], gmlp_ln_g[i], gmlp_ln_b[i])

        h = h + jnp.concatenate([attn, gm], axis=-1) @ w_out[i]

        h = h + cross_attention(rms_norm(h, cross_norm[i]), rms_norm(mem, mem_norm[i]),
                                cross_wq[i], cross_wkv[i], cross_wo[i])

        h = h + 0.5 * swiglu(rms_norm(h, ffn2_norm[i]), ffn2_wgu[i], ffn2_wd[i])
    return rms_norm(h, final_norm)


_drawn_inputs = setup_inputs


def setup_inputs(seed=0):
    import zlib

    import numpy as np

    out = dict(_drawn_inputs(seed))
    spreads = {}
    factors = {'ffn1_norm': 4.313,
     'lam_q2': 5.189,
     'subln': 4.606,
     'gmlp_ln_g': 8.0,
     'gmlp_ln_b': 8.0,
     'gmlp_bs': 5.954,
     'cross_norm': 8.0,
     'mem_norm': 8.0,
     'ffn2_norm': 6.488,
     'final_norm': 2.816}
    for name, (base, spread) in spreads.items():
        noise = np.random.default_rng([zlib.crc32(name.encode()), seed]).standard_normal(out[name].shape)
        drawn = base * np.exp(spread * noise) if base else spread * noise
        out[name] = __import__('jax').numpy.asarray(drawn.astype(out[name].dtype))
    for name, factor in factors.items():
        out[name] = (out[name] * factor).astype(out[name].dtype)
    return out
```

```python
import math
from contextlib import ExitStack

import numpy as np
import concourse.bass as bass
from concourse import mybir

P = 128
D = 1024
S = 512
M = 256
LAYERS = 2
FF = 2816
KT = D // P
ST = S // P
MT = M // P
HT = FF // P
HK = HT // 2
HEADS = 4
HALF = 8
EPS = 1e-6
QK_SCALE = 64.0 ** -0.5
CROSS_SCALE = 256.0 ** -0.5
NEG = -1e30

UP1 = 0
DN1 = UP1 + HT
GV = DN1 + 16
QQ = GV + 2
KK = QQ + 2
GU = KK + 2
VV = GU + 2
CK = VV + 2
WO = CK + 4
CV = WO + 4
WQ = CV + 4
CO = WQ + 4
UP2 = CO + 4
DN2 = UP2 + HT
UNITS = DN2 + 16
assert UNITS % 2 == 0

STAGES = 4


def unit_size(u):
    return HK * P if DN1 <= u < GV or u >= DN2 else 2048


def macaron_kernel(nc, x, mem, positions, ffn1_norm, ffn1_wgu, ffn1_wd, mix_norm, w_in,
                   lam_q1, lam_k1, lam_q2, lam_k2, subln, gmlp_ln_g, gmlp_ln_b, gmlp_ws,
                   gmlp_bs, w_out, cross_norm, mem_norm, cross_wq, cross_wkv, cross_wo,
                   ffn2_norm, ffn2_wgu, ffn2_wd, final_norm, out):
    f32 = mybir.dt.float32
    f32r = mybir.dt.float32r
    i32 = mybir.dt.int32
    ALU = mybir.AluOpType
    ACT = mybir.ActivationFunctionType
    AX = mybir.AxisListType
    ds = bass.ds

    ctx = ExitStack()
    with ctx:
        def sem(name):
            return ctx.enter_context(nc.semaphore(name))

        top = [16512]

        def sb(name, shape, dt=f32, at=None):
            size = 4 * int(np.prod(shape[1:]))
            size += -size % 32
            if at is None:
                at = top[0]
                top[0] += size
            return nc.alloc_sbuf_tensor_at(name, shape, dt, offset=at)

        h = sb("h", [P, KT, S])
        hn_at = top[0]
        hn_hi = sb("hn_hi", [P, KT, S], f32r)
        hn_lo = sb("hn_lo", [P, KT, S], f32r)
        memT = sb("memT", [P, KT, M])
        raw = sb("raw", [P, 2, 2048])
        w_hi = sb("w_hi", [P, 2, 2048], f32r)
        w_lo = sb("w_lo", [P, 2, 2048], f32r)
        sumsq = sb("sumsq", [P, S])
        rb = sb("rb", [P, S])
        tmp = sb("tmp", [P, 3, S])
        ident = sb("ident", [P, P])
        ones = sb("ones", [P, P])
        ident_r = sb("ident_r", [P, P], f32r)
        mask_r = sb("mask_r", [P, P], f32r)
        wsr = sb("wsr", [P, HEADS, P])
        gains = sb("gains", [P, 90])
        rope = sb("rope", [P, ST, 2, 2 * HALF])
        rtok = sb("rtok", [P, ST])
        msq = sb("msq", [P, ST])
        m_half = sb("m_half", [P, 16])
        lam = sb("lam", [P, LAYERS])
        gsub = sb("gsub", [P, LAYERS])
        mv = sb("mv", [P, ST, HEADS, 2])
        rstd = sb("rstd", [P, ST, HEADS])
        vareps = sb("vareps", [P, ST, HEADS])
        mx = sb("mx", [P, 2, 2])
        nb = sb("nb", [P, 2, 2])
        sm = sb("sm", [P, 2, 2])
        rc = sb("rc", [P, 2, 2])
        msh = sb("msh", [P, ST])
        rh = sb("rh", [P, ST])
        cmx = sb("cmx", [P, ST])
        cnb = sb("cnb", [P, ST])
        csm = sb("csm", [P, ST])
        crc = sb("crc", [P, ST])
        crs = sb("crs", [P, ST])
        sh = top[0]
        assert sh + 2 * HT * S * 4 <= 229344, sh + 2 * HT * S * 4
        K1 = 1024
        hid_hi = sb("hid_hi", [P, HT, S], f32r, sh)
        hid_lo = sb("hid_lo", [P, HT, S], f32r, sh + 44 * K1)
        gu = sb("gu", [P, HEADS, S], f32, sh)
        wsT_hi = sb("wsT_hi", [P, HEADS, P], f32r, sh + 8 * K1)
        wsT_lo = sb("wsT_lo", [P, HEADS, P], f32r, sh + 10 * K1)
        ln_g = sb("ln_g", [P, HEADS * P], f32, sh + 12 * K1)
        ln_b = sb("ln_b", [P, HEADS * P], f32, sh + 14 * K1)
        bs_b = sb("bs_b", [P, HEADS * P], f32, sh + 16 * K1)
        bst = sb("bst", [P, ST, HEADS, 6], f32, sh + 18 * K1)
        k_tok = sb("k_tok", [P, ST, S], f32, sh + 24 * K1)
        mg_hi = sb("mg_hi", [P, KT, M], f32r, sh)
        mg_lo = sb("mg_lo", [P, KT, M], f32r, sh + 8 * K1)
        kc_hi = sb("kc_hi", [P, KT, M], f32r, sh + 16 * K1)
        kc_lo = sb("kc_lo", [P, KT, M], f32r, sh + 24 * K1)
        qT_hi = sb("qT_hi", [P, HEADS, S], f32r, sh + 32 * K1)
        qT_lo = sb("qT_lo", [P, HEADS, S], f32r, sh + 40 * K1)
        gm_hi = sb("gm_hi", [P, HEADS, S], f32r, sh + 48 * K1)
        gm_lo = sb("gm_lo", [P, HEADS, S], f32r, sh + 56 * K1)
        kT_hi = sb("kT_hi", [P, HEADS, S], f32r, sh + 64 * K1)
        kT_lo = sb("kT_lo", [P, HEADS, S], f32r, sh + 72 * K1)
        q_tok = sb("q_tok", [P, ST, S], f32, sh + 80 * K1)
        ex = sb("ex", [P, 2, 2, S], f32, sh + 80 * K1)
        v_hi = sb("v_hi", [P, ST, S], f32r, hn_at)
        v_lo = sb("v_lo", [P, ST, S], f32r, hn_at + 8 * K1)
        wT_hi = sb("wT_hi", [P, ST, S], f32r, hn_at + 16 * K1)
        wT_lo = sb("wT_lo", [P, ST, S], f32r, hn_at + 24 * K1)
        qc_hi = sb("qc_hi", [P, 2, 2, S], f32r, sh)
        qc_lo = sb("qc_lo", [P, 2, 2, S], f32r, sh + 8 * K1)
        o_hi = sb("o_hi", [P, KT, S], f32r, sh + 32 * K1)
        o_lo = sb("o_lo", [P, KT, S], f32r, sh + 48 * K1)
        vc_hi = sb("vc_hi", [P, MT, D], f32r, sh + 64 * K1)
        vc_lo = sb("vc_lo", [P, MT, D], f32r, sh + 72 * K1)
        wc_hi = sb("wc_hi", [P, MT, S], f32r, sh + 80 * K1)
        wc_lo = sb("wc_lo", [P, MT, S], f32r, sh + 84 * K1)
        x_in = sb("x_in", [P, ST, D], f32, sh)
        mem_in = sb("mem_in", [P, MT, D], f32, sh + 16 * K1)
        mem_sq = sb("mem_sq", [P, D], f32, sh + 24 * K1)
        rows = sb("rows", [90, P], f32, sh + 28 * K1)
        lam_in = sb("lam_in", [P, 4, LAYERS * 64], f32, sh + 29 * K1)
        lam_pr = sb("lam_pr", [P, 2, LAYERS, 64], f32, sh + 31 * K1)
        lam_s = sb("lam_s", [P, 2, LAYERS], f32, sh + 32 * K1)
        pos_i = sb("pos_i", [ST, P], i32, sh + 33 * K1)
        pos_f = sb("pos_f", [ST, P], f32, sh + 34 * K1)
        pos_t = sb("pos_t", [P, ST], f32, sh + 35 * K1)
        invf = sb("invf", [P, HALF], f32, sh + 36 * K1)
        ang = sb("ang", [P, 5, ST, HALF], f32, sh + 37 * K1)
        mss = sb("mss", [P, 3, MT], f32, sh + 38 * K1)
        hg = sb("hg", [P, KT, S], f32, sh)
        o_sb = sb("o_sb", [P, ST, D], f32, sh + 16 * K1)
        diag = tmp[:, 2, :].rearrange("p (t c) -> p t c", c=P)

        ps = ctx.enter_context(nc.psum_tensor("ps", [P, 8, 512], f32))

        x_loaded = sem("x_loaded")
        consts_loaded = sem("consts_loaded")
        mem_loaded = sem("mem_loaded")
        setup_pool = sem("setup_pool")
        setup_dve = sem("setup_dve")
        setup_act = sem("setup_act")
        setup_pe = sem("setup_pe")
        w_loaded = [sem("w_loaded0"), sem("w_loaded1")]
        w_rounded = sem("w_rounded")
        w_split = sem("w_split")
        w_used = sem("w_used")
        x_turned = sem("x_turned")
        mem_ms_ready = sem("mem_ms_ready")
        lam_sums_ready = sem("lam_sums_ready")
        angles_ready = sem("angles_ready")
        mem_normed = sem("mem_normed")
        memT_ready = sem("memT_ready")
        h_ready = sem("h_ready")
        hn_rounded = sem("hn_rounded")
        hn_ready = sem("hn_ready")
        sq_ready = sem("sq_ready")
        sum_ready = sem("sum_ready")
        stat_done = sem("stat_done")
        ms_ready = sem("ms_ready")
        r_ready = sem("r_ready")
        diag_ready = sem("diag_ready")
        rb_done = sem("rb_done")
        rb_ready = sem("rb_ready")
        gate_ready = sem("gate_ready")
        up_read = sem("up_read")
        silu_ready = sem("silu_ready")
        prod_ready = sem("prod_ready")
        hid_rounded = sem("hid_rounded")
        hid_ready = sem("hid_ready")
        small_loaded = sem("small_loaded")
        ws_masked = sem("ws_masked")
        gelu_ready = sem("gelu_ready")
        var_ready = sem("var_ready")
        rstd_ready = sem("rstd_ready")
        vn_final = sem("vn_final")
        vn_rounded = sem("vn_rounded")
        vn_ready = sem("vn_ready")
        qk_copied = sem("qk_copied")
        qk_roped = sem("qk_roped")
        qk_turned = sem("qk_turned")
        qkT_rounded = sem("qkT_rounded")
        qkT_ready = sem("qkT_ready")
        ws_turned = sem("ws_turned")
        wsT_rounded = sem("wsT_rounded")
        wsT_ready = sem("wsT_ready")
        gu_scaled = sem("gu_scaled")
        gu_ready = sem("gu_ready")
        mix_done = sem("mix_done")
        gm_final = sem("gm_final")
        gm_rounded = sem("gm_rounded")
        gm_ready = sem("gm_ready")
        v_rounded = sem("v_rounded")
        v_ready = sem("v_ready")
        mg_rounded = sem("mg_rounded")
        mg_ready = sem("mg_ready")
        sc_done = sem("sc_done")
        nb_ready = sem("nb_ready")
        exp_done = sem("exp_done")
        attn_w_ready = sem("attn_w_ready")
        attn_w_turned = sem("attn_w_turned")
        wT_rounded = sem("wT_rounded")
        wT_ready = sem("wT_ready")
        pv_done = sem("pv_done")
        osq_ready = sem("osq_ready")
        ostat_done = sem("ostat_done")
        oms_ready = sem("oms_ready")
        rh_ready = sem("rh_ready")
        odiag_ready = sem("odiag_ready")
        orb_done = sem("orb_done")
        orb_ready = sem("orb_ready")
        attn_final = sem("attn_final")
        attn_rounded = sem("attn_rounded")
        attn_ready = sem("attn_ready")
        kc_rounded = sem("kc_rounded")
        kc_ready = sem("kc_ready")
        vc_rounded = sem("vc_rounded")
        vc_ready = sem("vc_ready")
        qc_rounded = sem("qc_rounded")
        qc_ready = sem("qc_ready")
        csc_done = sem("csc_done")
        cnb_ready = sem("cnb_ready")
        cexp_done = sem("cexp_done")
        cw_ready = sem("cw_ready")
        cw_turned = sem("cw_turned")
        wc_rounded = sem("wc_rounded")
        wc_ready = sem("wc_ready")
        cpv_done = sem("cpv_done")
        o_rounded = sem("o_rounded")
        o_ready = sem("o_ready")
        dve_chain = sem("dve_chain")
        hg_ready = sem("hg_ready")
        fin_turned = sem("fin_turned")
        fin_ready = sem("fin_ready")
        out_stored = sem("out_stored")

        CHAIN = ST * 4 + 2 * ST + ST + 16 * 4 + 1 + 2 * HEADS

        def unit_no(L, u, i=0, per=2):
            return L * UNITS + u + per * i

        def used(L, u, i=0, per=2):
            return unit_no(L, u, i, per) + 3

        def tile_no(L, stage, m):
            return KT + (L * STAGES + stage) * KT + m + 1

        def hn_no(L, stage, t):
            return (L * STAGES + stage) * KT + t + 1

        def sum_no(L, stage, m):
            return 9 + (L * STAGES + stage) * 9 + m + 2

        def ffn_no(L, f, j):
            return (L * 2 + f) * HT + j + 1

        def wait_apart(eng, signal, value):
            eng.compute_val(value)
            eng.wait_ge(setup_pool, 1)
            eng.wait_ge(signal, value)

        def down_loop(eng, body):
            with eng.Fori(0, KT // 2 - 1) as i:
                body(i, False)
            body(KT // 2 - 1, True)

        def up_loop(eng, body):
            body(0, "first")
            with eng.Fori(1, HT // 2 - 1) as i:
                body(i, "")
            body(HT // 2 - 1, "last")

        block = ctx.enter_context(nc.Block())

        @block.sync
        def _(sp):
            def load(L, u, i, per, parts):
                wait_apart(sp, w_split, unit_no(L, u, i, per) + 1)
                for (a, k, c, src) in parts:
                    dst = raw[:, u % 2, a:a + k * c].rearrange("p (k c) -> p k c", c=c)
                    sp.dma_start(dst, src.rearrange("o (k p) c -> (o p) k c", p=P))\
                      .then_inc(w_loaded[u % 2], 16)

            def ffn_loads(L, up, dn, wgu, wd):
                with sp.Fori(0, HT // 2) as i:
                    for s in range(2):
                        col = i * (2 * P) + s * P
                        load(L, up + s, i, 2, [(0, KT, P, wgu[ds(L, 1), :, ds(col, P)]),
                                               (1024, KT, P, wgu[ds(L, 1), :, ds(col + FF, P)])])
                with sp.Fori(0, KT) as m:
                    for s in range(2):
                        k0 = s * HK
                        load(L, dn + s, m, 2,
                             [(0, 6, P, wd[ds(L, 1), k0 * P:(k0 + 6) * P, ds(m * P, P)]),
                              (768, HK - 6, P, wd[ds(L, 1), (k0 + 6) * P:(k0 + HK) * P, ds(m * P, P)])])

            def token_loads(L, u, w, col):
                for s in range(2):
                    load(L, u + s, 0, 2,
                         [(n * 1024, 2, 512, w[ds(L, 1), (4 * s + 2 * n) * P:(4 * s + 2 * n + 2) * P, col:col + 512])
                          for n in range(2)])

            def feature_loads(L, u, w, col, n_units):
                for t in range(n_units):
                    c0 = col + t * 256
                    load(L, u + t, 0, 2,
                         [(n * 1024, 4, 256, w[ds(L, 1), n * 512:(n + 1) * 512, c0:c0 + 256]) for n in range(2)])

            for t in range(ST):
                sp.dma_start(x_in[:, t, :], x[0, t * P:(t + 1) * P, :]).then_inc(x_loaded, 16)
            with sp.Fori(0, LAYERS) as L:
                ffn_loads(L, UP1, DN1, ffn1_wgu, ffn1_wd)
                token_loads(L, GV, w_in, 2048)
                token_loads(L, QQ, w_in, 0)
                token_loads(L, KK, w_in, 512)
                feature_loads(L, GU, w_in, 1536, 2)
                token_loads(L, VV, w_in, 1024)
                feature_loads(L, CK, cross_wkv, 0, 4)
                feature_loads(L, WO, w_out, 0, 4)
                token_loads(L, CV, cross_wkv, D)
                token_loads(L, CV + 2, cross_wkv, D + 512)
                feature_loads(L, WQ, cross_wq, 0, 4)
                feature_loads(L, CO, cross_wo, 0, 4)
                ffn_loads(L, UP2, DN2, ffn2_wgu, ffn2_wd)
            for t in range(ST):
                sp.wait_ge(fin_ready, t + 1)
                sp.dma_start(out[0, t * P:(t + 1) * P, :], o_sb[:, t, :]).then_inc(out_stored, 16)
            sp.wait_ge(out_stored, 16 * ST)

        @block.gpsimd
        def _(pool):
            pool.memset(ident[:, :], 0.0).then_inc(setup_pool, 1)
            pool.memset(ones[:, :], 1.0).then_inc(setup_pool, 1)
            pool.memset(rb[:, 0:P], 0.0).then_inc(setup_pool, 1)
            pool.memset(m_half[:, :], -0.5).then_inc(setup_pool, 1)
            pool.wait_ge(setup_pool, 4)
            pool.affine_select(out=ident[:, :], in_=ident[:, :], compare_op=ALU.not_equal, fill=1.0,
                               base=0, pattern=[[-1, P]], channel_multiplier=1).then_inc(setup_pool, 1)
            pool.affine_select(out=rb[:, 0:P], in_=rb[:, 0:P], compare_op=ALU.is_ge, fill=NEG,
                               base=0, pattern=[[-1, P]], channel_multiplier=1).then_inc(setup_pool, 1)

            def clear_sum(first_sum):
                pool.memset(sumsq[:, :], 0.0).then_inc(sum_ready, 1)

            def add_square(sq_no, before, m2):
                pool.wait_ge(sq_ready, sq_no)
                pool.wait_ge(sum_ready, before)
                pool.tensor_tensor(out=sumsq[:, :], in0=sumsq[:, :], in1=tmp[:, m2, :], op=ALU.add)\
                    .then_inc(sum_ready, 1)

            def inverse_rms(n):
                pool.wait_ge(ms_ready, n)
                pool.tensor_tensor(out=rtok[:, :], in0=msq[:, :], in1=m_half[:, 0:ST], op=ALU.pow)\
                    .then_inc(r_ready, 1)

            clear_sum(0)
            for m in range(KT):
                add_square(m + 1, m + 1, m % 2)
            pool.wait_ge(mem_ms_ready, 1)
            pool.tensor_tensor(out=mss[:, 2, :], in0=mss[:, 1, :], in1=m_half[:, 0:MT], op=ALU.pow)\
                .then_inc(setup_pool, 1)

            def stage_sums(L, stage, stats_before):
                wait_apart(pool, stat_done, L * 4 + stats_before)
                clear_sum(0)
                if stage in (0, 3):
                    def body(i, last):
                        for b in range(2):
                            m = 2 * i + b
                            add_square(tile_no(L, stage, m), sum_no(L, stage, m) - 1, b)
                    down_loop(pool, body)
                else:
                    for m in range(KT):
                        add_square(tile_no(L, stage, m), sum_no(L, stage, m) - 1, m % 2)

            with pool.Fori(0, LAYERS) as L:
                inverse_rms(L * 4 + 1)
                stage_sums(L, 0, 1)
                inverse_rms(L * 4 + 2)
                wait_apart(pool, small_loaded, L * 64 + 64)
                pool.affine_select(out=wsr[:, :, :], in_=wsr[:, :, :], compare_op=ALU.is_ge, fill=0.0,
                                   base=0, pattern=[[0, HEADS], [-1, P]], channel_multiplier=1)\
                    .then_inc(ws_masked, 1)
                pool.wait_ge(var_ready, L + 1)
                pool.tensor_tensor(out=rstd[:, :, :], in0=vareps[:, :, :],
                                   in1=m_half[:, :].rearrange("p (a b) -> p a b", b=HEADS), op=ALU.pow)\
                    .then_inc(rstd_ready, 1)
                for hd in range(HEADS):
                    pool.wait_ge(oms_ready, L * 4 + hd + 1)
                    pool.tensor_tensor(out=rh[:, :], in0=msh[:, :], in1=m_half[:, 0:ST], op=ALU.pow)\
                        .then_inc(rh_ready, 1)
                stage_sums(L, 1, 2)
                inverse_rms(L * 4 + 3)
                stage_sums(L, 2, 3)
                inverse_rms(L * 4 + 4)
                stage_sums(L, 3, 4)
            inverse_rms(LAYERS * 4 + 1)

        @block.scalar
        def _(act):
            n_consts = 0

            def load_const(dst, src):
                nonlocal n_consts
                n_consts += 1
                act.dma_start(dst, src).then_inc(consts_loaded, 16)

            for n, g in enumerate([ffn1_norm, mix_norm, cross_norm, ffn2_norm, mem_norm]):
                for l in range(LAYERS):
                    load_const(rows[l * 40 + n * 8:l * 40 + n * 8 + 8, :], g[l].rearrange("(t p) -> t p", p=P))
            load_const(rows[80:88, :], final_norm.rearrange("(t p) -> t p", p=P))
            load_const(rows[88:90, :], subln)
            load_const(pos_i[:, :], positions[0].rearrange("(t p) -> t p", p=P))
            for n, v in enumerate([lam_q1, lam_k1, lam_q2, lam_k2]):
                load_const(lam_in[:, n, :], v.rearrange("l d -> (l d)").unsqueeze(0).to_broadcast([P, LAYERS * 64]))
            assert n_consts == 17
            for t in range(MT):
                act.dma_start(mem_in[:, t, :], mem[0, t * P:(t + 1) * P, :]).then_inc(mem_loaded, 16)

            act.wait_ge(setup_pool, 6)
            act.activation(ident_r[:, :], ident[:, :], ACT.Copy).then_inc(setup_act, 1)
            act.activation(mask_r[:, :], rb[:, 0:P], ACT.Copy).then_inc(setup_act, 1)

            def round_unit(L, u, i=0, per=2):
                n = unit_no(L, u, i, per)
                s = u % 2
                act.wait_ge(w_loaded[s], 32 * (L * (UNITS // 2) + u // 2 + (per // 2) * i + 1))
                act.wait_ge(w_used, n + 1)
                z = unit_size(u)
                act.activation(w_hi[:, s, 0:z], raw[:, s, 0:z], ACT.Copy).then_inc(w_rounded, 1)

            def round_tile(no, m, gcol):
                wait_apart(act, h_ready, no)
                act.activation(hn_hi[:, ds(m, 1), :], h[:, ds(m, 1), :], ACT.Copy,
                               scale=gains[:, ds(gcol, 1)]).then_inc(hn_rounded, 1)

            def square_tile(m, b, sum_before):
                if sum_before is not None:
                    wait_apart(act, sum_ready, sum_before)
                act.activation(tmp[:, b:b + 1, :], h[:, ds(m, 1), :], ACT.Square).then_inc(sq_ready, 1)

            def copy_rb(n, bank):
                act.wait_ge(rb_done, n)
                act.activation(rb[:, :], ps[:, bank, :], ACT.Copy).then_inc(rb_ready, 1)

            for m in range(KT):
                round_tile(m + 1, m, m)
                square_tile(m, m % 2, m if m >= 2 else None)
            for t in range(MT):
                act.wait_ge(mem_loaded, 16 * MT)
                if t:
                    act.wait_ge(setup_act, 2 + t)
                act.activation(mem_sq[:, :], mem_in[:, t, :], ACT.Square, accum_out=mss[:, 0, t:t + 1])\
                   .then_inc(setup_act, 1)
            act.wait_ge(lam_sums_ready, 1)
            act.activation(lam_s[:, :, :], lam_s[:, :, :], ACT.Exp).then_inc(setup_act, 1)
            act.wait_ge(angles_ready, 1)
            act.activation(ang[:, 3, :, :], ang[:, 1, :, :], ACT.Sin).then_inc(setup_act, 1)
            act.activation(ang[:, 4, :, :], ang[:, 2, :, :], ACT.Sin).then_inc(setup_act, 1)

            def ffn(L, f, up, dn, stage, rb_no, next_gain, next_unit):
                def up_body(i, where):
                    if where == "first":
                        copy_rb(rb_no, 7)
                    for s in range(2):
                        u = up + s
                        if where == "last":
                            round_unit(L, dn + s)
                        else:
                            round_unit(L, u + 2, i)
                        n = ffn_no(L, f, 2 * i + s)
                        act.wait_ge(gate_ready, n)
                        act.activation(tmp[:, 1, :], tmp[:, 0, :], ACT.Silu).then_inc(silu_ready, 1)
                        wait_apart(act, prod_ready, n)
                        act.activation(hid_hi[:, ds(2 * i + s, 1), :], tmp[:, 1:2, :], ACT.Copy)\
                           .then_inc(hid_rounded, 1)
                up_loop(act, up_body)

                def down_body(i, last):
                    for b in range(2):
                        m = 2 * i + b
                        no = tile_no(L, stage, m)
                        at_end = last and b == 1
                        for s in range(2):
                            if s == 1:
                                round_tile(no, m, L * 40 + next_gain + m)
                            if not at_end:
                                round_unit(L, dn + 2 * b + 2 + s, i, 4)
                            elif next_unit is not None:
                                round_unit(L, next_unit + s)
                        square_tile(m, b, sum_no(L, stage, m) - 2)
                down_loop(act, down_body)

            with act.Fori(0, LAYERS) as L:
                round_unit(L, 0)
                round_unit(L, 1)
                ffn(L, 0, UP1, DN1, 0, L * 3 + 1, 8, GV)

                act.wait_ge(hn_ready, hn_no(L, 1, KT - 1))
                act.dma_start(wsr[:, :, :], gmlp_ws[ds(L, 1)].rearrange("o g t s -> (o t) g s")).then_inc(small_loaded, 16)
                for dst, src in ((ln_g, gmlp_ln_g), (ln_b, gmlp_ln_b), (bs_b, gmlp_bs)):
                    act.dma_start(dst[:, :], src[ds(L, 1)].rearrange("o g c -> o (g c)").to_broadcast([P, HEADS * P]))\
                       .then_inc(small_loaded, 16)

                round_unit(L, QQ)
                round_unit(L, QQ + 1)
                act.wait_ge(w_used, used(L, GV + 1))
                act.wait_ge(r_ready, L * 4 + 2)
                for t in range(ST):
                    act.activation(k_tok[:, t, :], ps[:, t, :], ACT.Gelu, scale=rtok[:, t:t + 1])\
                       .then_inc(gelu_ready, 1)
                round_unit(L, KK)
                for t in range(ST):
                    act.wait_ge(vn_final, L * 4 + t + 1)
                    act.activation(gm_hi[:, :, t * P:(t + 1) * P],
                                   k_tok[:, t, :].rearrange("p (g c) -> p g c", c=P), ACT.Copy)\
                       .then_inc(vn_rounded, 1)
                round_unit(L, KK + 1)
                act.wait_ge(w_used, used(L, QQ + 1))
                for t in range(ST):
                    act.activation(q_tok[:, t, :], ps[:, 4 + t, :], ACT.Copy, scale=rtok[:, t:t + 1])\
                       .then_inc(qk_copied, 1)
                round_unit(L, GU)
                copy_rb(L * 3 + 2, 4)
                act.wait_ge(ws_turned, L + 1)
                act.activation(wsT_hi[:, :, :], ps[:, 5, :].rearrange("p (g c) -> p g c", c=P), ACT.Copy)\
                   .then_inc(wsT_rounded, 1)
                round_unit(L, GU + 1)
                act.wait_ge(w_used, used(L, KK + 1))
                act.wait_ge(vn_ready, L * 4 + 4)
                for t in range(ST):
                    act.activation(k_tok[:, t, :], ps[:, t, :], ACT.Copy, scale=rtok[:, t:t + 1])\
                       .then_inc(qk_copied, 1)

                def gelu_gu(half):
                    act.wait_ge(gu_scaled, L * 2 + half + 1)
                    act.activation(gu[:, 2 * half:2 * half + 2, :], gu[:, 2 * half:2 * half + 2, :], ACT.Gelu)\
                       .then_inc(gu_ready, 1)

                def round_turned(n, dst):
                    act.wait_ge(qk_turned, L * 8 + n + 1)
                    t = n % ST
                    act.activation(dst[:, :, t * P:(t + 1) * P],
                                   ps[:, t, :].rearrange("p (g c) -> p g c", c=P), ACT.Copy)\
                       .then_inc(qkT_rounded, 1)

                round_unit(L, VV)
                gelu_gu(0)
                for t in range(ST):
                    round_turned(t, qT_hi)
                round_unit(L, VV + 1)
                gelu_gu(1)
                for t in range(ST):
                    round_turned(ST + t, kT_hi)
                for t in range(ST):
                    act.wait_ge(gm_final, L * 4 + t + 1)
                    act.activation(gm_hi[:, :, t * P:(t + 1) * P],
                                   tmp[:, t % 2, :].rearrange("p (g c) -> p g c", c=P), ACT.Copy)\
                       .then_inc(gm_rounded, 1)
                for m in range(KT):
                    if m == 0:
                        wait_apart(act, gm_ready, L * 4 + 4)
                    act.activation(mg_hi[:, m, :], memT[:, m, :], ACT.Copy, scale=gains[:, ds(L * 40 + 32 + m, 1)])\
                       .then_inc(mg_rounded, 1)
                round_unit(L, CK)
                round_unit(L, CK + 1)
                act.wait_ge(w_used, used(L, VV + 1))
                for t in range(ST):
                    act.activation(v_hi[:, t, :], ps[:, t, :], ACT.Copy, scale=rtok[:, t:t + 1])\
                       .then_inc(v_rounded, 1)

                for s in range(22):
                    if 2 <= s < 18:
                        n = s - 2
                        qb = n % 4
                        act.wait_ge(attn_w_turned, L * 16 + n + 1)
                        if qb == 0 and n:
                            act.wait_ge(pv_done, L * 4 + n // 4)
                        act.activation(wT_hi[:, 0:qb + 1, qb * P:(qb + 1) * P],
                                       ps[:, 0, 0:(qb + 1) * P].rearrange("p (k c) -> p k c", c=P), ACT.Copy)\
                           .then_inc(wT_rounded, 1)
                    if s < 16:
                        qb, b = s % 4, s % 2
                        N = (qb + 1) * P
                        act.wait_ge(nb_ready, L * 16 + s + 1)
                        if s >= 2:
                            act.wait_ge(attn_w_turned, L * 16 + s - 1)
                        for br in range(2):
                            last = act.activation(ex[:, b, br, 0:N], ps[:, 4 + 2 * b + br, 0:N], ACT.Exp,
                                                  bias=nb[:, b, br:br + 1], scale=QK_SCALE,
                                                  accum_out=sm[:, b, br:br + 1])
                        last.then_inc(exp_done, 1)
                    if s >= 4 and s % 4 == 0 and s <= 16:
                        hd = s // 4 - 1
                        act.wait_ge(w_used, used(L, CK + hd))
                        act.activation(kc_hi[:, 2 * hd:2 * hd + 2, :],
                                       ps[:, 2, :].rearrange("p (k c) -> p k c", c=M), ACT.Copy)\
                           .then_inc(kc_rounded, 1)
                        round_unit(L, CK + hd + 2)
                    if s >= 5:
                        hd, part = divmod(s - 5, 4)
                        if part == 0 and hd < 4:
                            act.wait_ge(pv_done, L * 4 + hd + 1)
                            if hd:
                                act.wait_ge(attn_ready, L * 4 + hd)
                            act.activation(tmp[:, 0, :], ps[:, 1, :], ACT.Square).then_inc(osq_ready, 1)
                        if part == 2:
                            act.wait_ge(orb_done, L * 4 + hd + 1)
                            act.activation(tmp[:, 1, :], ps[:, 3, :], ACT.Copy).then_inc(orb_ready, 1)
                        if part == 3:
                            act.wait_ge(attn_final, L * 4 + hd + 1)
                            act.activation(qT_hi[:, hd, :], tmp[:, 0, :], ACT.Copy).then_inc(attn_rounded, 1)

                def projected(stage, u, gcol, after):
                    for t in range(4):
                        for b in range(2):
                            round_tile(tile_no(L, stage, 2 * t + b), 2 * t + b, L * 40 + gcol + 2 * t + b)
                        round_unit(L, u + t + 2)
                        for b in range(2):
                            m = 2 * t + b
                            square_tile(m, b, sum_no(L, stage, m) - 2)

                projected(1, WO, 16, CV)

                for c in range(2):
                    round_unit(L, CV + 2 * c + 2)
                    act.wait_ge(w_used, used(L, CV + 2 * c + 1))
                    for t in range(MT):
                        last = act.activation(vc_hi[:, t, c * 512:(c + 1) * 512], ps[:, 2 * c + t, :], ACT.Copy)
                    last.then_inc(vc_rounded, 1)
                    round_unit(L, CV + 2 * c + 3)

                def round_qc(hd):
                    b = hd % 2
                    act.wait_ge(w_used, used(L, WQ + hd))
                    act.activation(qc_hi[:, b, :, :], ps[:, 4 + 2 * b:6 + 2 * b, :], ACT.Copy).then_inc(qc_rounded, 1)
                    round_unit(L, WQ + hd + 2)

                def cross_exp(hd):
                    act.wait_ge(cnb_ready, L * 4 + hd + 1)
                    if hd:
                        act.wait_ge(cw_turned, L * 4 + hd)
                    for qb in range(ST):
                        last = act.activation(tmp[:, qb // 2, (qb % 2) * M:(qb % 2 + 1) * M],
                                              ps[:, qb // 2, (qb % 2) * M:(qb % 2 + 1) * M], ACT.Exp,
                                              bias=cnb[:, qb:qb + 1], scale=crs[:, qb:qb + 1],
                                              accum_out=csm[:, qb:qb + 1])
                    last.then_inc(cexp_done, 1)

                round_qc(0)
                cross_exp(0)
                round_qc(1)
                for hd in range(HEADS):
                    act.wait_ge(cw_turned, L * 4 + hd + 1)
                    if hd:
                        act.wait_ge(cpv_done, L * 4 + hd)
                    act.activation(wc_hi[:, :, :], ps[:, 2:4, :], ACT.Copy).then_inc(wc_rounded, 1)
                    if hd < 3:
                        cross_exp(hd + 1)
                    act.wait_ge(cpv_done, L * 4 + hd + 1)
                    act.activation(o_hi[:, 2 * hd:2 * hd + 2, :], ps[:, 2:4, :], ACT.Copy).then_inc(o_rounded, 1)
                    if hd < 2:
                        round_qc(hd + 2)

                projected(2, CO, 24, UP2)
                ffn(L, 1, UP2, DN2, 3, L * 3 + 3, 40, None)

            for t in range(ST):
                act.wait_ge(fin_turned, t + 1)
                act.wait_ge(r_ready, LAYERS * 4 + 1)
                b = 2 * (t % 2)
                act.activation(o_sb[:, t, :].rearrange("p (a c) -> p a c", c=512), ps[:, b:b + 2, :], ACT.Copy,
                               scale=rtok[:, t:t + 1]).then_inc(fin_ready, 1)

        @block.vector
        def _(dve):
            def split_unit(L, u, i=0, per=2):
                s = u % 2
                dve.wait_ge(w_rounded, unit_no(L, u, i, per) + 1)
                z = unit_size(u)
                dve.tensor_tensor(out=w_lo[:, s, 0:z], in0=raw[:, s, 0:z], in1=w_hi[:, s, 0:z].bitcast(f32),
                                  op=ALU.subtract).then_inc(w_split, 1)

            def add_tile(products, m, bank, factor):
                dve.wait_ge(w_used, products)
                dve.scalar_tensor_tensor(out=h[:, ds(m, 1), :], in0=ps[:, bank:bank + 1, :], scalar=factor,
                                         in1=h[:, ds(m, 1), :], op0=ALU.mult, op1=ALU.add).then_inc(h_ready, 1)

            def low_tile(no, m, gcol):
                dve.wait_ge(hn_rounded, no)
                dve.scalar_tensor_tensor(out=hn_lo[:, ds(m, 1), :], in0=h[:, ds(m, 1), :],
                                         scalar=gains[:, ds(gcol, 1)],
                                         in1=hn_hi[:, ds(m, 1), :].bitcast(f32),
                                         op0=ALU.mult, op1=ALU.subtract).then_inc(hn_ready, 1)

            def mean_square(n, bank):
                dve.wait_ge(stat_done, n)
                dve.tensor_scalar(msq[:, :], ps[:, bank, 0:ST], 1.0 / D, EPS, ALU.mult, ALU.add)\
                   .then_inc(ms_ready, 1)

            def make_diag(r_no):
                dve.wait_ge(r_ready, r_no)
                for t in range(ST):
                    last = dve.tensor_scalar(diag[:, t, :], ident[:, :], rtok[:, t:t + 1], None, ALU.mult)
                last.then_inc(diag_ready, 1)

            done = [0]

            def setup(ins):
                done[0] += 1
                ins.then_inc(setup_dve, 1)
                dve.wait_ge(setup_dve, done[0])

            dve.memset(msh[:, :], 0.0).then_inc(w_split, 2)
            dve.memset(rh[:, :], 0.0).then_inc(w_used, 2)
            inv = (1.0 / np.power(np.float32(500000.0), np.arange(0, 16, 2, dtype=np.float32) / np.float32(16))).astype(np.float32)
            for j in range(HALF):
                setup(dve.memset(invf[:, j:j + 1], float(inv[j])))
            dve.wait_ge(consts_loaded, 16 * 17)
            setup(dve.tensor_copy(pos_f[:, :], pos_i[:, :]))
            dve.wait_ge(setup_pe, 1)
            setup(dve.tensor_copy(gains[:, :], ps[:, 6, 0:90]))
            dve.wait_ge(setup_pe, 2)
            setup(dve.tensor_copy(pos_t[:, :], ps[:, 7, 0:ST]))
            for m in range(KT):
                dve.wait_ge(x_turned, m + 1)
                dve.tensor_copy(h[:, m, :], ps[:, m % 4, :]).then_inc(h_ready, 1)
                low_tile(m + 1, m, m)
            for t in range(ST):
                setup(dve.tensor_scalar(ang[:, 0, t, :], invf[:, :], pos_t[:, t:t + 1], None, ALU.mult))
            magic = float(1.5 * 2 ** 23)
            setup(dve.tensor_scalar(ang[:, 1, :, :], ang[:, 0, :, :], 1.0 / (2 * math.pi), None, ALU.mult))
            setup(dve.tensor_scalar(ang[:, 1, :, :], ang[:, 1, :, :], magic, None, ALU.add))
            setup(dve.tensor_scalar(ang[:, 1, :, :], ang[:, 1, :, :], -magic, None, ALU.add))
            c1 = 6.28125
            c2 = float(round((2 * math.pi - c1) * 2 ** 20) / 2 ** 20)
            c3 = 2 * math.pi - c1 - c2
            for c in (c1, c2, c3):
                setup(dve.scalar_tensor_tensor(out=ang[:, 0, :, :], in0=ang[:, 1, :, :], scalar=-c,
                                               in1=ang[:, 0, :, :], op0=ALU.mult, op1=ALU.add))
            setup(dve.tensor_scalar(ang[:, 1, :, :], ang[:, 0, :, :], 3.1415925, -3.1415925, ALU.min, ALU.max))
            setup(dve.tensor_scalar(ang[:, 2, :, :], ang[:, 1, :, :], -1.0, None, ALU.mult))
            setup(dve.tensor_tensor(out=ang[:, 2, :, :], in0=ang[:, 2, :, :], in1=ang[:, 1, :, :], op=ALU.max))
            dve.tensor_scalar(ang[:, 2, :, :], ang[:, 2, :, :], -1.0, math.pi / 2, ALU.mult, ALU.add).then_inc(angles_ready, 1)
            for n in range(2):
                setup(dve.tensor_tensor(out=lam_pr[:, n, :, :],
                                        in0=lam_in[:, 2 * n, :].rearrange("p (l d) -> p l d", d=64),
                                        in1=lam_in[:, 2 * n + 1, :].rearrange("p (l d) -> p l d", d=64), op=ALU.mult))
            dve.tensor_reduce(lam_s[:, :, :], lam_pr[:, :, :, :], AX.X, ALU.add).then_inc(lam_sums_ready, 1)
            for l in range(LAYERS):
                setup(dve.tensor_scalar(gsub[:, l:l + 1], gains[:, 88 + l:89 + l],
                                        1.0 - (0.8 - 0.6 * math.exp(-0.3 * l)), None, ALU.mult))
            dve.wait_ge(setup_act, 4)
            dve.tensor_scalar(mss[:, 1, :], mss[:, 0, :], 1.0 / D, EPS, ALU.mult, ALU.add).then_inc(mem_ms_ready, 1)
            dve.wait_ge(setup_pool, 7)
            for t in range(MT):
                last = dve.tensor_scalar(mem_in[:, t, :], mem_in[:, t, :], mss[:, 2, t:t + 1], None, ALU.mult)
            last.then_inc(mem_normed, 1)
            dve.wait_ge(setup_act, 5)
            setup(dve.tensor_tensor(out=lam[:, :], in0=lam_s[:, 0, :], in1=lam_s[:, 1, :], op=ALU.subtract))
            for l in range(LAYERS):
                setup(dve.tensor_scalar(lam[:, l:l + 1], lam[:, l:l + 1], 0.8 - 0.6 * math.exp(-0.3 * l), None, ALU.add))
            dve.wait_ge(setup_act, 7)
            for a, src in ((0, 4), (1, 3)):
                for b in range(2):
                    setup(dve.tensor_copy(rope[:, :, a, b * HALF:(b + 1) * HALF], ang[:, src, :, :]))
            for m in range(KT // 2):
                dve.wait_ge(setup_pe, 3 + m)
                dve.tensor_copy(memT[:, 2 * m:2 * m + 2, :],
                                ps[:, 4 + m % 2, :].rearrange("p (k c) -> p k c", c=M)).then_inc(memT_ready, 1)

            def ffn(L, f, up, dn, stage, stat_no, next_gain, next_unit):
                def up_body(i, where):
                    if where == "first":
                        mean_square(stat_no, 6)
                        make_diag(stat_no)
                        dve.wait_ge(rb_ready, L * 3 + (1 if f == 0 else 3))
                    for s in range(2):
                        n = ffn_no(L, f, 2 * i + s)
                        dve.wait_ge(w_used, used(L, up + s, i))
                        dve.tensor_tensor(out=tmp[:, 0, :], in0=ps[:, 2 * s, :], in1=rb[:, :], op=ALU.mult)\
                           .then_inc(gate_ready, 1)
                        dve.tensor_tensor(out=tmp[:, 2, :], in0=ps[:, 2 * s + 1, :], in1=rb[:, :], op=ALU.mult)\
                           .then_inc(up_read, 1)
                        if where == "last":
                            split_unit(L, dn + s)
                        else:
                            split_unit(L, up + s + 2, i)
                        dve.wait_ge(silu_ready, n)
                        dve.wait_ge(up_read, n)
                        dve.tensor_tensor(out=tmp[:, 1, :], in0=tmp[:, 1, :], in1=tmp[:, 2, :], op=ALU.mult)\
                           .then_inc(prod_ready, 1)
                        dve.wait_ge(hid_rounded, n)
                        dve.tensor_tensor(out=hid_lo[:, ds(2 * i + s, 1), :], in0=tmp[:, 1:2, :],
                                          in1=hid_hi[:, ds(2 * i + s, 1), :].bitcast(f32), op=ALU.subtract)\
                           .then_inc(hid_ready, 1)
                up_loop(dve, up_body)

                def down_body(i, last):
                    for b in range(2):
                        m = 2 * i + b
                        no = tile_no(L, stage, m)
                        at_end = last and b == 1
                        for s in range(2):
                            if s == 1:
                                add_tile(used(L, dn + 2 * b + 1, i, 4), m, 4 + b, 0.5)
                                low_tile(no, m, L * 40 + next_gain + m)
                            if not at_end:
                                split_unit(L, dn + 2 * b + 2 + s, i, 4)
                            elif next_unit is not None:
                                split_unit(L, next_unit + s)
                down_loop(dve, down_body)

            with dve.Fori(0, LAYERS) as L:
                count = [0]

                def link(ins):
                    count[0] += 1
                    ins.then_inc(dve_chain, 1)
                    dve.wait_ge(dve_chain, L * CHAIN + count[0])

                split_unit(L, 0)
                split_unit(L, 1)
                ffn(L, 0, UP1, DN1, 0, L * 4 + 1, 8, GV)

                split_unit(L, QQ)
                split_unit(L, QQ + 1)
                mean_square(L * 4 + 2, 7)
                dve.wait_ge(small_loaded, L * 64 + 64)
                for t in range(ST):
                    dve.wait_ge(gelu_ready, L * 4 + t + 1)
                    for g in range(HEADS):
                        last = dve.bn_stats(bst[:, t, g, :], k_tok[:, t, g * P:(g + 1) * P])
                    count[0] += 1
                    last.then_inc(dve_chain, 1)
                    wait_apart(dve, dve_chain, L * CHAIN + count[0])
                    for g in range(HEADS):
                        last = dve.bn_aggr(mv[:, t, g, :], bst[:, t, g, :])
                    link(last)
                dve.tensor_scalar(vareps[:, :, :], mv[:, :, :, 1], EPS, None, ALU.add).then_inc(var_ready, 1)
                make_diag(L * 4 + 2)
                split_unit(L, KK)
                dve.wait_ge(rstd_ready, L + 1)
                for t in range(ST):
                    for g in range(HEADS):
                        last = dve.tensor_scalar(k_tok[:, t, g * P:(g + 1) * P], k_tok[:, t, g * P:(g + 1) * P],
                                                 mv[:, t, g, 0:1], rstd[:, t, g:g + 1], ALU.subtract, ALU.mult)
                    link(last)
                    link(dve.tensor_tensor(out=k_tok[:, t, :], in0=k_tok[:, t, :], in1=ln_g[:, :], op=ALU.mult))
                    dve.tensor_tensor(out=k_tok[:, t, :], in0=k_tok[:, t, :], in1=ln_b[:, :], op=ALU.add)\
                       .then_inc(vn_final, 1)
                for t in range(ST):
                    dve.wait_ge(vn_rounded, L * 4 + t + 1)
                    dve.tensor_tensor(out=gm_lo[:, :, t * P:(t + 1) * P],
                                      in0=k_tok[:, t, :].rearrange("p (g c) -> p g c", c=P),
                                      in1=gm_hi[:, :, t * P:(t + 1) * P].bitcast(f32), op=ALU.subtract)\
                       .then_inc(vn_ready, 1)
                split_unit(L, KK + 1)

                def rotate(n, tok):
                    t = n % ST
                    dve.wait_ge(qk_copied, L * 8 + n + 1)
                    part = tok[:, t, :].rearrange("p (h d) -> p h d", d=64)[:, :, 0:2 * HALF]
                    a = tmp[:, 0, 0:P].rearrange("p (h d) -> p h d", d=2 * HALF)
                    b = tmp[:, 1, 0:P].rearrange("p (h d) -> p h d", d=2 * HALF)
                    cos, sin = (rope[:, t, i:i + 1, :].to_broadcast([P, 8, 2 * HALF]) for i in range(2))
                    dve.tensor_tensor(out=a, in0=part, in1=cos, op=ALU.mult)
                    link(dve.tensor_tensor(out=b, in0=part, in1=sin, op=ALU.mult))
                    dve.tensor_tensor(out=part[:, :, 0:HALF], in0=a[:, :, 0:HALF], in1=b[:, :, HALF:], op=ALU.subtract)
                    dve.tensor_tensor(out=part[:, :, HALF:], in0=a[:, :, HALF:], in1=b[:, :, 0:HALF], op=ALU.add)\
                       .then_inc(qk_roped, 1)
                    dve.wait_ge(qk_roped, L * 8 + n + 1)

                for t in range(ST):
                    rotate(t, q_tok)
                split_unit(L, GU)
                dve.wait_ge(wsT_rounded, L + 1)
                dve.tensor_tensor(out=wsT_lo[:, :, :], in0=ps[:, 5, :].rearrange("p (g c) -> p g c", c=P),
                                  in1=wsT_hi[:, :, :].bitcast(f32), op=ALU.subtract).then_inc(wsT_ready, 1)
                split_unit(L, GU + 1)
                for t in range(ST):
                    rotate(ST + t, k_tok)

                def scale_gu(half, bank):
                    dve.wait_ge(w_used, used(L, GU + half))
                    if half == 0:
                        dve.wait_ge(rb_ready, L * 3 + 2)
                    for b in range(2):
                        last = dve.tensor_tensor(out=gu[:, 2 * half + b, :], in0=ps[:, bank + b, :], in1=rb[:, :],
                                                 op=ALU.mult)
                    last.then_inc(gu_scaled, 1)

                def low_turned(n, hi, lo):
                    dve.wait_ge(qkT_rounded, L * 8 + n + 1)
                    t = n % ST
                    dve.tensor_tensor(out=lo[:, :, t * P:(t + 1) * P],
                                      in0=ps[:, t, :].rearrange("p (g c) -> p g c", c=P),
                                      in1=hi[:, :, t * P:(t + 1) * P].bitcast(f32), op=ALU.subtract)\
                       .then_inc(qkT_ready, 1)

                split_unit(L, VV)
                scale_gu(0, 6)
                for t in range(ST):
                    low_turned(t, qT_hi, qT_lo)
                split_unit(L, VV + 1)
                scale_gu(1, 4)
                for t in range(ST):
                    low_turned(ST + t, kT_hi, kT_lo)
                for t in range(ST):
                    dve.wait_ge(mix_done, L * 4 + t + 1)
                    if t == 0:
                        dve.wait_ge(gu_ready, L * 2 + 2)
                    if t >= 2:
                        dve.wait_ge(gm_ready, L * 4 + t - 1)
                    link(dve.tensor_tensor(out=tmp[:, t % 2, :], in0=ps[:, 6 + t % 2, :], in1=bs_b[:, :], op=ALU.add))
                    dve.tensor_tensor(out=tmp[:, t % 2, :].rearrange("p (g c) -> p g c", c=P),
                                      in0=tmp[:, t % 2, :].rearrange("p (g c) -> p g c", c=P),
                                      in1=gu[:, :, t * P:(t + 1) * P], op=ALU.mult).then_inc(gm_final, 1)
                    dve.wait_ge(gm_rounded, L * 4 + t + 1)
                    dve.tensor_tensor(out=gm_lo[:, :, t * P:(t + 1) * P],
                                      in0=tmp[:, t % 2, :].rearrange("p (g c) -> p g c", c=P),
                                      in1=gm_hi[:, :, t * P:(t + 1) * P].bitcast(f32), op=ALU.subtract)\
                       .then_inc(gm_ready, 1)
                for m in range(KT):
                    dve.wait_ge(mg_rounded, L * 8 + m + 1)
                    dve.scalar_tensor_tensor(out=mg_lo[:, m, :], in0=memT[:, m, :],
                                             scalar=gains[:, ds(L * 40 + 32 + m, 1)],
                                             in1=mg_hi[:, m, :].bitcast(f32), op0=ALU.mult, op1=ALU.subtract)\
                       .then_inc(mg_ready, 1)
                split_unit(L, CK)
                split_unit(L, CK + 1)
                for t in range(ST):
                    dve.wait_ge(v_rounded, L * 4 + t + 1)
                    dve.scalar_tensor_tensor(out=v_lo[:, t, :], in0=ps[:, t, :], scalar=rtok[:, t:t + 1],
                                             in1=v_hi[:, t, :].bitcast(f32), op0=ALU.mult, op1=ALU.subtract)\
                       .then_inc(v_ready, 1)

                for s in range(22):
                    if s >= 5:
                        hd, part = divmod(s - 5, 4)
                        if part == 0 and hd >= 1:
                            dve.wait_ge(attn_rounded, L * 4 + hd)
                            dve.tensor_tensor(out=qT_lo[:, hd - 1, :], in0=tmp[:, 0, :],
                                              in1=qT_hi[:, hd - 1, :].bitcast(f32), op=ALU.subtract)\
                               .then_inc(attn_ready, 1)
                        if part == 2:
                            dve.wait_ge(rh_ready, L * 4 + hd + 1)
                            for t in range(ST):
                                last = dve.tensor_scalar(diag[:, t, :], ident[:, :], rh[:, t:t + 1], None, ALU.mult)
                            last.then_inc(odiag_ready, 1)
                    if 2 <= s < 18:
                        n = s - 2
                        qb = n % 4
                        dve.wait_ge(wT_rounded, L * 16 + n + 1)
                        dve.tensor_tensor(out=wT_lo[:, 0:qb + 1, qb * P:(qb + 1) * P],
                                          in0=ps[:, 0, 0:(qb + 1) * P].rearrange("p (k c) -> p k c", c=P),
                                          in1=wT_hi[:, 0:qb + 1, qb * P:(qb + 1) * P].bitcast(f32),
                                          op=ALU.subtract).then_inc(wT_ready, 1)
                    if s < 16:
                        qb, b = s % 4, s % 2
                        N = (qb + 1) * P
                        dve.wait_ge(sc_done, L * 16 + s + 1)
                        link(dve.tensor_reduce(mx[:, b, :], ps[:, 4 + 2 * b:6 + 2 * b, 0:N], AX.X, ALU.max))
                        dve.tensor_scalar(nb[:, b, :], mx[:, b, :], -QK_SCALE, None, ALU.mult).then_inc(nb_ready, 1)
                    if 1 <= s < 17:
                        n = s - 1
                        qb, b = n % 4, n % 2
                        N = (qb + 1) * P
                        dve.wait_ge(exp_done, L * 16 + n + 1)
                        link(dve.reciprocal(rc[:, b, :], sm[:, b, :]))
                        link(dve.tensor_tensor(out=rc[:, b, 1:2], in0=rc[:, b, 1:2], in1=lam[:, ds(L, 1)], op=ALU.mult))
                        link(dve.tensor_scalar(ex[:, b, 1, 0:N], ex[:, b, 1, 0:N], rc[:, b, 1:2], None, ALU.mult))
                        dve.scalar_tensor_tensor(out=ex[:, b, 0, 0:N], in0=ex[:, b, 0, 0:N], scalar=rc[:, b, 0:1],
                                                 in1=ex[:, b, 1, 0:N], op0=ALU.mult, op1=ALU.subtract)\
                           .then_inc(attn_w_ready, 1)
                    if s >= 4 and s % 4 == 0 and s <= 16:
                        hd = s // 4 - 1
                        dve.wait_ge(kc_rounded, L * 4 + hd + 1)
                        dve.tensor_tensor(out=kc_lo[:, 2 * hd:2 * hd + 2, :],
                                          in0=ps[:, 2, :].rearrange("p (k c) -> p k c", c=M),
                                          in1=kc_hi[:, 2 * hd:2 * hd + 2, :].bitcast(f32), op=ALU.subtract)\
                           .then_inc(kc_ready, 1)
                        split_unit(L, CK + hd + 2)
                    if s >= 5:
                        hd, part = divmod(s - 5, 4)
                        if part == 1:
                            dve.wait_ge(ostat_done, L * 4 + hd + 1)
                            dve.tensor_scalar(msh[:, :], ps[:, 3, 0:ST], 1.0 / P, EPS, ALU.mult, ALU.add)\
                               .then_inc(oms_ready, 1)
                        if part == 3:
                            dve.wait_ge(orb_ready, L * 4 + hd + 1)
                            dve.scalar_tensor_tensor(out=tmp[:, 0, :], in0=ps[:, 1, :], scalar=gsub[:, ds(L, 1)],
                                                     in1=tmp[:, 1, :], op0=ALU.mult, op1=ALU.mult)\
                               .then_inc(attn_final, 1)

                def projected(stage, u, gcol):
                    for t in range(4):
                        for b in range(2):
                            add_tile(used(L, u + t), 2 * t + b, 4 + 2 * (t % 2) + b, 1.0)
                        for b in range(2):
                            low_tile(tile_no(L, stage, 2 * t + b), 2 * t + b, L * 40 + gcol + 2 * t + b)
                        split_unit(L, u + t + 2)

                projected(1, WO, 16)

                for c in range(2):
                    split_unit(L, CV + 2 * c + 2)
                    dve.wait_ge(vc_rounded, L * 2 + c + 1)
                    for t in range(MT):
                        last = dve.tensor_tensor(out=vc_lo[:, t, c * 512:(c + 1) * 512], in0=ps[:, 2 * c + t, :],
                                                 in1=vc_hi[:, t, c * 512:(c + 1) * 512].bitcast(f32), op=ALU.subtract)
                    last.then_inc(vc_ready, 1)
                    split_unit(L, CV + 2 * c + 3)
                    if c == 0:
                        mean_square(L * 4 + 3, 6)
                dve.wait_ge(r_ready, L * 4 + 3)
                link(dve.tensor_scalar(crs[:, :], rtok[:, :], CROSS_SCALE, None, ALU.mult))

                def low_qc(hd):
                    b = hd % 2
                    dve.wait_ge(qc_rounded, L * 4 + hd + 1)
                    dve.tensor_tensor(out=qc_lo[:, b, :, :], in0=ps[:, 4 + 2 * b:6 + 2 * b, :],
                                      in1=qc_hi[:, b, :, :].bitcast(f32), op=ALU.subtract).then_inc(qc_ready, 1)
                    split_unit(L, WQ + hd + 2)

                def cross_max(hd):
                    dve.wait_ge(csc_done, L * 4 + hd + 1)
                    link(dve.tensor_reduce(cmx[:, :], ps[:, 0:2, :].rearrange("p a (b m) -> p (a b) m", m=M),
                                           AX.X, ALU.max))
                    dve.scalar_tensor_tensor(out=cnb[:, :], in0=cmx[:, :], scalar=-1.0, in1=crs[:, :],
                                             op0=ALU.mult, op1=ALU.mult).then_inc(cnb_ready, 1)

                def cross_norm_w(hd):
                    dve.wait_ge(cexp_done, L * 4 + hd + 1)
                    link(dve.reciprocal(crc[:, :], csm[:, :]))
                    for qb in range(ST):
                        part = tmp[:, qb // 2, (qb % 2) * M:(qb % 2 + 1) * M]
                        last = dve.tensor_scalar(part, part, crc[:, qb:qb + 1], None, ALU.mult)
                    last.then_inc(cw_ready, 1)

                low_qc(0)
                cross_max(0)
                cross_norm_w(0)
                low_qc(1)
                for hd in range(HEADS):
                    dve.wait_ge(wc_rounded, L * 4 + hd + 1)
                    dve.tensor_tensor(out=wc_lo[:, :, :], in0=ps[:, 2:4, :], in1=wc_hi[:, :, :].bitcast(f32),
                                      op=ALU.subtract).then_inc(wc_ready, 1)
                    if hd < 3:
                        cross_max(hd + 1)
                        cross_norm_w(hd + 1)
                    dve.wait_ge(o_rounded, L * 4 + hd + 1)
                    dve.tensor_tensor(out=o_lo[:, 2 * hd:2 * hd + 2, :], in0=ps[:, 2:4, :],
                                      in1=o_hi[:, 2 * hd:2 * hd + 2, :].bitcast(f32), op=ALU.subtract)\
                       .then_inc(o_ready, 1)
                    if hd < 2:
                        low_qc(hd + 2)

                projected(2, CO, 24)
                ffn(L, 1, UP2, DN2, 3, L * 4 + 4, 40, None)
                assert count[0] == CHAIN, count[0]

            mean_square(LAYERS * 4 + 1, 6)
            for m in range(KT):
                dve.tensor_scalar(hg[:, m, :], h[:, m, :], gains[:, 80 + m:81 + m], None, ALU.mult)\
                   .then_inc(hg_ready, 1)

        @block.tensor
        def _(pe):
            def product(dst, a_hi, a_lo, b_hi, b_lo, start, stop, extra=None):
                pe.matmul(dst, a_hi, b_hi, start=start, stop=False)
                if extra:
                    extra()
                pe.matmul(dst, a_hi, b_lo, start=False, stop=False)
                return pe.matmul(dst, a_lo, b_hi, start=False, stop=stop)

            def wait_unit(L, u, i=0, per=2):
                pe.wait_ge(w_split, unit_no(L, u, i, per) + 3)

            def wtile(u, a, n=P):
                return w_hi[:, u % 2, a:a + n], w_lo[:, u % 2, a:a + n]

            def token_sums(sum_no_, bank):
                pe.wait_ge(sum_ready, sum_no_)
                for t in range(ST):
                    last = pe.matmul(ps[:, bank, t:t + 1], sumsq[:, t * P:(t + 1) * P], ones[:, 0:1],
                                     start=True, stop=True)
                last.then_inc(stat_done, 1)

            def broadcast(bank, done_sem):
                for t in range(ST):
                    last = pe.matmul(ps[:, bank, t * P:(t + 1) * P], ones[:, :], diag[:, t, :], start=True, stop=True)
                last.then_inc(done_sem, 1)

            pe.wait_ge(setup_pool, 6)
            pe.wait_ge(consts_loaded, 16 * 17)
            pe.transpose(ps[:, 6, 0:90], rows[:, :], ident[0:90, 0:90]).then_inc(setup_pe, 1)
            pe.wait_ge(setup_dve, 9)
            pe.transpose(ps[:, 7, 0:ST], pos_f[:, :], ident[0:ST, 0:ST]).then_inc(setup_pe, 1)
            pe.wait_ge(x_loaded, 16 * ST)
            for m in range(KT):
                if m >= 4:
                    pe.wait_ge(h_ready, m - 3)
                for t in range(ST):
                    last = pe.transpose(ps[:, m % 4, t * P:(t + 1) * P], x_in[:, t, m * P:(m + 1) * P], ident[:, :])
                last.then_inc(x_turned, 1)
            pe.wait_ge(mem_normed, 1)
            for m in range(KT // 2):
                if m >= 2:
                    pe.wait_ge(memT_ready, m - 1)
                for a in range(2):
                    for t in range(MT):
                        last = pe.transpose(ps[:, 4 + m % 2, a * M + t * P:a * M + (t + 1) * P],
                                            mem_in[:, t, (2 * m + a) * P:(2 * m + a + 1) * P], ident[:, :])
                last.then_inc(setup_pe, 1)

            def ffn(L, f, up, dn, stage):
                def up_unit(i, s, hook=None, waits=False):
                    u = up + s
                    wait_unit(L, u, i)
                    if not waits:
                        pe.wait_ge(up_read, ffn_no(L, f, 2 * i + s) - 2)
                    for k in range(KT):
                        if waits:
                            pe.wait_ge(hn_ready, hn_no(L, stage, k))
                        if hook and k == 4:
                            hook()
                        for g in range(2):
                            a_hi, a_lo = wtile(u, g * 1024 + k * P)
                            last = product(ps[:, 2 * s + g, :], a_hi, a_lo, hn_hi[:, k, :], hn_lo[:, k, :],
                                           k == 0, k == KT - 1)
                    last.then_inc(w_used, 1)
                    return last

                def send_rb():
                    pe.wait_ge(diag_ready, L * 3 + (1 if f == 0 else 3))
                    broadcast(7, rb_done)

                def body(i, where):
                    first = where == "first"
                    up_unit(i, 0, None, first)
                    if first:
                        token_sums(9 + (L * STAGES + stage) * 9, 6)
                    up_unit(i, 1, send_rb if first else None, first)
                up_loop(pe, body)

                def down_body(i, last_two):
                    for b in range(2):
                        m = 2 * i + b
                        pe.wait_ge(h_ready, tile_no(L, stage, m) - 2)
                        for s in range(2):
                            u = dn + 2 * b + s
                            wait_unit(L, u, i, 4)
                            pe.wait_ge(hid_ready, ffn_no(L, f, HK * (s + 1) - 1))
                            for k in range(HK):
                                a_hi, a_lo = wtile(u, k * P)
                                kk = s * HK + k
                                last = product(ps[:, 4 + b, :], a_hi, a_lo, hid_hi[:, kk, :], hid_lo[:, kk, :],
                                               kk == 0, kk == HT - 1)
                            last.then_inc(w_used, 1)
                down_loop(pe, down_body)

            def head_norm(L, hd, part):
                if part == 1:
                    pe.wait_ge(osq_ready, L * 4 + hd + 1)
                    for t in range(ST):
                        last = pe.matmul(ps[:, 3, t:t + 1], tmp[:, 0, t * P:(t + 1) * P], ones[:, 0:1],
                                         start=True, stop=True)
                    last.then_inc(ostat_done, 1)
                if part == 2:
                    pe.wait_ge(odiag_ready, L * 4 + hd + 1)
                    broadcast(3, orb_done)

            def token_unit(L, u, s, bank, n_tok, src_hi, src_lo, stage=None, wait=None):
                wait_unit(L, u)
                for k4 in range(4):
                    k = 4 * s + k4
                    if stage is not None:
                        pe.wait_ge(hn_ready, hn_no(L, stage, k))
                    w1, w2 = wtile(u, k4 * 512, 512)
                    for t in range(n_tok):
                        if wait and k == 0:
                            wait(t)
                        last = product(ps[:, bank + t, :], src_hi[:, k, t * P:(t + 1) * P],
                                       src_lo[:, k, t * P:(t + 1) * P], w1, w2, k == 0, k == KT - 1)
                return last.then_inc(w_used, 1)

            def feature_unit(L, u, bank, ks, src, first=True, last_part=True, before=None):
                for k in ks:
                    if before:
                        before(k)
                    s_hi, s_lo = src(k)
                    for b in range(2):
                        a_hi, a_lo = wtile(u, k * 256 + b * P)
                        last = product(ps[:, bank + b, :], a_hi, a_lo, s_hi, s_lo,
                                       first and k == ks[0], last_part and k == ks[-1])
                return last

            with pe.Fori(0, LAYERS) as L:
                ffn(L, 0, UP1, DN1, 0)

                for s in range(2):
                    token_unit(L, GV + s, s, 0, ST, hn_hi, hn_lo, stage=1)
                token_sums(9 + (L * STAGES + 1) * 9, 7)
                def after_ms(t):
                    if t == 3:
                        pe.wait_ge(ms_ready, L * 4 + 2)
                for s in range(2):
                    token_unit(L, QQ + s, s, 4, ST, hn_hi, hn_lo, wait=after_ms)
                for s in range(2):
                    token_unit(L, KK + s, s, 0, ST, hn_hi, hn_lo,
                               wait=lambda t: pe.wait_ge(gelu_ready, L * 4 + t + 1))
                pe.wait_ge(qk_copied, L * 8 + 4)
                pe.wait_ge(diag_ready, L * 3 + 2)
                broadcast(4, rb_done)
                pe.wait_ge(ws_masked, L + 1)
                for g in range(HEADS):
                    last = pe.transpose(ps[:, 5, g * P:(g + 1) * P], wsr[:, g, :], ident[:, :])
                last.then_inc(ws_turned, 1)
                hn_tile = lambda k: (hn_hi[:, k, :], hn_lo[:, k, :])
                wait_unit(L, GU)
                last = feature_unit(L, GU, 6, range(KT), hn_tile)
                last.then_inc(w_used, 1)

                def turn(n, tok):
                    t = n % ST
                    pe.wait_ge(qk_roped, L * 8 + n + 1)
                    if n < ST:
                        pe.wait_ge(qk_copied, L * 8 + ST + t + 1)
                    else:
                        pe.wait_ge(qkT_ready, L * 8 + t + 1)
                    for hd in range(HEADS):
                        last = pe.transpose(ps[:, t, hd * P:(hd + 1) * P], tok[:, t, hd * P:(hd + 1) * P], ident[:, :])
                    last.then_inc(qk_turned, 1)

                for t in range(ST):
                    turn(t, q_tok)
                wait_unit(L, GU + 1)
                pe.wait_ge(rb_ready, L * 3 + 2)
                pe.wait_ge(wsT_ready, L + 1)
                last = feature_unit(L, GU + 1, 4, range(KT), hn_tile)
                last.then_inc(w_used, 1)
                for t in range(ST):
                    turn(ST + t, k_tok)
                for t in range(ST):
                    pe.wait_ge(vn_ready, L * 4 + t + 1)
                    if t == 0:
                        pe.wait_ge(gu_scaled, L * 2 + 1)
                    if t < 2:
                        for g in range(HEADS):
                            c = slice(t * P, (t + 1) * P)
                            last = product(ps[:, 6 + t % 2, g * P:(g + 1) * P], gm_hi[:, g, c], gm_lo[:, g, c],
                                           wsT_hi[:, g, :], wsT_lo[:, g, :], True, True)
                        last.then_inc(mix_done, 1)
                for s in range(2):
                    token_unit(L, VV + s, s, 0, ST, hn_hi, hn_lo,
                               wait=lambda t: pe.wait_ge(qkT_ready, L * 8 + 4 + t + 1))
                    t = 2 + s
                    pe.wait_ge(gm_final, L * 4 + t - 1)
                    for g in range(HEADS):
                        c = slice(t * P, (t + 1) * P)
                        last = product(ps[:, 6 + t % 2, g * P:(g + 1) * P], gm_hi[:, g, c], gm_lo[:, g, c],
                                       wsT_hi[:, g, :], wsT_lo[:, g, :], True, True)
                    last.then_inc(mix_done, 1)

                for s in range(19):
                    if s < 16:
                        hd, qb, b = s // 4, s % 4, s % 2
                        N = (qb + 1) * P
                        if s == 0:
                            pe.wait_ge(gu_scaled, L * 2 + 2)
                        if s == 1:
                            pe.wait_ge(gm_final, L * 4 + 4)
                        if s >= 2:
                            pe.wait_ge(exp_done, L * 16 + s - 1)
                        for br in range(2):
                            r = slice(64 * br, 64 * br + 64)
                            bank = 4 + 2 * b + br
                            q = slice(qb * P, (qb + 1) * P)

                            def mask():
                                pe.matmul(ps[:, bank, N - P:N], ident_r[:, :], mask_r[:, :], start=False, stop=False)
                            last = product(ps[:, bank, 0:N], qT_hi[r, hd, q], qT_lo[r, hd, q],
                                           kT_hi[r, hd, 0:N], kT_lo[r, hd, 0:N], True, True, extra=mask)
                        last.then_inc(sc_done, 1)
                        if qb == 0:
                            wait_unit(L, CK + hd)
                            if hd:
                                pe.wait_ge(kc_ready, L * 4 + hd)
                            else:
                                pe.wait_ge(v_ready, L * 4 + 4)
                        c = qb // 2
                        for k in range(4 * (qb % 2), 4 * (qb % 2) + 4):
                            if s < 2:
                                pe.wait_ge(mg_ready, L * 8 + k + 1)
                            a_hi, a_lo = wtile(CK + hd, k * 256 + c * P)
                            last = product(ps[:, 2, c * M:(c + 1) * M], a_hi, a_lo, mg_hi[:, k, :], mg_lo[:, k, :],
                                           k == 0, k == KT - 1)
                        if qb == 3:
                            last.then_inc(w_used, 1)
                    if s >= 5:
                        hd, part = divmod(s - 5, 4)
                        if part == 0 and hd < 4:
                            pe.wait_ge(wT_ready, L * 16 + 4 * hd + 4)
                            if hd:
                                pe.wait_ge(attn_final, L * 4 + hd)
                            for kb in range(ST):
                                c = slice(hd * P, (hd + 1) * P)
                                last = product(ps[:, 1, kb * P:512], v_hi[:, kb, c], v_lo[:, kb, c],
                                               wT_hi[:, kb, kb * P:512], wT_lo[:, kb, kb * P:512], kb == 0, kb == 3)
                            last.then_inc(pv_done, 1)
                    if 1 <= s < 17:
                        n = s - 1
                        qb, b = n % 4, n % 2
                        pe.wait_ge(attn_w_ready, L * 16 + n + 1)
                        if n:
                            pe.wait_ge(wT_ready, L * 16 + n)
                        for kb in range(qb + 1):
                            last = pe.transpose(ps[:, 0, kb * P:(kb + 1) * P], ex[:, b, 0, kb * P:(kb + 1) * P],
                                                ident[:, :])
                        last.then_inc(attn_w_turned, 1)
                    if s >= 5:
                        head_norm(L, *divmod(s - 5, 4))

                def cat_tile(k):
                    return (gm_hi[:, k - 4, :], gm_lo[:, k - 4, :]) if k >= 4 else (qT_hi[:, k, :], qT_lo[:, k, :])

                for t in range(4):
                    wait_unit(L, WO + t)
                    if t >= 2:
                        pe.wait_ge(h_ready, tile_no(L, 1, 2 * t - 3))
                    if t == 0:
                        feature_unit(L, WO, 4, [4, 5, 6, 7, 0, 1], cat_tile, last_part=False,
                                     before=lambda k: pe.wait_ge(attn_ready, L * 4 + k + 1) if k < 4 else None)
                        head_norm(L, 3, 2)
                        last = feature_unit(L, WO, 4, [2, 3], cat_tile, first=False,
                                            before=lambda k: pe.wait_ge(attn_ready, L * 4 + k + 1))
                    else:
                        last = feature_unit(L, WO + t, 4 + 2 * (t % 2), range(KT), cat_tile)
                    last.then_inc(w_used, 1)

                for c in range(2):
                    for s in range(2):
                        token_unit(L, CV + 2 * c + s, s, 2 * c, MT, mg_hi, mg_lo)
                    if c == 0:
                        token_sums(9 + (L * STAGES + 2) * 9, 6)

                def queries(hd):
                    wait_unit(L, WQ + hd)
                    if hd == 1:
                        pe.wait_ge(ms_ready, L * 4 + 3)
                    if hd >= 2:
                        pe.wait_ge(qc_ready, L * 4 + hd - 1)
                    last = feature_unit(L, WQ + hd, 4 + 2 * (hd % 2), range(KT), hn_tile,
                                        before=(lambda k: pe.wait_ge(hn_ready, hn_no(L, 2, k))) if hd == 0 else None)
                    last.then_inc(w_used, 1)

                def cross_scores(hd):
                    pe.wait_ge(qc_ready, L * 4 + hd + 1)
                    if hd:
                        pe.wait_ge(cexp_done, L * 4 + hd)
                    else:
                        pe.wait_ge(vc_ready, L * 2 + 2)
                    for qb in range(ST):
                        for d in range(2):
                            q = slice(qb * P, (qb + 1) * P)
                            last = product(ps[:, qb // 2, (qb % 2) * M:(qb % 2 + 1) * M],
                                           qc_hi[:, hd % 2, d, q], qc_lo[:, hd % 2, d, q],
                                           kc_hi[:, 2 * hd + d, :], kc_lo[:, 2 * hd + d, :], d == 0, d == 1)
                    last.then_inc(csc_done, 1)

                def cross_turn(hd):
                    pe.wait_ge(cw_ready, L * 4 + hd + 1)
                    if hd:
                        pe.wait_ge(o_ready, L * 4 + hd)
                    for t in range(MT):
                        for qb in range(ST):
                            c0 = (qb % 2) * M + t * P
                            last = pe.transpose(ps[:, 2 + t, qb * P:(qb + 1) * P], tmp[:, qb // 2, c0:c0 + P], ident[:, :])
                    last.then_inc(cw_turned, 1)

                def cross_values(hd):
                    pe.wait_ge(wc_ready, L * 4 + hd + 1)
                    for d in range(2):
                        for t in range(MT):
                            c = slice(hd * 256 + d * P, hd * 256 + (d + 1) * P)
                            last = product(ps[:, 2 + d, :], vc_hi[:, t, c], vc_lo[:, t, c],
                                           wc_hi[:, t, :], wc_lo[:, t, :], t == 0, t == 1)
                    last.then_inc(cpv_done, 1)

                queries(0)
                cross_scores(0)
                queries(1)
                for hd in range(HEADS):
                    cross_turn(hd)
                    if hd < 3:
                        cross_scores(hd + 1)
                    cross_values(hd)
                    if hd < 2:
                        queries(hd + 2)

                o_tile = lambda k: (o_hi[:, k, :], o_lo[:, k, :])
                for t in range(4):
                    wait_unit(L, CO + t)
                    if t >= 2:
                        pe.wait_ge(h_ready, tile_no(L, 2, 2 * t - 3))
                    last = feature_unit(L, CO + t, 4 + 2 * (t % 2), range(KT), o_tile,
                                        before=(lambda k: pe.wait_ge(o_ready, L * 4 + k // 2 + 1)) if t == 0 else None)
                    last.then_inc(w_used, 1)

                ffn(L, 1, UP2, DN2, 3)

            token_sums(9 + LAYERS * STAGES * 9, 6)
            pe.wait_ge(hg_ready, KT)
            for t in range(ST):
                if t >= 2:
                    pe.wait_ge(fin_ready, t - 1)
                for m in range(KT):
                    last = pe.transpose(ps[:, 2 * (t % 2) + m // 4, (m % 4) * P:(m % 4 + 1) * P],
                                        hg[:, m, t * P:(t + 1) * P], ident[:, :])
                last.then_inc(fin_turned, 1)


_INS = ['x', 'mem', 'positions', 'ffn1_norm', 'ffn1_wgu', 'ffn1_wd', 'mix_norm', 'w_in', 'lam_q1', 'lam_k1',
        'lam_q2', 'lam_k2', 'subln', 'gmlp_ln_g', 'gmlp_ln_b', 'gmlp_ws', 'gmlp_bs', 'w_out', 'cross_norm',
        'mem_norm', 'cross_wq', 'cross_wkv', 'cross_wo', 'ffn2_norm', 'ffn2_wgu', 'ffn2_wd', 'final_norm']


def kernel(**inputs):
    import numpy as _np
    import concourse.bacc as _bacc
    from concourse import mybir as _mybir
    from concourse.bass_utils import run_bass_kernel_spmd as _run

    nc = _bacc.Bacc("TRN2", target_bir_lowering=False, num_devices=1)
    arrays, args = {}, []
    for name in _INS:
        a = _np.ascontiguousarray(inputs[name])
        arrays[f"in_{name}_dram"] = a
        args.append(nc.dram_tensor(f"in_{name}_dram", a.shape, _mybir.dt.from_np(a.dtype), kind="ExternalInput").ap())
    args.append(nc.dram_tensor("out_dram", (1, S, D), _mybir.dt.float32, kind="ExternalOutput").ap())
    macaron_kernel(nc, *args)
    r = _run(nc, [arrays], core_ids=[0])
    return r.results[0]["out_dram"]
```

```python
import math
from contextlib import ExitStack

import numpy as np
import concourse.bass as bass
from concourse import mybir

P = 128
D = 1024
S = 512
M = 256
LAYERS = 2
FF = 2816
KT = D // P
ST = S // P
MT = M // P
HT = FF // P
HK = HT // 2
HEADS = 4
HALF = 8
EPS = 1e-6
QK_SCALE = 64.0 ** -0.5
CROSS_SCALE = 256.0 ** -0.5
NEG = -1e30

UP1 = 0
DN1 = UP1 + HT
GV = DN1 + 16
QQ = GV + 2
KK = QQ + 2
GU = KK + 2
VV = GU + 2
CK = VV + 2
CV = CK + 4
WO = CV + 4
WQ = WO + 4
CO = WQ + 4
UP2 = CO + 4
DN2 = UP2 + HT
UNITS = DN2 + 16
assert UNITS % 2 == 0

STAGES = 4


G_FFN1, G_FINAL, G_MIX, G_CROSS, G_FFN2, G_MEM, G_SUBLN = 0, 16, 24, 40, 56, 72, 88


def unit_size(u):
    u %= UNITS
    return HK * P if DN1 <= u < GV or u >= DN2 else 2048


def macaron_kernel(nc, x, mem, positions, ffn1_norm, ffn1_wgu, ffn1_wd, mix_norm, w_in,
                   lam_q1, lam_k1, lam_q2, lam_k2, subln, gmlp_ln_g, gmlp_ln_b, gmlp_ws,
                   gmlp_bs, w_out, cross_norm, mem_norm, cross_wq, cross_wkv, cross_wo,
                   ffn2_norm, ffn2_wgu, ffn2_wd, final_norm, out):
    f32 = mybir.dt.float32
    f32r = mybir.dt.float32r
    i32 = mybir.dt.int32
    ALU = mybir.AluOpType
    ACT = mybir.ActivationFunctionType
    AX = mybir.AxisListType
    ds = bass.ds

    ctx = ExitStack()
    with ctx:
        def sem(name):
            return ctx.enter_context(nc.semaphore(name))

        top = [16512]

        def sb(name, shape, dt=f32, at=None):
            size = 4 * int(np.prod(shape[1:]))
            size += -size % 32
            if at is None:
                at = top[0]
                top[0] += size
            return nc.alloc_sbuf_tensor_at(name, shape, dt, offset=at)

        h = sb("h", [P, KT, S])
        hn_at = top[0]
        hn_hi = sb("hn_hi", [P, KT, S], f32r)
        hn_lo = sb("hn_lo", [P, KT, S], f32r)
        aux_at = top[0]
        mem_in = sb("mem_in", [P, MT, D])
        raw = sb("raw", [P, 2, 2048])
        w_hi = sb("w_hi", [P, 2, 2048], f32r)
        w_lo = sb("w_lo", [P, 2, 2048], f32r)
        sumsq_at = top[0]
        sumsq = sb("sumsq", [P, S])
        rb = sb("rb", [P, S])
        tmp = sb("tmp", [P, 3, S])
        ident = sb("ident", [P, P])
        ones = sb("ones", [P, P])
        ident_r = sb("ident_r", [P, P], f32r)
        mask_r = sb("mask_r", [P, P], f32r)
        wsr = sb("wsr", [P, HEADS, P])
        gains = sb("gains", [P, 90])
        rope = sb("rope", [P, ST, 2, 2 * HALF])
        rtok = sb("rtok", [P, ST])
        msq = sb("msq", [P, ST])
        m_half = sb("m_half", [P, 16])
        lam = sb("lam", [P, LAYERS])
        gsub = sb("gsub", [P, LAYERS])
        mv = sb("mv", [P, ST, HEADS, 2])
        rstd = sb("rstd", [P, ST, HEADS])
        vareps = sb("vareps", [P, ST, HEADS])
        mx = sb("mx", [P, 2, 2])
        nb = sb("nb", [P, 2, 2])
        sm = sb("sm", [P, 2, 2])
        rc = sb("rc", [P, 2, 2])
        msh = sb("msh", [P, ST])
        mss = sb("mss", [P, 3, MT])
        rh = sb("rh", [P, ST])
        cmx = sb("cmx", [P, ST])
        cnb = sb("cnb", [P, ST])
        csm = sb("csm", [P, ST])
        crc = sb("crc", [P, ST])
        crs = sb("crs", [P, ST])
        sh = top[0]
        assert sh + 2 * HT * S * 4 <= 229344, sh + 2 * HT * S * 4
        K1 = 1024
        hid_hi = sb("hid_hi", [P, HT, S], f32r, sh)
        hid_lo = sb("hid_lo", [P, HT, S], f32r, sh + 44 * K1)
        gu = sb("gu", [P, HEADS, S], f32, sh)
        wsT_hi = sb("wsT_hi", [P, HEADS, P], f32r, sh + 8 * K1)
        wsT_lo = sb("wsT_lo", [P, HEADS, P], f32r, sh + 10 * K1)
        ln_g = sb("ln_g", [P, HEADS * P], f32, sh + 12 * K1)
        ln_b = sb("ln_b", [P, HEADS * P], f32, sh + 14 * K1)
        bs_b = sb("bs_b", [P, HEADS * P], f32, sumsq_at)
        bst = sb("bst", [P, ST, HEADS, 6], f32, sh + 32 * K1)
        k_tok = sb("k_tok", [P, ST, S], f32, sh + 24 * K1)
        mg_hi = sb("mg_hi", [P, KT, M], f32r, sh + 16 * K1)
        mg_lo = sb("mg_lo", [P, KT, M], f32r, sh + 24 * K1)
        kc_hi = sb("kc_hi", [P, KT, M], f32r, sh)
        kc_lo = sb("kc_lo", [P, KT, M], f32r, sh + 8 * K1)
        vc_at = [(aux_at, aux_at + 4 * K1), (aux_at + 2 * K1, aux_at + 6 * K1),
                 (sh + 64 * K1, sh + 72 * K1), (sh + 66 * K1, sh + 74 * K1)]
        vc_hi = [sb(f"vc_hi{n}", [P, MT, 256], f32r, a) for n, (a, _) in enumerate(vc_at)]
        vc_lo = [sb(f"vc_lo{n}", [P, MT, 256], f32r, a) for n, (_, a) in enumerate(vc_at)]
        qT_hi = sb("qT_hi", [P, HEADS, S], f32r, sh + 32 * K1)
        qT_lo = sb("qT_lo", [P, HEADS, S], f32r, sh + 40 * K1)
        gm_hi = sb("gm_hi", [P, HEADS, S], f32r, sh + 48 * K1)
        gm_lo = sb("gm_lo", [P, HEADS, S], f32r, sh + 56 * K1)
        kT_hi = sb("kT_hi", [P, HEADS, S], f32r, sh + 64 * K1)
        kT_lo = sb("kT_lo", [P, HEADS, S], f32r, sh + 72 * K1)
        q_tok = sb("q_tok", [P, ST, S], f32, sh + 80 * K1)
        ex = sb("ex", [P, 2, 2, S], f32, sh + 80 * K1)
        v_hi = sb("v_hi", [P, ST, S], f32r, hn_at)
        v_lo = sb("v_lo", [P, ST, S], f32r, hn_at + 8 * K1)
        wT_hi = sb("wT_hi", [P, ST, S], f32r, hn_at + 16 * K1)
        wT_lo = sb("wT_lo", [P, ST, S], f32r, hn_at + 24 * K1)
        qc_hi = sb("qc_hi", [P, 2, 2, S], f32r, sh + 16 * K1)
        qc_lo = sb("qc_lo", [P, 2, 2, S], f32r, sh + 24 * K1)
        o_hi = sb("o_hi", [P, KT, S], f32r, sh + 32 * K1)
        o_lo = sb("o_lo", [P, KT, S], f32r, sh + 48 * K1)
        wc_hi = sb("wc_hi", [P, MT, S], f32r, sh + 80 * K1)
        wc_lo = sb("wc_lo", [P, MT, S], f32r, sh + 84 * K1)
        x_in = sb("x_in", [P, ST, D], f32, sh)
        rows = sb("rows", [90, P], f32, sh + 28 * K1)
        lam_in = sb("lam_in", [P, 4, LAYERS * 64], f32, sh + 29 * K1)
        lam_pr = sb("lam_pr", [P, 2, LAYERS, 64], f32, sh + 31 * K1)
        lam_s = sb("lam_s", [P, 2, LAYERS], f32, sh + 32 * K1)
        pos_i = sb("pos_i", [ST, P], i32, sh + 33 * K1)
        pos_f = sb("pos_f", [ST, P], f32, sh + 34 * K1)
        pos_t = sb("pos_t", [P, ST], f32, sh + 35 * K1)
        invf = sb("invf", [P, HALF], f32, sh + 36 * K1)
        ang = sb("ang", [P, 5, ST, HALF], f32, sh + 37 * K1)
        hg = sb("hg", [P, KT, S], f32, sh)
        o_sb = sb("o_sb", [P, ST, D], f32, sh + 16 * K1)

        ps = ctx.enter_context(nc.psum_tensor("ps", [P, 8, 512], f32))

        x_loaded = sem("x_loaded")
        consts_loaded = sem("consts_loaded")
        lam_loaded = sem("lam_loaded")
        mem_loaded = sem("mem_loaded")
        setup_pool = sem("setup_pool")
        setup_dve = sem("setup_dve")
        setup_act = sem("setup_act")
        setup_pe = sem("setup_pe")
        w_loaded = [sem("w_loaded0"), sem("w_loaded1")]
        w_rounded = sem("w_rounded")
        w_split = sem("w_split")
        w_used = sem("w_used")
        x_turned = sem("x_turned")
        mem_sq_ready = sem("mem_sq_ready")
        mem_ms_ready = sem("mem_ms_ready")
        mem_r_ready = sem("mem_r_ready")
        lam_sums_ready = sem("lam_sums_ready")
        angles_ready = sem("angles_ready")
        mem_normed = sem("mem_normed")
        mem_turned = sem("mem_turned")
        h_ready = sem("h_ready")
        hn_rounded = sem("hn_rounded")
        hn_ready = sem("hn_ready")
        sq_ready = sem("sq_ready")
        sum_ready = sem("sum_ready")
        stat_done = sem("stat_done")
        ms_ready = sem("ms_ready")
        r_ready = sem("r_ready")
        rb_done = sem("rb_done")
        rb_ready = sem("rb_ready")
        gate_ready = sem("gate_ready")
        up_read = sem("up_read")
        silu_ready = sem("silu_ready")
        prod_ready = sem("prod_ready")
        hid_rounded = sem("hid_rounded")
        hid_ready = sem("hid_ready")
        small_loaded = sem("small_loaded")
        ws_masked = sem("ws_masked")
        gelu_ready = sem("gelu_ready")
        var_ready = sem("var_ready")
        rstd_ready = sem("rstd_ready")
        vn_final = sem("vn_final")
        vn_rounded = sem("vn_rounded")
        vn_ready = sem("vn_ready")
        qk_copied = sem("qk_copied")
        qk_roped = sem("qk_roped")
        qk_turned = sem("qk_turned")
        qkT_rounded = sem("qkT_rounded")
        qkT_ready = sem("qkT_ready")
        ws_turned = sem("ws_turned")
        wsT_rounded = sem("wsT_rounded")
        wsT_ready = sem("wsT_ready")
        gu_scaled = sem("gu_scaled")
        gu_ready = sem("gu_ready")
        mix_done = sem("mix_done")
        gm_final = sem("gm_final")
        gm_rounded = sem("gm_rounded")
        gm_ready = sem("gm_ready")
        v_rounded = sem("v_rounded")
        v_ready = sem("v_ready")
        mg_rounded = sem("mg_rounded")
        mg_ready = sem("mg_ready")
        sc_done = sem("sc_done")
        nb_ready = sem("nb_ready")
        exp_done = sem("exp_done")
        attn_w_ready = sem("attn_w_ready")
        attn_w_turned = sem("attn_w_turned")
        wT_rounded = sem("wT_rounded")
        wT_ready = sem("wT_ready")
        pv_done = sem("pv_done")
        osq_ready = sem("osq_ready")
        ostat_done = sem("ostat_done")
        oms_ready = sem("oms_ready")
        rh_ready = sem("rh_ready")
        orb_done = sem("orb_done")
        orb_ready = sem("orb_ready")
        attn_final = sem("attn_final")
        attn_rounded = sem("attn_rounded")
        attn_ready = sem("attn_ready")
        kv_rounded = sem("kv_rounded")
        kv_ready = sem("kv_ready")
        qc_rounded = sem("qc_rounded")
        qc_ready = sem("qc_ready")
        csc_done = sem("csc_done")
        cnb_ready = sem("cnb_ready")
        cexp_done = sem("cexp_done")
        cw_ready = sem("cw_ready")
        cw_turned = sem("cw_turned")
        wc_rounded = sem("wc_rounded")
        wc_ready = sem("wc_ready")
        cpv_done = sem("cpv_done")
        o_rounded = sem("o_rounded")
        o_ready = sem("o_ready")
        dve_chain = sem("dve_chain")
        hg_ready = sem("hg_ready")
        fin_turned = sem("fin_turned")
        fin_ready = sem("fin_ready")
        out_stored = sem("out_stored")

        CHAIN = ST * 4 + 2 * ST + ST + 16 * 4 + 1 + 2 * HEADS

        def unit_no(L, u, i=0, per=2):
            return L * UNITS + u + per * i

        def used(L, u, i=0, per=2):
            return unit_no(L, u, i, per) + 3

        def tile_no(L, stage, m):
            return KT + (L * STAGES + stage) * KT + m + 1

        def hn_no(L, stage, t):
            return (L * STAGES + stage) * KT + t + 1

        def sum_no(L, stage, m):
            return 9 + (L * STAGES + stage) * 9 + m + 2

        def ffn_no(L, f, j):
            return (L * 2 + f) * HT + j + 1

        def wait_apart(eng, signal, value):
            eng.compute_val(value)
            eng.wait_ge(setup_pool, 1)
            eng.wait_ge(signal, value)

        def down_loop(eng, body):
            with eng.Fori(0, KT // 2 - 1) as i:
                body(i, False)
            body(KT // 2 - 1, True)

        def up_loop(eng, body):
            body(0, "first")
            with eng.Fori(1, HT // 2 - 1) as i:
                body(i, "")
            body(HT // 2 - 1, "last")

        block = ctx.enter_context(nc.Block())

        @block.sync
        def _(sp):
            def load(L, u, i, per, parts):
                assert len(parts) == 2
                wait_apart(sp, w_split, unit_no(L, u, i, per) + 1)
                for (a, k, c, src) in parts:
                    dst = raw[:, u % 2, a:a + k * c].rearrange("p (k c) -> p k c", c=c)
                    sp.dma_start(dst, src.rearrange("o (k p) c -> (o p) k c", p=P))\
                      .then_inc(w_loaded[u % 2], 16)

            def ffn_loads(L, up, dn, wgu, wd):
                with sp.Fori(0, HT // 2) as i:
                    for s in range(2):
                        col = i * (2 * P) + s * P
                        load(L, up + s, i, 2, [(0, KT, P, wgu[ds(L, 1), :, ds(col, P)]),
                                               (1024, KT, P, wgu[ds(L, 1), :, ds(col + FF, P)])])
                with sp.Fori(0, KT) as m:
                    for s in range(2):
                        k0 = s * HK
                        load(L, dn + s, m, 2,
                             [(0, 6, P, wd[ds(L, 1), k0 * P:(k0 + 6) * P, ds(m * P, P)]),
                              (768, HK - 6, P, wd[ds(L, 1), (k0 + 6) * P:(k0 + HK) * P, ds(m * P, P)])])

            def token_loads(L, u, w, col):
                for s in range(2):
                    load(L, u + s, 0, 2,
                         [(n * 1024, 2, 512, w[ds(L, 1), (4 * s + 2 * n) * P:(4 * s + 2 * n + 2) * P, col:col + 512])
                          for n in range(2)])

            def feature_loads(L, u, w, col, n_units):
                for t in range(n_units):
                    c0 = col + t * 256
                    load(L, u + t, 0, 2,
                         [(n * 1024, 4, 256, w[ds(L, 1), n * 512:(n + 1) * 512, c0:c0 + 256]) for n in range(2)])

            for t in range(ST):
                sp.dma_start(x_in[:, t, :], x[0, t * P:(t + 1) * P, :]).then_inc(x_loaded, 16)
            with sp.Fori(0, LAYERS) as L:
                ffn_loads(L, UP1, DN1, ffn1_wgu, ffn1_wd)
                token_loads(L, GV, w_in, 2048)
                token_loads(L, QQ, w_in, 0)
                token_loads(L, KK, w_in, 512)
                feature_loads(L, GU, w_in, 1536, 2)
                token_loads(L, VV, w_in, 1024)
                feature_loads(L, CK, cross_wkv, 0, 8)
                feature_loads(L, WO, w_out, 0, 4)
                feature_loads(L, WQ, cross_wq, 0, 4)
                feature_loads(L, CO, cross_wo, 0, 4)
                ffn_loads(L, UP2, DN2, ffn2_wgu, ffn2_wd)
            for s in range(2):
                load(LAYERS, s, 0, 2, [(g * 1024, KT, P, ffn1_wgu[0:1, :, g * FF + s * P:g * FF + (s + 1) * P])
                                       for g in range(2)])
            for t in range(ST):
                sp.wait_ge(fin_ready, t + 1)
                sp.dma_start(out[0, t * P:(t + 1) * P, :], o_sb[:, t, :]).then_inc(out_stored, 16)
            sp.wait_ge(out_stored, 16 * ST)

        @block.gpsimd
        def _(pool):
            pool.memset(ident[:, :], 0.0).then_inc(setup_pool, 1)
            pool.memset(ones[:, :], 1.0).then_inc(setup_pool, 1)
            pool.memset(rb[:, 0:P], 0.0).then_inc(setup_pool, 1)
            pool.memset(m_half[:, :], -0.5).then_inc(setup_pool, 1)
            pool.wait_ge(setup_pool, 4)
            pool.affine_select(out=ident[:, :], in_=ident[:, :], compare_op=ALU.not_equal, fill=1.0,
                               base=0, pattern=[[-1, P]], channel_multiplier=1).then_inc(setup_pool, 1)
            pool.affine_select(out=rb[:, 0:P], in_=rb[:, 0:P], compare_op=ALU.is_ge, fill=NEG,
                               base=0, pattern=[[-1, P]], channel_multiplier=1).then_inc(setup_pool, 1)

            def clear_sum(first_sum):
                pool.memset(sumsq[:, :], 0.0).then_inc(sum_ready, 1)

            def add_square(sq_no, before, m2):
                pool.wait_ge(sq_ready, sq_no)
                pool.wait_ge(sum_ready, before)
                pool.tensor_tensor(out=sumsq[:, :], in0=sumsq[:, :], in1=tmp[:, m2, :], op=ALU.add)\
                    .then_inc(sum_ready, 1)

            def inverse_rms(n):
                pool.wait_ge(ms_ready, n)
                pool.tensor_tensor(out=rtok[:, :], in0=msq[:, :], in1=m_half[:, 0:ST], op=ALU.pow)\
                    .then_inc(r_ready, 1)

            clear_sum(0)
            for m in range(KT):
                add_square(m + 1, m + 1, m % 2)

            def stage_sums(L, stage, stats_before):
                wait_apart(pool, stat_done, L * 4 + stats_before)
                clear_sum(0)
                if stage in (0, 3):
                    def body(i, last):
                        for b in range(2):
                            m = 2 * i + b
                            add_square(tile_no(L, stage, m), sum_no(L, stage, m) - 1, b)
                    down_loop(pool, body)
                else:
                    for m in range(KT):
                        add_square(tile_no(L, stage, m), sum_no(L, stage, m) - 1, m % 2)

            with pool.Fori(0, LAYERS) as L:
                inverse_rms(L * 4 + 1)
                stage_sums(L, 0, 1)
                inverse_rms(L * 4 + 2)
                wait_apart(pool, small_loaded, L * 64 + 64)
                pool.affine_select(out=wsr[:, :, :], in_=wsr[:, :, :], compare_op=ALU.is_ge, fill=0.0,
                                   base=0, pattern=[[0, HEADS], [-1, P]], channel_multiplier=1)\
                    .then_inc(ws_masked, 1)
                pool.wait_ge(var_ready, L + 1)
                pool.tensor_tensor(out=rstd[:, :, :], in0=vareps[:, :, :],
                                   in1=m_half[:, :].rearrange("p (a b) -> p a b", b=HEADS), op=ALU.pow)\
                    .then_inc(rstd_ready, 1)
                pool.wait_ge(mem_ms_ready, L + 1)
                pool.tensor_tensor(out=mss[:, 2, :], in0=mss[:, 1, :], in1=m_half[:, 0:MT], op=ALU.pow)\
                    .then_inc(mem_r_ready, 1)
                for hd in range(HEADS):
                    pool.wait_ge(oms_ready, L * 4 + hd + 1)
                    pool.tensor_tensor(out=rh[:, :], in0=msh[:, :], in1=m_half[:, 0:ST], op=ALU.pow)\
                        .then_inc(rh_ready, 1)
                stage_sums(L, 1, 2)
                inverse_rms(L * 4 + 3)
                stage_sums(L, 2, 3)
                inverse_rms(L * 4 + 4)
                stage_sums(L, 3, 4)
            inverse_rms(LAYERS * 4 + 1)

        @block.scalar
        def _(act):
            n_consts = 0

            def load_const(dst, src):
                nonlocal n_consts
                n_consts += 1
                act.dma_start(dst, src).then_inc(consts_loaded, 16)

            for col, g in ((G_FFN1, ffn1_norm), (G_MIX, mix_norm), (G_CROSS, cross_norm), (G_FFN2, ffn2_norm),
                           (G_MEM, mem_norm)):
                load_const(rows[col:col + LAYERS * KT, :], g.rearrange("l (t p) -> (l t) p", p=P))
            load_const(rows[G_FINAL:G_FINAL + KT, :], final_norm.rearrange("(t p) -> t p", p=P))
            load_const(rows[G_SUBLN:G_SUBLN + LAYERS, :], subln)
            load_const(pos_i[:, :], positions[0].rearrange("(t p) -> t p", p=P))
            assert n_consts == 8
            for n, v in enumerate([lam_q1, lam_k1, lam_q2, lam_k2]):
                act.dma_start(lam_in[:, n, :], v.rearrange("l d -> (l d)").unsqueeze(0).to_broadcast([P, LAYERS * 64]))\
                   .then_inc(lam_loaded, 16)

            act.wait_ge(setup_pool, 6)
            act.activation(ident_r[:, :], ident[:, :], ACT.Copy).then_inc(setup_act, 1)
            act.activation(mask_r[:, :], rb[:, 0:P], ACT.Copy).then_inc(setup_act, 1)

            def round_unit(L, u, i=0, per=2):
                n = unit_no(L, u, i, per)
                s = u % 2
                act.wait_ge(w_loaded[s], 32 * (L * (UNITS // 2) + u // 2 + (per // 2) * i + 1))
                act.wait_ge(w_used, n + 1)
                z = unit_size(u)
                act.activation(w_hi[:, s, 0:z], raw[:, s, 0:z], ACT.Copy).then_inc(w_rounded, 1)

            def round_tile(no, m, gcol):
                wait_apart(act, h_ready, no)
                act.activation(hn_hi[:, ds(m, 1), :], h[:, ds(m, 1), :], ACT.Copy,
                               scale=gains[:, ds(gcol, 1)]).then_inc(hn_rounded, 1)

            def square_tile(m, b, sum_before):
                if sum_before is not None:
                    wait_apart(act, sum_ready, sum_before)
                act.activation(tmp[:, b:b + 1, :], h[:, ds(m, 1), :], ACT.Square).then_inc(sq_ready, 1)

            def copy_rb(n, bank):
                act.wait_ge(rb_done, n)
                act.activation(rb[:, :], ps[:, bank, :], ACT.Copy).then_inc(rb_ready, 1)

            for m in range(KT):
                round_tile(m + 1, m, m)
                square_tile(m, m % 2, m if m >= 2 else None)
            round_unit(0, 0)
            round_unit(0, 1)
            act.wait_ge(lam_sums_ready, 1)
            act.activation(lam_s[:, :, :], lam_s[:, :, :], ACT.Exp).then_inc(setup_act, 1)
            act.wait_ge(angles_ready, 1)
            act.activation(ang[:, 3, :, :], ang[:, 1, :, :], ACT.Sin).then_inc(setup_act, 1)
            act.activation(ang[:, 4, :, :], ang[:, 2, :, :], ACT.Sin).then_inc(setup_act, 1)

            def ffn(L, f, up, dn, stage, rb_no, next_gain, next_unit):
                def up_body(i, where):
                    if where == "first":
                        copy_rb(rb_no, 7)
                    for s in range(2):
                        u = up + s
                        if where == "last":
                            round_unit(L, dn + s)
                        else:
                            round_unit(L, u + 2, i)
                        n = ffn_no(L, f, 2 * i + s)
                        act.wait_ge(gate_ready, n)
                        act.activation(tmp[:, 1, :], tmp[:, 0, :], ACT.Silu).then_inc(silu_ready, 1)
                        wait_apart(act, prod_ready, n)
                        act.activation(hid_hi[:, ds(2 * i + s, 1), :], tmp[:, 1:2, :], ACT.Copy)\
                           .then_inc(hid_rounded, 1)
                up_loop(act, up_body)

                def down_body(i, last):
                    for b in range(2):
                        m = 2 * i + b
                        no = tile_no(L, stage, m)
                        at_end = last and b == 1
                        for s in range(2):
                            if s == 1:
                                round_tile(no, m, L * KT + next_gain + m)
                            if not at_end:
                                round_unit(L, dn + 2 * b + 2 + s, i, 4)
                            else:
                                round_unit(L, next_unit + s)
                        square_tile(m, b, sum_no(L, stage, m) - 2)
                down_loop(act, down_body)

            with act.Fori(0, LAYERS) as L:
                ffn(L, 0, UP1, DN1, 0, L * 3 + 1, G_MIX, GV)

                act.wait_ge(hn_ready, hn_no(L, 1, KT - 1))
                for t in range(MT):
                    act.dma_start(mem_in[:, t, :], mem[0, t * P:(t + 1) * P, :]).then_inc(mem_loaded, 16)
                act.dma_start(wsr[:, :, :], gmlp_ws[ds(L, 1)].rearrange("o g t s -> (o t) g s")).then_inc(small_loaded, 16)
                for dst, src in ((ln_g, gmlp_ln_g), (ln_b, gmlp_ln_b), (bs_b, gmlp_bs)):
                    if dst is bs_b:
                        act.wait_ge(stat_done, L * 4 + 2)
                    act.dma_start(dst[:, :], src[ds(L, 1)].rearrange("o g c -> o (g c)").to_broadcast([P, HEADS * P]))\
                       .then_inc(small_loaded, 16)

                round_unit(L, QQ)
                round_unit(L, QQ + 1)
                act.wait_ge(w_used, used(L, GV + 1))
                act.wait_ge(r_ready, L * 4 + 2)
                for t in range(ST):
                    act.activation(k_tok[:, t, :], ps[:, t, :], ACT.Gelu, scale=rtok[:, t:t + 1])\
                       .then_inc(gelu_ready, 1)
                for t in range(MT):
                    if t:
                        act.wait_ge(mem_sq_ready, L * 2 + t)
                    else:
                        act.wait_ge(mem_loaded, L * 32 + 32)
                    act.activation(tmp[:, 0:2, :], mem_in[:, t, :].rearrange("p (a c) -> p a c", c=S), ACT.Square,
                                   accum_out=mss[:, 0, t:t + 1]).then_inc(mem_sq_ready, 1)
                round_unit(L, KK)
                for t in range(ST):
                    act.wait_ge(vn_final, L * 4 + t + 1)
                    act.activation(gm_hi[:, :, t * P:(t + 1) * P],
                                   k_tok[:, t, :].rearrange("p (g c) -> p g c", c=P), ACT.Copy)\
                       .then_inc(vn_rounded, 1)
                round_unit(L, KK + 1)
                act.wait_ge(w_used, used(L, QQ + 1))
                for t in range(ST):
                    act.activation(q_tok[:, t, :], ps[:, 4 + t, :], ACT.Copy, scale=rtok[:, t:t + 1])\
                       .then_inc(qk_copied, 1)
                round_unit(L, GU)
                copy_rb(L * 3 + 2, 4)
                act.wait_ge(ws_turned, L + 1)
                act.activation(wsT_hi[:, :, :], ps[:, 5, :].rearrange("p (g c) -> p g c", c=P), ACT.Copy)\
                   .then_inc(wsT_rounded, 1)
                round_unit(L, GU + 1)
                act.wait_ge(w_used, used(L, KK + 1))
                act.wait_ge(vn_ready, L * 4 + 4)
                for t in range(ST):
                    act.activation(k_tok[:, t, :], ps[:, t, :], ACT.Copy, scale=rtok[:, t:t + 1])\
                       .then_inc(qk_copied, 1)

                def gelu_gu(half):
                    act.wait_ge(gu_scaled, L * 2 + half + 1)
                    act.activation(gu[:, 2 * half:2 * half + 2, :], gu[:, 2 * half:2 * half + 2, :], ACT.Gelu)\
                       .then_inc(gu_ready, 1)

                def round_turned(n, dst):
                    act.wait_ge(qk_turned, L * 8 + n + 1)
                    t = n % ST
                    act.activation(dst[:, :, t * P:(t + 1) * P],
                                   ps[:, t, :].rearrange("p (g c) -> p g c", c=P), ACT.Copy)\
                       .then_inc(qkT_rounded, 1)

                round_unit(L, VV)
                gelu_gu(0)
                for t in range(ST):
                    round_turned(t, qT_hi)
                round_unit(L, VV + 1)
                gelu_gu(1)
                for t in range(ST):
                    round_turned(ST + t, kT_hi)
                def round_gm(t):
                    act.wait_ge(gm_final, L * 4 + t + 1)
                    act.activation(gm_hi[:, :, t * P:(t + 1) * P],
                                   tmp[:, t % 2, :].rearrange("p (g c) -> p g c", c=P), ACT.Copy)\
                       .then_inc(gm_rounded, 1)

                def round_mg(half):
                    wait_apart(act, mem_turned, L * 2 + half + 1)
                    for n in range(4):
                        m = 4 * half + n
                        act.activation(mg_hi[:, m, :], ps[:, 4 + n // 2, (n % 2) * M:(n % 2 + 1) * M], ACT.Copy,
                                       scale=gains[:, ds(L * KT + G_MEM + m, 1)]).then_inc(mg_rounded, 1)

                round_gm(0)
                round_gm(1)
                round_mg(0)
                round_unit(L, CK)
                round_gm(2)
                round_mg(1)
                act.wait_ge(w_used, used(L, VV + 1))
                for t in range(ST):
                    act.activation(v_hi[:, t, :], ps[:, t, :], ACT.Copy, scale=rtok[:, t:t + 1])\
                       .then_inc(v_rounded, 1)
                round_gm(3)
                round_unit(L, CK + 1)

                for s in range(22):
                    if 2 <= s < 18:
                        n = s - 2
                        qb = n % 4
                        act.wait_ge(attn_w_turned, L * 16 + n + 1)
                        if qb == 0 and n:
                            act.wait_ge(pv_done, L * 4 + n // 4)
                        act.activation(wT_hi[:, 0:qb + 1, qb * P:(qb + 1) * P],
                                       ps[:, 0, 0:(qb + 1) * P].rearrange("p (k c) -> p k c", c=P), ACT.Copy)\
                           .then_inc(wT_rounded, 1)
                    if s < 16:
                        qb, b = s % 4, s % 2
                        N = (qb + 1) * P
                        act.wait_ge(nb_ready, L * 16 + s + 1)
                        if s >= 2:
                            act.wait_ge(attn_w_turned, L * 16 + s - 1)
                        for br in range(2):
                            last = act.activation(ex[:, b, br, 0:N], ps[:, 4 + 2 * b + br, 0:N], ACT.Exp,
                                                  bias=nb[:, b, br:br + 1], scale=QK_SCALE,
                                                  accum_out=sm[:, b, br:br + 1])
                        last.then_inc(exp_done, 1)
                    if s % 2 == 0 and 2 <= s <= 16:
                        n = s // 2 - 1
                        act.wait_ge(w_used, used(L, CK + n))
                        act.activation(kc_hi[:, 2 * n:2 * n + 2, :] if n < 4 else vc_hi[n - 4][:, :, :],
                                       ps[:, 2, :].rearrange("p (k c) -> p k c", c=M), ACT.Copy)\
                           .then_inc(kv_rounded, 1)
                        round_unit(L, CK + n + 2)
                    if s >= 5:
                        hd, part = divmod(s - 5, 4)
                        if part == 0 and hd < 4:
                            act.wait_ge(pv_done, L * 4 + hd + 1)
                            if hd:
                                act.wait_ge(attn_ready, L * 4 + hd)
                            act.activation(tmp[:, 0, :], ps[:, 1, :], ACT.Square).then_inc(osq_ready, 1)
                        if part == 2:
                            act.wait_ge(orb_done, L * 4 + hd + 1)
                            act.activation(tmp[:, 1, :], ps[:, 3, :], ACT.Copy).then_inc(orb_ready, 1)
                        if part == 3:
                            act.wait_ge(attn_final, L * 4 + hd + 1)
                            act.activation(qT_hi[:, hd, :], tmp[:, 0, :], ACT.Copy).then_inc(attn_rounded, 1)

                def projected(stage, u, gcol):
                    for t in range(4):
                        for b in range(2):
                            round_tile(tile_no(L, stage, 2 * t + b), 2 * t + b, L * KT + gcol + 2 * t + b)
                        round_unit(L, u + t + 2)
                        for b in range(2):
                            m = 2 * t + b
                            square_tile(m, b, sum_no(L, stage, m) - 2)

                projected(1, WO, G_CROSS)

                def round_qc(hd):
                    b = hd % 2
                    act.wait_ge(w_used, used(L, WQ + hd))
                    act.activation(qc_hi[:, b, :, :], ps[:, 4 + 2 * b:6 + 2 * b, :], ACT.Copy).then_inc(qc_rounded, 1)
                    round_unit(L, WQ + hd + 2)

                def cross_exp(hd):
                    act.wait_ge(cnb_ready, L * 4 + hd + 1)
                    if hd:
                        act.wait_ge(cw_turned, L * 4 + hd)
                    for qb in range(ST):
                        last = act.activation(tmp[:, qb // 2, (qb % 2) * M:(qb % 2 + 1) * M],
                                              ps[:, qb // 2, (qb % 2) * M:(qb % 2 + 1) * M], ACT.Exp,
                                              bias=cnb[:, qb:qb + 1], scale=crs[:, qb:qb + 1],
                                              accum_out=csm[:, qb:qb + 1])
                    last.then_inc(cexp_done, 1)

                round_qc(0)
                round_qc(1)
                cross_exp(0)
                round_qc(2)
                for hd in range(HEADS):
                    act.wait_ge(cw_turned, L * 4 + hd + 1)
                    if hd:
                        act.wait_ge(cpv_done, L * 4 + hd)
                    act.activation(wc_hi[:, :, :], ps[:, 2:4, :], ACT.Copy).then_inc(wc_rounded, 1)
                    if hd < 3:
                        cross_exp(hd + 1)
                    act.wait_ge(cpv_done, L * 4 + hd + 1)
                    act.activation(o_hi[:, 2 * hd:2 * hd + 2, :], ps[:, 2:4, :], ACT.Copy).then_inc(o_rounded, 1)
                    if hd == 0:
                        round_qc(3)

                projected(2, CO, G_FFN2)
                ffn(L, 1, UP2, DN2, 3, L * 3 + 3, G_FFN1 + KT, UNITS)

            for t in range(ST):
                act.wait_ge(fin_turned, t + 1)
                act.wait_ge(r_ready, LAYERS * 4 + 1)
                b = 2 * (t % 2)
                act.activation(o_sb[:, t, :].rearrange("p (a c) -> p a c", c=512), ps[:, b:b + 2, :], ACT.Copy,
                               scale=rtok[:, t:t + 1]).then_inc(fin_ready, 1)

        @block.vector
        def _(dve):
            def split_unit(L, u, i=0, per=2):
                s = u % 2
                dve.wait_ge(w_rounded, unit_no(L, u, i, per) + 1)
                z = unit_size(u)
                dve.tensor_tensor(out=w_lo[:, s, 0:z], in0=raw[:, s, 0:z], in1=w_hi[:, s, 0:z].bitcast(f32),
                                  op=ALU.subtract).then_inc(w_split, 1)

            def add_tile(products, m, bank, factor):
                dve.wait_ge(w_used, products)
                dve.scalar_tensor_tensor(out=h[:, ds(m, 1), :], in0=ps[:, bank:bank + 1, :], scalar=factor,
                                         in1=h[:, ds(m, 1), :], op0=ALU.mult, op1=ALU.add).then_inc(h_ready, 1)

            def low_tile(no, m, gcol):
                dve.wait_ge(hn_rounded, no)
                dve.scalar_tensor_tensor(out=hn_lo[:, ds(m, 1), :], in0=h[:, ds(m, 1), :],
                                         scalar=gains[:, ds(gcol, 1)],
                                         in1=hn_hi[:, ds(m, 1), :].bitcast(f32),
                                         op0=ALU.mult, op1=ALU.subtract).then_inc(hn_ready, 1)

            def mean_square(n, bank):
                dve.wait_ge(stat_done, n)
                dve.tensor_scalar(msq[:, :], ps[:, bank, 0:ST], 1.0 / D, EPS, ALU.mult, ALU.add)\
                   .then_inc(ms_ready, 1)

            done = [0]

            def setup(ins):
                done[0] += 1
                ins.then_inc(setup_dve, 1)
                dve.wait_ge(setup_dve, done[0])

            dve.memset(msh[:, :], 0.0).then_inc(w_split, 2)
            dve.memset(rh[:, :], 0.0).then_inc(w_used, 2)
            inv = (1.0 / np.power(np.float32(500000.0), np.arange(0, 16, 2, dtype=np.float32) / np.float32(16))).astype(np.float32)
            for j in range(HALF):
                setup(dve.memset(invf[:, j:j + 1], float(inv[j])))
            dve.wait_ge(consts_loaded, 16 * 8)
            setup(dve.tensor_copy(pos_f[:, :], pos_i[:, :]))
            dve.wait_ge(setup_pe, 1)
            setup(dve.tensor_copy(gains[:, :], ps[:, 6, 0:90]))
            dve.wait_ge(setup_pe, 2)
            setup(dve.tensor_copy(pos_t[:, :], ps[:, 7, 0:ST]))
            for m in range(KT):
                dve.wait_ge(x_turned, m + 1)
                dve.tensor_copy(h[:, m, :], ps[:, m % 4, :]).then_inc(h_ready, 1)
                low_tile(m + 1, m, m)
            split_unit(0, 0)
            split_unit(0, 1)
            for t in range(ST):
                setup(dve.tensor_scalar(ang[:, 0, t, :], invf[:, :], pos_t[:, t:t + 1], None, ALU.mult))
            magic = float(1.5 * 2 ** 23)
            setup(dve.tensor_scalar(ang[:, 1, :, :], ang[:, 0, :, :], 1.0 / (2 * math.pi), None, ALU.mult))
            setup(dve.tensor_scalar(ang[:, 1, :, :], ang[:, 1, :, :], magic, None, ALU.add))
            setup(dve.tensor_scalar(ang[:, 1, :, :], ang[:, 1, :, :], -magic, None, ALU.add))
            c1 = 6.28125
            c2 = float(round((2 * math.pi - c1) * 2 ** 20) / 2 ** 20)
            c3 = 2 * math.pi - c1 - c2
            for c in (c1, c2, c3):
                setup(dve.scalar_tensor_tensor(out=ang[:, 0, :, :], in0=ang[:, 1, :, :], scalar=-c,
                                               in1=ang[:, 0, :, :], op0=ALU.mult, op1=ALU.add))
            setup(dve.tensor_scalar(ang[:, 1, :, :], ang[:, 0, :, :], 3.1415925, -3.1415925, ALU.min, ALU.max))
            setup(dve.tensor_scalar(ang[:, 2, :, :], ang[:, 1, :, :], -1.0, None, ALU.mult))
            setup(dve.tensor_tensor(out=ang[:, 2, :, :], in0=ang[:, 2, :, :], in1=ang[:, 1, :, :], op=ALU.max))
            dve.tensor_scalar(ang[:, 2, :, :], ang[:, 2, :, :], -1.0, math.pi / 2, ALU.mult, ALU.add).then_inc(angles_ready, 1)
            dve.wait_ge(lam_loaded, 16 * 4)
            for n in range(2):
                setup(dve.tensor_tensor(out=lam_pr[:, n, :, :],
                                        in0=lam_in[:, 2 * n, :].rearrange("p (l d) -> p l d", d=64),
                                        in1=lam_in[:, 2 * n + 1, :].rearrange("p (l d) -> p l d", d=64), op=ALU.mult))
            dve.tensor_reduce(lam_s[:, :, :], lam_pr[:, :, :, :], AX.X, ALU.add).then_inc(lam_sums_ready, 1)
            for l in range(LAYERS):
                setup(dve.tensor_scalar(gsub[:, l:l + 1], gains[:, G_SUBLN + l:G_SUBLN + l + 1],
                                        1.0 - (0.8 - 0.6 * math.exp(-0.3 * l)), None, ALU.mult))
            dve.wait_ge(setup_act, 3)
            setup(dve.tensor_tensor(out=lam[:, :], in0=lam_s[:, 0, :], in1=lam_s[:, 1, :], op=ALU.subtract))
            for l in range(LAYERS):
                setup(dve.tensor_scalar(lam[:, l:l + 1], lam[:, l:l + 1], 0.8 - 0.6 * math.exp(-0.3 * l), None, ALU.add))
            dve.wait_ge(setup_act, 5)
            for a, src in ((0, 4), (1, 3)):
                for b in range(2):
                    setup(dve.tensor_copy(rope[:, :, a, b * HALF:(b + 1) * HALF], ang[:, src, :, :]))

            def ffn(L, f, up, dn, stage, stat_no, next_gain, next_unit):
                def up_body(i, where):
                    if where == "first":
                        mean_square(stat_no, 6)
                        dve.wait_ge(rb_ready, L * 3 + (1 if f == 0 else 3))
                    for s in range(2):
                        n = ffn_no(L, f, 2 * i + s)
                        dve.wait_ge(w_used, used(L, up + s, i))
                        dve.tensor_tensor(out=tmp[:, 0, :], in0=ps[:, 2 * s, :], in1=rb[:, :], op=ALU.mult)\
                           .then_inc(gate_ready, 1)
                        dve.tensor_tensor(out=tmp[:, 2, :], in0=ps[:, 2 * s + 1, :], in1=rb[:, :], op=ALU.mult)\
                           .then_inc(up_read, 1)
                        if where == "last":
                            split_unit(L, dn + s)
                        else:
                            split_unit(L, up + s + 2, i)
                        dve.wait_ge(silu_ready, n)
                        dve.wait_ge(up_read, n)
                        dve.tensor_tensor(out=tmp[:, 1, :], in0=tmp[:, 1, :], in1=tmp[:, 2, :], op=ALU.mult)\
                           .then_inc(prod_ready, 1)
                        dve.wait_ge(hid_rounded, n)
                        dve.tensor_tensor(out=hid_lo[:, ds(2 * i + s, 1), :], in0=tmp[:, 1:2, :],
                                          in1=hid_hi[:, ds(2 * i + s, 1), :].bitcast(f32), op=ALU.subtract)\
                           .then_inc(hid_ready, 1)
                up_loop(dve, up_body)

                def down_body(i, last):
                    for b in range(2):
                        m = 2 * i + b
                        no = tile_no(L, stage, m)
                        at_end = last and b == 1
                        for s in range(2):
                            if s == 1:
                                add_tile(used(L, dn + 2 * b + 1, i, 4), m, 4 + b, 0.5)
                                low_tile(no, m, L * KT + next_gain + m)
                            if not at_end:
                                split_unit(L, dn + 2 * b + 2 + s, i, 4)
                            else:
                                split_unit(L, next_unit + s)
                down_loop(dve, down_body)

            with dve.Fori(0, LAYERS) as L:
                count = [0]

                def link(ins):
                    count[0] += 1
                    ins.then_inc(dve_chain, 1)
                    dve.wait_ge(dve_chain, L * CHAIN + count[0])

                ffn(L, 0, UP1, DN1, 0, L * 4 + 1, G_MIX, GV)

                split_unit(L, QQ)
                split_unit(L, QQ + 1)
                mean_square(L * 4 + 2, 7)
                dve.wait_ge(small_loaded, L * 64 + 64)
                for t in range(ST):
                    dve.wait_ge(gelu_ready, L * 4 + t + 1)
                    for g in range(HEADS):
                        last = dve.bn_stats(bst[:, t, g, :], k_tok[:, t, g * P:(g + 1) * P])
                    count[0] += 1
                    last.then_inc(dve_chain, 1)
                    wait_apart(dve, dve_chain, L * CHAIN + count[0])
                    for g in range(HEADS):
                        last = dve.bn_aggr(mv[:, t, g, :], bst[:, t, g, :])
                    link(last)
                dve.tensor_scalar(vareps[:, :, :], mv[:, :, :, 1], EPS, None, ALU.add).then_inc(var_ready, 1)
                dve.wait_ge(mem_sq_ready, L * 2 + 2)
                dve.tensor_scalar(mss[:, 1, :], mss[:, 0, :], 1.0 / D, EPS, ALU.mult, ALU.add).then_inc(mem_ms_ready, 1)
                split_unit(L, KK)
                dve.wait_ge(rstd_ready, L + 1)
                for t in range(ST):
                    for g in range(HEADS):
                        last = dve.tensor_scalar(k_tok[:, t, g * P:(g + 1) * P], k_tok[:, t, g * P:(g + 1) * P],
                                                 mv[:, t, g, 0:1], rstd[:, t, g:g + 1], ALU.subtract, ALU.mult)
                    link(last)
                    link(dve.tensor_tensor(out=k_tok[:, t, :], in0=k_tok[:, t, :], in1=ln_g[:, :], op=ALU.mult))
                    dve.tensor_tensor(out=k_tok[:, t, :], in0=k_tok[:, t, :], in1=ln_b[:, :], op=ALU.add)\
                       .then_inc(vn_final, 1)
                for t in range(ST):
                    dve.wait_ge(vn_rounded, L * 4 + t + 1)
                    dve.tensor_tensor(out=gm_lo[:, :, t * P:(t + 1) * P],
                                      in0=k_tok[:, t, :].rearrange("p (g c) -> p g c", c=P),
                                      in1=gm_hi[:, :, t * P:(t + 1) * P].bitcast(f32), op=ALU.subtract)\
                       .then_inc(vn_ready, 1)
                dve.wait_ge(mem_r_ready, L + 1)
                for t in range(MT):
                    last = dve.tensor_scalar(mem_in[:, t, :], mem_in[:, t, :], mss[:, 2, t:t + 1], None, ALU.mult)
                last.then_inc(mem_normed, 1)
                split_unit(L, KK + 1)

                def rotate(n, tok):
                    t = n % ST
                    dve.wait_ge(qk_copied, L * 8 + n + 1)
                    part = tok[:, t, :].rearrange("p (h d) -> p h d", d=64)[:, :, 0:2 * HALF]
                    a = tmp[:, 0, 0:P].rearrange("p (h d) -> p h d", d=2 * HALF)
                    b = tmp[:, 1, 0:P].rearrange("p (h d) -> p h d", d=2 * HALF)
                    cos, sin = (rope[:, t, i:i + 1, :].to_broadcast([P, 8, 2 * HALF]) for i in range(2))
                    dve.tensor_tensor(out=a, in0=part, in1=cos, op=ALU.mult)
                    link(dve.tensor_tensor(out=b, in0=part, in1=sin, op=ALU.mult))
                    dve.tensor_tensor(out=part[:, :, 0:HALF], in0=a[:, :, 0:HALF], in1=b[:, :, HALF:], op=ALU.subtract)
                    dve.tensor_tensor(out=part[:, :, HALF:], in0=a[:, :, HALF:], in1=b[:, :, 0:HALF], op=ALU.add)\
                       .then_inc(qk_roped, 1)
                    dve.wait_ge(qk_roped, L * 8 + n + 1)

                for t in range(ST):
                    rotate(t, q_tok)
                split_unit(L, GU)
                dve.wait_ge(wsT_rounded, L + 1)
                dve.tensor_tensor(out=wsT_lo[:, :, :], in0=ps[:, 5, :].rearrange("p (g c) -> p g c", c=P),
                                  in1=wsT_hi[:, :, :].bitcast(f32), op=ALU.subtract).then_inc(wsT_ready, 1)
                split_unit(L, GU + 1)
                for t in range(ST):
                    rotate(ST + t, k_tok)

                def scale_gu(half, bank):
                    dve.wait_ge(w_used, used(L, GU + half))
                    if half == 0:
                        dve.wait_ge(rb_ready, L * 3 + 2)
                    for b in range(2):
                        last = dve.tensor_tensor(out=gu[:, 2 * half + b, :], in0=ps[:, bank + b, :], in1=rb[:, :],
                                                 op=ALU.mult)
                    last.then_inc(gu_scaled, 1)

                def low_turned(n, hi, lo):
                    dve.wait_ge(qkT_rounded, L * 8 + n + 1)
                    t = n % ST
                    dve.tensor_tensor(out=lo[:, :, t * P:(t + 1) * P],
                                      in0=ps[:, t, :].rearrange("p (g c) -> p g c", c=P),
                                      in1=hi[:, :, t * P:(t + 1) * P].bitcast(f32), op=ALU.subtract)\
                       .then_inc(qkT_ready, 1)

                def gate_chunk(t):
                    dve.wait_ge(mix_done, L * 4 + t + 1)
                    if t == 0:
                        dve.wait_ge(gu_ready, L * 2 + 2)
                    if t >= 2:
                        dve.wait_ge(gm_ready, L * 4 + t - 1)
                    link(dve.tensor_tensor(out=tmp[:, t % 2, :], in0=ps[:, 6 + t % 2, :], in1=bs_b[:, :], op=ALU.add))
                    dve.tensor_tensor(out=tmp[:, t % 2, :].rearrange("p (g c) -> p g c", c=P),
                                      in0=tmp[:, t % 2, :].rearrange("p (g c) -> p g c", c=P),
                                      in1=gu[:, :, t * P:(t + 1) * P], op=ALU.mult).then_inc(gm_final, 1)

                def low_gm(t):
                    dve.wait_ge(gm_rounded, L * 4 + t + 1)
                    dve.tensor_tensor(out=gm_lo[:, :, t * P:(t + 1) * P],
                                      in0=tmp[:, t % 2, :].rearrange("p (g c) -> p g c", c=P),
                                      in1=gm_hi[:, :, t * P:(t + 1) * P].bitcast(f32), op=ALU.subtract)\
                       .then_inc(gm_ready, 1)

                def low_mg(half):
                    for n in range(4):
                        m = 4 * half + n
                        if n % 2 == 0:
                            dve.wait_ge(mg_rounded, L * 8 + m + 2)
                        dve.scalar_tensor_tensor(out=mg_lo[:, m, :], in0=ps[:, 4 + n // 2, (n % 2) * M:(n % 2 + 1) * M],
                                                 scalar=gains[:, ds(L * KT + G_MEM + m, 1)],
                                                 in1=mg_hi[:, m, :].bitcast(f32), op0=ALU.mult, op1=ALU.subtract)\
                           .then_inc(mg_ready, 1)

                scale_gu(0, 6)
                split_unit(L, VV)
                for t in range(ST):
                    low_turned(t, qT_hi, qT_lo)
                scale_gu(1, 4)
                split_unit(L, VV + 1)
                for t in range(ST):
                    low_turned(ST + t, kT_hi, kT_lo)
                gate_chunk(0)
                gate_chunk(1)
                low_gm(0)
                low_gm(1)
                low_mg(0)
                split_unit(L, CK)
                gate_chunk(2)
                low_gm(2)
                low_mg(1)
                for t in range(ST):
                    dve.wait_ge(v_rounded, L * 4 + t + 1)
                    dve.scalar_tensor_tensor(out=v_lo[:, t, :], in0=ps[:, t, :], scalar=rtok[:, t:t + 1],
                                             in1=v_hi[:, t, :].bitcast(f32), op0=ALU.mult, op1=ALU.subtract)\
                       .then_inc(v_ready, 1)
                gate_chunk(3)
                low_gm(3)
                split_unit(L, CK + 1)

                for s in range(22):
                    if s >= 5:
                        hd, part = divmod(s - 5, 4)
                        if part == 0 and hd >= 1:
                            dve.wait_ge(attn_rounded, L * 4 + hd)
                            dve.tensor_tensor(out=qT_lo[:, hd - 1, :], in0=tmp[:, 0, :],
                                              in1=qT_hi[:, hd - 1, :].bitcast(f32), op=ALU.subtract)\
                               .then_inc(attn_ready, 1)
                    if 2 <= s < 18:
                        n = s - 2
                        qb = n % 4
                        dve.wait_ge(wT_rounded, L * 16 + n + 1)
                        dve.tensor_tensor(out=wT_lo[:, 0:qb + 1, qb * P:(qb + 1) * P],
                                          in0=ps[:, 0, 0:(qb + 1) * P].rearrange("p (k c) -> p k c", c=P),
                                          in1=wT_hi[:, 0:qb + 1, qb * P:(qb + 1) * P].bitcast(f32),
                                          op=ALU.subtract).then_inc(wT_ready, 1)
                    if s < 16:
                        qb, b = s % 4, s % 2
                        N = (qb + 1) * P
                        dve.wait_ge(sc_done, L * 16 + s + 1)
                        link(dve.tensor_reduce(mx[:, b, :], ps[:, 4 + 2 * b:6 + 2 * b, 0:N], AX.X, ALU.max))
                        dve.tensor_scalar(nb[:, b, :], mx[:, b, :], -QK_SCALE, None, ALU.mult).then_inc(nb_ready, 1)
                    if 1 <= s < 17:
                        n = s - 1
                        qb, b = n % 4, n % 2
                        N = (qb + 1) * P
                        dve.wait_ge(exp_done, L * 16 + n + 1)
                        link(dve.reciprocal(rc[:, b, :], sm[:, b, :]))
                        link(dve.tensor_tensor(out=rc[:, b, 1:2], in0=rc[:, b, 1:2], in1=lam[:, ds(L, 1)], op=ALU.mult))
                        link(dve.tensor_scalar(ex[:, b, 1, 0:N], ex[:, b, 1, 0:N], rc[:, b, 1:2], None, ALU.mult))
                        dve.scalar_tensor_tensor(out=ex[:, b, 0, 0:N], in0=ex[:, b, 0, 0:N], scalar=rc[:, b, 0:1],
                                                 in1=ex[:, b, 1, 0:N], op0=ALU.mult, op1=ALU.subtract)\
                           .then_inc(attn_w_ready, 1)
                    if s % 2 == 0 and 2 <= s <= 16:
                        n = s // 2 - 1
                        dve.wait_ge(kv_rounded, L * 8 + n + 1)
                        hi, lo = ((kc_hi[:, 2 * n:2 * n + 2, :], kc_lo[:, 2 * n:2 * n + 2, :]) if n < 4
                                  else (vc_hi[n - 4][:, :, :], vc_lo[n - 4][:, :, :]))
                        dve.tensor_tensor(out=lo, in0=ps[:, 2, :].rearrange("p (k c) -> p k c", c=M),
                                          in1=hi.bitcast(f32), op=ALU.subtract).then_inc(kv_ready, 1)
                        split_unit(L, CK + n + 2)
                    if s >= 5:
                        hd, part = divmod(s - 5, 4)
                        if part == 1:
                            dve.wait_ge(ostat_done, L * 4 + hd + 1)
                            dve.tensor_scalar(msh[:, :], ps[:, 3, 0:ST], 1.0 / P, EPS, ALU.mult, ALU.add)\
                               .then_inc(oms_ready, 1)
                        if part == 3:
                            dve.wait_ge(orb_ready, L * 4 + hd + 1)
                            dve.scalar_tensor_tensor(out=tmp[:, 0, :], in0=ps[:, 1, :], scalar=gsub[:, ds(L, 1)],
                                                     in1=tmp[:, 1, :], op0=ALU.mult, op1=ALU.mult)\
                               .then_inc(attn_final, 1)

                def projected(stage, u, gcol):
                    for t in range(4):
                        for b in range(2):
                            add_tile(used(L, u + t), 2 * t + b, 4 + 2 * (t % 2) + b, 1.0)
                        for b in range(2):
                            low_tile(tile_no(L, stage, 2 * t + b), 2 * t + b, L * KT + gcol + 2 * t + b)
                        split_unit(L, u + t + 2)

                projected(1, WO, G_CROSS)
                mean_square(L * 4 + 3, 0)
                dve.wait_ge(r_ready, L * 4 + 3)
                link(dve.tensor_scalar(crs[:, :], rtok[:, :], CROSS_SCALE, None, ALU.mult))

                def low_qc(hd):
                    b = hd % 2
                    dve.wait_ge(qc_rounded, L * 4 + hd + 1)
                    dve.tensor_tensor(out=qc_lo[:, b, :, :], in0=ps[:, 4 + 2 * b:6 + 2 * b, :],
                                      in1=qc_hi[:, b, :, :].bitcast(f32), op=ALU.subtract).then_inc(qc_ready, 1)
                    split_unit(L, WQ + hd + 2)

                def cross_max(hd):
                    dve.wait_ge(csc_done, L * 4 + hd + 1)
                    link(dve.tensor_reduce(cmx[:, :], ps[:, 0:2, :].rearrange("p a (b m) -> p (a b) m", m=M),
                                           AX.X, ALU.max))
                    dve.scalar_tensor_tensor(out=cnb[:, :], in0=cmx[:, :], scalar=-1.0, in1=crs[:, :],
                                             op0=ALU.mult, op1=ALU.mult).then_inc(cnb_ready, 1)

                def cross_norm_w(hd):
                    dve.wait_ge(cexp_done, L * 4 + hd + 1)
                    link(dve.reciprocal(crc[:, :], csm[:, :]))
                    for qb in range(ST):
                        part = tmp[:, qb // 2, (qb % 2) * M:(qb % 2 + 1) * M]
                        last = dve.tensor_scalar(part, part, crc[:, qb:qb + 1], None, ALU.mult)
                    last.then_inc(cw_ready, 1)

                low_qc(0)
                low_qc(1)
                cross_max(0)
                cross_norm_w(0)
                low_qc(2)
                for hd in range(HEADS):
                    dve.wait_ge(wc_rounded, L * 4 + hd + 1)
                    dve.tensor_tensor(out=wc_lo[:, :, :], in0=ps[:, 2:4, :], in1=wc_hi[:, :, :].bitcast(f32),
                                      op=ALU.subtract).then_inc(wc_ready, 1)
                    if hd < 3:
                        cross_max(hd + 1)
                        cross_norm_w(hd + 1)
                    dve.wait_ge(o_rounded, L * 4 + hd + 1)
                    dve.tensor_tensor(out=o_lo[:, 2 * hd:2 * hd + 2, :], in0=ps[:, 2:4, :],
                                      in1=o_hi[:, 2 * hd:2 * hd + 2, :].bitcast(f32), op=ALU.subtract)\
                       .then_inc(o_ready, 1)
                    if hd == 0:
                        low_qc(3)

                projected(2, CO, G_FFN2)
                ffn(L, 1, UP2, DN2, 3, L * 4 + 4, G_FFN1 + KT, UNITS)
                assert count[0] == CHAIN, count[0]

            mean_square(LAYERS * 4 + 1, 6)
            for m in range(KT):
                dve.tensor_scalar(hg[:, m, :], h[:, m, :], gains[:, G_FINAL + m:G_FINAL + m + 1], None, ALU.mult)\
                   .then_inc(hg_ready, 1)

        @block.tensor
        def _(pe):
            def product(dst, a_hi, a_lo, b_hi, b_lo, start, stop, extra=None):
                pe.matmul(dst, a_hi, b_hi, start=start, stop=False)
                if extra:
                    extra()
                pe.matmul(dst, a_hi, b_lo, start=False, stop=False)
                return pe.matmul(dst, a_lo, b_hi, start=False, stop=stop)

            def wait_unit(L, u, i=0, per=2):
                pe.wait_ge(w_split, unit_no(L, u, i, per) + 3)

            def wtile(u, a, n=P):
                return w_hi[:, u % 2, a:a + n], w_lo[:, u % 2, a:a + n]

            def token_sums(sum_no_, bank):
                pe.wait_ge(sum_ready, sum_no_)
                for t in range(ST):
                    last = pe.matmul(ps[:, bank, t:t + 1], sumsq[:, t * P:(t + 1) * P], ones[:, 0:1],
                                     start=True, stop=True)
                last.then_inc(stat_done, 1)

            def broadcast(values, bank, done_sem):
                for t in range(ST):
                    last = pe.transpose(ps[:, bank, t * P:(t + 1) * P], values[:, t:t + 1].to_broadcast([P, P]),
                                        ident[:, :])
                last.then_inc(done_sem, 1)

            pe.wait_ge(setup_pool, 6)
            pe.wait_ge(consts_loaded, 16 * 8)
            pe.transpose(ps[:, 6, 0:90], rows[:, :], ident[0:90, 0:90]).then_inc(setup_pe, 1)
            pe.wait_ge(setup_dve, 9)
            pe.transpose(ps[:, 7, 0:ST], pos_f[:, :], ident[0:ST, 0:ST]).then_inc(setup_pe, 1)
            pe.wait_ge(x_loaded, 16 * ST)
            for m in range(KT):
                if m >= 4:
                    pe.wait_ge(h_ready, m - 3)
                for t in range(ST):
                    last = pe.transpose(ps[:, m % 4, t * P:(t + 1) * P], x_in[:, t, m * P:(m + 1) * P], ident[:, :])
                last.then_inc(x_turned, 1)

            def ffn(L, f, up, dn, stage):
                def up_unit(i, s, hook=None, waits=False):
                    u = up + s
                    wait_unit(L, u, i)
                    if not waits:
                        pe.wait_ge(up_read, ffn_no(L, f, 2 * i + s) - 2)
                    for k in range(KT):
                        if waits:
                            pe.wait_ge(hn_ready, hn_no(L, stage, k))
                        if hook and k == 4:
                            hook()
                        for g in range(2):
                            a_hi, a_lo = wtile(u, g * 1024 + k * P)
                            last = product(ps[:, 2 * s + g, :], a_hi, a_lo, hn_hi[:, k, :], hn_lo[:, k, :],
                                           k == 0, k == KT - 1)
                    last.then_inc(w_used, 1)
                    return last

                def send_rb():
                    pe.wait_ge(r_ready, L * 4 + (1 if f == 0 else 4))
                    broadcast(rtok, 7, rb_done)

                def body(i, where):
                    first = where == "first"
                    up_unit(i, 0, None, first)
                    if first:
                        token_sums(9 + (L * STAGES + stage) * 9, 6)
                    up_unit(i, 1, send_rb if first else None, first)
                up_loop(pe, body)

                def down_body(i, last_two):
                    for b in range(2):
                        m = 2 * i + b
                        pe.wait_ge(h_ready, tile_no(L, stage, m) - 2)
                        for s in range(2):
                            u = dn + 2 * b + s
                            wait_unit(L, u, i, 4)
                            pe.wait_ge(hid_ready, ffn_no(L, f, HK * (s + 1) - 1))
                            for k in range(HK):
                                a_hi, a_lo = wtile(u, k * P)
                                kk = s * HK + k
                                last = product(ps[:, 4 + b, :], a_hi, a_lo, hid_hi[:, kk, :], hid_lo[:, kk, :],
                                               kk == 0, kk == HT - 1)
                            last.then_inc(w_used, 1)
                down_loop(pe, down_body)

            def head_norm(L, hd, part):
                if part == 1:
                    pe.wait_ge(osq_ready, L * 4 + hd + 1)
                    for t in range(ST):
                        last = pe.matmul(ps[:, 3, t:t + 1], tmp[:, 0, t * P:(t + 1) * P], ones[:, 0:1],
                                         start=True, stop=True)
                    last.then_inc(ostat_done, 1)
                if part == 2:
                    pe.wait_ge(rh_ready, L * 4 + hd + 1)
                    broadcast(rh, 3, orb_done)

            def token_unit(L, u, s, bank, n_tok, src_hi, src_lo, stage=None, wait=None):
                wait_unit(L, u)
                for k4 in range(4):
                    k = 4 * s + k4
                    if stage is not None:
                        pe.wait_ge(hn_ready, hn_no(L, stage, k))
                    w1, w2 = wtile(u, k4 * 512, 512)
                    for t in range(n_tok):
                        if wait and k == 0:
                            wait(t)
                        last = product(ps[:, bank + t, :], src_hi[:, k, t * P:(t + 1) * P],
                                       src_lo[:, k, t * P:(t + 1) * P], w1, w2, k == 0, k == KT - 1)
                return last.then_inc(w_used, 1)

            def feature_unit(L, u, bank, ks, src, first=True, last_part=True, before=None):
                for k in ks:
                    if before:
                        before(k)
                    s_hi, s_lo = src(k)
                    for b in range(2):
                        a_hi, a_lo = wtile(u, k * 256 + b * P)
                        last = product(ps[:, bank + b, :], a_hi, a_lo, s_hi, s_lo,
                                       first and k == ks[0], last_part and k == ks[-1])
                return last

            with pe.Fori(0, LAYERS) as L:
                ffn(L, 0, UP1, DN1, 0)

                for s in range(2):
                    token_unit(L, GV + s, s, 0, ST, hn_hi, hn_lo, stage=1)
                token_sums(9 + (L * STAGES + 1) * 9, 7)
                def after_ms(t):
                    if t == 3:
                        pe.wait_ge(ms_ready, L * 4 + 2)
                for s in range(2):
                    token_unit(L, QQ + s, s, 4, ST, hn_hi, hn_lo, wait=after_ms)
                for s in range(2):
                    token_unit(L, KK + s, s, 0, ST, hn_hi, hn_lo,
                               wait=lambda t: pe.wait_ge(gelu_ready, L * 4 + t + 1))
                pe.wait_ge(qk_copied, L * 8 + 4)
                pe.wait_ge(r_ready, L * 4 + 2)
                broadcast(rtok, 4, rb_done)
                pe.wait_ge(ws_masked, L + 1)
                for g in range(HEADS):
                    last = pe.transpose(ps[:, 5, g * P:(g + 1) * P], wsr[:, g, :], ident[:, :])
                last.then_inc(ws_turned, 1)
                hn_tile = lambda k: (hn_hi[:, k, :], hn_lo[:, k, :])
                wait_unit(L, GU)
                last = feature_unit(L, GU, 6, range(KT), hn_tile)
                last.then_inc(w_used, 1)

                def turn(n, tok):
                    t = n % ST
                    pe.wait_ge(qk_roped, L * 8 + n + 1)
                    if n < ST:
                        pe.wait_ge(qk_copied, L * 8 + ST + t + 1)
                    else:
                        pe.wait_ge(qkT_ready, L * 8 + t + 1)
                    for hd in range(HEADS):
                        last = pe.transpose(ps[:, t, hd * P:(hd + 1) * P], tok[:, t, hd * P:(hd + 1) * P], ident[:, :])
                    last.then_inc(qk_turned, 1)

                for t in range(ST):
                    turn(t, q_tok)
                wait_unit(L, GU + 1)
                pe.wait_ge(rb_ready, L * 3 + 2)
                pe.wait_ge(wsT_ready, L + 1)
                last = feature_unit(L, GU + 1, 4, range(KT), hn_tile)
                last.then_inc(w_used, 1)
                for t in range(ST):
                    turn(ST + t, k_tok)
                def mix_chunk(t):
                    pe.wait_ge(vn_ready, L * 4 + t + 1)
                    if t == 0:
                        pe.wait_ge(gu_scaled, L * 2 + 1)
                    if t >= 2:
                        pe.wait_ge(gm_final, L * 4 + t - 1)
                    for g in range(HEADS):
                        c = slice(t * P, (t + 1) * P)
                        last = product(ps[:, 6 + t % 2, g * P:(g + 1) * P], gm_hi[:, g, c], gm_lo[:, g, c],
                                       wsT_hi[:, g, :], wsT_lo[:, g, :], True, True)
                    last.then_inc(mix_done, 1)

                def turn_memory(half):
                    if half == 0:
                        pe.wait_ge(mem_normed, L + 1)
                        pe.wait_ge(gu_scaled, L * 2 + 2)
                    else:
                        pe.wait_ge(mg_ready, L * 8 + 4)
                    for n in range(4):
                        for t in range(MT):
                            c = (n % 2) * M + t * P
                            m = 4 * half + n
                            last = pe.transpose(ps[:, 4 + n // 2, c:c + P], mem_in[:, t, m * P:(m + 1) * P], ident[:, :])
                    last.then_inc(mem_turned, 1)

                mix_chunk(0)
                mix_chunk(1)
                turn_memory(0)
                for s in range(2):
                    token_unit(L, VV + s, s, 0, ST, hn_hi, hn_lo,
                               wait=lambda t: pe.wait_ge(qkT_ready, L * 8 + 4 + t + 1))
                    mix_chunk(2 + s)
                    if s == 0:
                        turn_memory(1)

                def cat_tile(k):
                    return (gm_hi[:, k - 4, :], gm_lo[:, k - 4, :]) if k >= 4 else (qT_hi[:, k, :], qT_lo[:, k, :])

                def attn_out(t, ks):
                    last = feature_unit(L, WO + t, 4 + 2 * t, ks, cat_tile, first=ks[0] == 4, last_part=ks[-1] == 3,
                                        before=lambda k: pe.wait_ge(attn_ready, L * 4 + k + 1) if k < 4 else None)
                    if ks[-1] == 3:
                        last.then_inc(w_used, 1)

                for s in range(19):
                    if s < 16:
                        hd, qb, b = s // 4, s % 4, s % 2
                        N = (qb + 1) * P
                        if s == 0:
                            pe.wait_ge(mg_ready, L * 8 + 8)
                        if s == 1:
                            pe.wait_ge(gm_final, L * 4 + 4)
                        if s >= 2:
                            pe.wait_ge(exp_done, L * 16 + s - 1)
                        for br in range(2):
                            r = slice(64 * br, 64 * br + 64)
                            bank = 4 + 2 * b + br
                            q = slice(qb * P, (qb + 1) * P)

                            def mask():
                                pe.matmul(ps[:, bank, N - P:N], ident_r[:, :], mask_r[:, :], start=False, stop=False)
                            last = product(ps[:, bank, 0:N], qT_hi[r, hd, q], qT_lo[r, hd, q],
                                           kT_hi[r, hd, 0:N], kT_lo[r, hd, 0:N], True, True, extra=mask)
                        last.then_inc(sc_done, 1)
                        n, c = s // 2, s % 2
                        if c == 0:
                            wait_unit(L, CK + n)
                            if n:
                                pe.wait_ge(kv_ready, L * 8 + n)
                            else:
                                pe.wait_ge(v_ready, L * 4 + 4)
                        for k in range(KT):
                            dst = ps[:, 2, c * M:(c + 1) * M]
                            if n < 4:
                                a_hi, a_lo = wtile(CK + n, k * 256 + c * P)
                                last = product(dst, a_hi, a_lo, mg_hi[:, k, :], mg_lo[:, k, :], k == 0, k == KT - 1)
                            else:
                                b_hi, b_lo = wtile(CK + n, k * 256, 256)
                                m = slice(c * P, (c + 1) * P)
                                last = product(dst, mg_hi[:, k, m], mg_lo[:, k, m], b_hi, b_lo, k == 0, k == KT - 1)
                        if c == 1:
                            last.then_inc(w_used, 1)
                    if s == 16:
                        wait_unit(L, WO)
                        attn_out(0, [4, 5, 6, 7])
                    if s == 17:
                        attn_out(0, [0, 1])
                    if s >= 5:
                        hd, part = divmod(s - 5, 4)
                        if part == 0 and hd < 4:
                            pe.wait_ge(wT_ready, L * 16 + 4 * hd + 4)
                            if hd:
                                pe.wait_ge(attn_final, L * 4 + hd)
                            for kb in range(ST):
                                c = slice(hd * P, (hd + 1) * P)
                                last = product(ps[:, 1, kb * P:512], v_hi[:, kb, c], v_lo[:, kb, c],
                                               wT_hi[:, kb, kb * P:512], wT_lo[:, kb, kb * P:512], kb == 0, kb == 3)
                            last.then_inc(pv_done, 1)
                    if 1 <= s < 17:
                        n = s - 1
                        qb, b = n % 4, n % 2
                        pe.wait_ge(attn_w_ready, L * 16 + n + 1)
                        if n:
                            pe.wait_ge(wT_ready, L * 16 + n)
                        for kb in range(qb + 1):
                            last = pe.transpose(ps[:, 0, kb * P:(kb + 1) * P], ex[:, b, 0, kb * P:(kb + 1) * P],
                                                ident[:, :])
                        last.then_inc(attn_w_turned, 1)
                    if s >= 5:
                        head_norm(L, *divmod(s - 5, 4))

                wait_unit(L, WO + 1)
                attn_out(1, [4, 5, 6, 7])
                head_norm(L, 3, 2)
                attn_out(1, [0, 1])
                attn_out(0, [2, 3])
                attn_out(1, [2, 3])
                for t in range(2, 4):
                    wait_unit(L, WO + t)
                    pe.wait_ge(h_ready, tile_no(L, 1, 2 * t - 3))
                    feature_unit(L, WO + t, 4 + 2 * (t % 2), range(KT), cat_tile).then_inc(w_used, 1)

                def queries(hd):
                    wait_unit(L, WQ + hd)
                    if hd >= 2:
                        pe.wait_ge(qc_ready, L * 4 + hd - 1)
                    last = feature_unit(L, WQ + hd, 4 + 2 * (hd % 2), range(KT), hn_tile,
                                        before=(lambda k: pe.wait_ge(hn_ready, hn_no(L, 2, k))) if hd == 0 else None)
                    last.then_inc(w_used, 1)

                def cross_scores(hd):
                    pe.wait_ge(qc_ready, L * 4 + hd + 1)
                    if hd:
                        pe.wait_ge(cexp_done, L * 4 + hd)
                    else:
                        pe.wait_ge(ms_ready, L * 4 + 3)
                    for qb in range(ST):
                        for d in range(2):
                            q = slice(qb * P, (qb + 1) * P)
                            last = product(ps[:, qb // 2, (qb % 2) * M:(qb % 2 + 1) * M],
                                           qc_hi[:, hd % 2, d, q], qc_lo[:, hd % 2, d, q],
                                           kc_hi[:, 2 * hd + d, :], kc_lo[:, 2 * hd + d, :], d == 0, d == 1)
                    last.then_inc(csc_done, 1)

                def cross_turn(hd):
                    pe.wait_ge(cw_ready, L * 4 + hd + 1)
                    if hd:
                        pe.wait_ge(o_ready, L * 4 + hd)
                    for t in range(MT):
                        for qb in range(ST):
                            c0 = (qb % 2) * M + t * P
                            last = pe.transpose(ps[:, 2 + t, qb * P:(qb + 1) * P], tmp[:, qb // 2, c0:c0 + P], ident[:, :])
                    last.then_inc(cw_turned, 1)

                def cross_values(hd):
                    pe.wait_ge(wc_ready, L * 4 + hd + 1)
                    for d in range(2):
                        for t in range(MT):
                            c = slice(d * P, (d + 1) * P)
                            last = product(ps[:, 2 + d, :], vc_hi[hd][:, t, c], vc_lo[hd][:, t, c],
                                           wc_hi[:, t, :], wc_lo[:, t, :], t == 0, t == 1)
                    last.then_inc(cpv_done, 1)

                def cross_out(t, ks):
                    if ks[0] == 0:
                        wait_unit(L, CO + t)
                        pe.wait_ge(qc_ready, L * 4 + 3 + t)
                    last = feature_unit(L, CO + t, 4 + 2 * t, ks, lambda k: (o_hi[:, k, :], o_lo[:, k, :]),
                                        first=ks[0] == 0, last_part=ks[-1] == 7,
                                        before=lambda k: pe.wait_ge(o_ready, L * 4 + k // 2 + 1))
                    if ks[-1] == 7:
                        last.then_inc(w_used, 1)

                queries(0)
                token_sums(9 + (L * STAGES + 2) * 9, 0)
                queries(1)
                cross_scores(0)
                queries(2)
                cross_turn(0)
                cross_scores(1)
                cross_values(0)
                queries(3)
                cross_turn(1)
                cross_scores(2)
                cross_values(1)
                cross_out(0, [0, 1])
                cross_out(1, [0, 1])
                cross_turn(2)
                cross_scores(3)
                cross_out(0, [2, 3])
                cross_values(2)
                cross_out(1, [2, 3])
                cross_turn(3)
                cross_out(0, [4, 5])
                cross_values(3)
                cross_out(1, [4, 5])
                cross_out(0, [6, 7])
                cross_out(1, [6, 7])
                for t in range(2, 4):
                    wait_unit(L, CO + t)
                    pe.wait_ge(h_ready, tile_no(L, 2, 2 * t - 3))
                    feature_unit(L, CO + t, 4 + 2 * (t % 2), range(KT), lambda k: (o_hi[:, k, :], o_lo[:, k, :]))\
                        .then_inc(w_used, 1)

                ffn(L, 1, UP2, DN2, 3)

            token_sums(9 + LAYERS * STAGES * 9, 6)
            pe.wait_ge(hg_ready, KT)
            for t in range(ST):
                if t >= 2:
                    pe.wait_ge(fin_ready, t - 1)
                for m in range(KT):
                    last = pe.transpose(ps[:, 2 * (t % 2) + m // 4, (m % 4) * P:(m % 4 + 1) * P],
                                        hg[:, m, t * P:(t + 1) * P], ident[:, :])
                last.then_inc(fin_turned, 1)


_INS = ['x', 'mem', 'positions', 'ffn1_norm', 'ffn1_wgu', 'ffn1_wd', 'mix_norm', 'w_in', 'lam_q1', 'lam_k1',
        'lam_q2', 'lam_k2', 'subln', 'gmlp_ln_g', 'gmlp_ln_b', 'gmlp_ws', 'gmlp_bs', 'w_out', 'cross_norm',
        'mem_norm', 'cross_wq', 'cross_wkv', 'cross_wo', 'ffn2_norm', 'ffn2_wgu', 'ffn2_wd', 'final_norm']


def kernel(**inputs):
    import numpy as _np
    import concourse.bacc as _bacc
    from concourse import mybir as _mybir
    from concourse.bass_utils import run_bass_kernel_spmd as _run

    nc = _bacc.Bacc("TRN2", target_bir_lowering=False, num_devices=1)
    arrays, args = {}, []
    for name in _INS:
        a = _np.ascontiguousarray(inputs[name])
        arrays[f"in_{name}_dram"] = a
        args.append(nc.dram_tensor(f"in_{name}_dram", a.shape, _mybir.dt.from_np(a.dtype), kind="ExternalInput").ap())
    args.append(nc.dram_tensor("out_dram", (1, S, D), _mybir.dt.float32, kind="ExternalOutput").ap())
    macaron_kernel(nc, *args)
    r = _run(nc, [arrays], core_ids=[0])
    return r.results[0]["out_dram"]
```

```python
import math
from contextlib import ExitStack

import numpy as np
import concourse.bass as bass
from concourse import mybir

P = 128
D = 1024
S = 512
M = 256
LAYERS = 2
FF = 2816
KT = D // P
ST = S // P
MT = M // P
HT = FF // P
HK = HT // 2
HEADS = 4
HALF = 8
EPS = 1e-6
QK_SCALE = 64.0 ** -0.5
CROSS_SCALE = 256.0 ** -0.5
NEG = -1e30

UP1 = 0
DN1 = UP1 + HT
GV = DN1 + 16
QQ = GV + 2
KK = QQ + 2
GU = KK + 2
VV = GU + 2
CK = VV + 2
CV = CK + 4
WO = CV + 4
WQ = WO + 4
CO = WQ + 4
UP2 = CO + 4
DN2 = UP2 + HT
UNITS = DN2 + 16
assert UNITS % 2 == 0

STAGES = 4


G_FFN1, G_FINAL, G_MIX, G_CROSS, G_FFN2, G_MEM, G_SUBLN = 0, 16, 24, 40, 56, 72, 88


def unit_size(u):
    u %= UNITS
    return HK * P if DN1 <= u < GV or u >= DN2 else 2048


def macaron_kernel(nc, x, mem, positions, ffn1_norm, ffn1_wgu, ffn1_wd, mix_norm, w_in,
                   lam_q1, lam_k1, lam_q2, lam_k2, subln, gmlp_ln_g, gmlp_ln_b, gmlp_ws,
                   gmlp_bs, w_out, cross_norm, mem_norm, cross_wq, cross_wkv, cross_wo,
                   ffn2_norm, ffn2_wgu, ffn2_wd, final_norm, out):
    f32 = mybir.dt.float32
    f32r = mybir.dt.float32r
    i32 = mybir.dt.int32
    ALU = mybir.AluOpType
    ACT = mybir.ActivationFunctionType
    AX = mybir.AxisListType
    ds = bass.ds

    ctx = ExitStack()
    with ctx:
        def sem(name):
            return ctx.enter_context(nc.semaphore(name))

        top = [16512]

        def sb(name, shape, dt=f32, at=None):
            size = 4 * int(np.prod(shape[1:]))
            size += -size % 32
            if at is None:
                at = top[0]
                top[0] += size
            return nc.alloc_sbuf_tensor_at(name, shape, dt, offset=at)

        h = sb("h", [P, KT, S])
        hn_at = top[0]
        hn_hi = sb("hn_hi", [P, KT, S], f32r)
        hn_lo = sb("hn_lo", [P, KT, S], f32r)
        aux_at = top[0]
        mem_in = sb("mem_in", [P, MT, D])
        raw = sb("raw", [P, 2, 2048])
        w_hi = sb("w_hi", [P, 2, 2048], f32r)
        w_lo = sb("w_lo", [P, 2, 2048], f32r)
        sumsq_at = top[0]
        sumsq = sb("sumsq", [P, S])
        rb = sb("rb", [P, S])
        tmp = sb("tmp", [P, 3, S])
        ident = sb("ident", [P, P])
        ones = sb("ones", [P, P])
        ident_r = sb("ident_r", [P, P], f32r)
        mask_r = sb("mask_r", [P, P], f32r)
        wsr = sb("wsr", [P, HEADS, P])
        gains = sb("gains", [P, 90])
        rope = sb("rope", [P, ST, 2, 2 * HALF])
        rtok = sb("rtok", [P, ST])
        msq = sb("msq", [P, ST])
        m_half = sb("m_half", [P, 16])
        neg_lam = sb("neg_lam", [P, LAYERS])
        gsub = sb("gsub", [P, LAYERS])
        mv = sb("mv", [P, ST, HEADS, 2])
        rstd = sb("rstd", [P, ST, HEADS])
        vareps = sb("vareps", [P, ST, HEADS])
        mx = sb("mx", [P, 2, 2])
        nb = sb("nb", [P, 2, 2])
        sm = sb("sm", [P, 2, 2])
        rs = sb("rs", [P, HEADS, 2, ST])
        ratio = sb("ratio", [P, 2])
        msh = sb("msh", [P, ST])
        mss = sb("mss", [P, 3, MT])
        rh = sb("rh", [P, ST])
        cmx = sb("cmx", [P, ST])
        cnb = sb("cnb", [P, ST])
        csm = sb("csm", [P, ST])
        crc = sb("crc", [P, ST])
        crs = sb("crs", [P, ST])
        sh = top[0]
        assert sh + 2 * HT * S * 4 <= 229344, sh + 2 * HT * S * 4
        K1 = 1024
        hid_hi = sb("hid_hi", [P, HT, S], f32r, sh)
        hid_lo = sb("hid_lo", [P, HT, S], f32r, sh + 44 * K1)
        gu = sb("gu", [P, HEADS, S], f32, sh)
        wsT_hi = sb("wsT_hi", [P, HEADS, P], f32r, sh + 8 * K1)
        wsT_lo = sb("wsT_lo", [P, HEADS, P], f32r, sh + 10 * K1)
        ln_g = sb("ln_g", [P, HEADS * P], f32, sh + 12 * K1)
        ln_b = sb("ln_b", [P, HEADS * P], f32, sh + 14 * K1)
        bs_b = sb("bs_b", [P, HEADS * P], f32, sumsq_at)
        bst = sb("bst", [P, ST, HEADS, 6], f32, sh + 32 * K1)
        k_tok = sb("k_tok", [P, ST, S], f32, sh + 24 * K1)
        mg_hi = sb("mg_hi", [P, KT, M], f32r, sh + 16 * K1)
        mg_lo = sb("mg_lo", [P, KT, M], f32r, sh + 24 * K1)
        kc_hi = sb("kc_hi", [P, KT, M], f32r, sh)
        kc_lo = sb("kc_lo", [P, KT, M], f32r, sh + 8 * K1)
        vc_at = [(aux_at, aux_at + 4 * K1), (aux_at + 2 * K1, aux_at + 6 * K1),
                 (sh + 64 * K1, sh + 72 * K1), (sh + 66 * K1, sh + 74 * K1)]
        vc_hi = [sb(f"vc_hi{n}", [P, MT, 256], f32r, a) for n, (a, _) in enumerate(vc_at)]
        vc_lo = [sb(f"vc_lo{n}", [P, MT, 256], f32r, a) for n, (_, a) in enumerate(vc_at)]
        qT_hi = sb("qT_hi", [P, HEADS, S], f32r, sh + 32 * K1)
        qT_lo = sb("qT_lo", [P, HEADS, S], f32r, sh + 40 * K1)
        gm_hi = sb("gm_hi", [P, HEADS, S], f32r, sh + 48 * K1)
        gm_lo = sb("gm_lo", [P, HEADS, S], f32r, sh + 56 * K1)
        kT_hi = sb("kT_hi", [P, HEADS, S], f32r, sh + 64 * K1)
        kT_lo = sb("kT_lo", [P, HEADS, S], f32r, sh + 72 * K1)
        q_tok = sb("q_tok", [P, ST, S], f32, sh + 80 * K1)
        ex = sb("ex", [P, 2, 2, S], f32, sh + 80 * K1)
        v_hi = sb("v_hi", [P, ST, S], f32r, hn_at)
        v_lo = sb("v_lo", [P, ST, S], f32r, hn_at + 8 * K1)
        wT_hi = sb("wT_hi", [P, ST, S], f32r, hn_at + 16 * K1)
        wT_lo = sb("wT_lo", [P, ST, S], f32r, hn_at + 24 * K1)
        qc_hi = sb("qc_hi", [P, 2, 2, S], f32r, sh + 16 * K1)
        qc_lo = sb("qc_lo", [P, 2, 2, S], f32r, sh + 24 * K1)
        o_hi = sb("o_hi", [P, KT, S], f32r, sh + 32 * K1)
        o_lo = sb("o_lo", [P, KT, S], f32r, sh + 48 * K1)
        wc_hi = sb("wc_hi", [P, MT, S], f32r, sh + 80 * K1)
        wc_lo = sb("wc_lo", [P, MT, S], f32r, sh + 84 * K1)
        x_in = sb("x_in", [P, ST, D], f32, sh)
        rows = sb("rows", [90, P], f32, sh + 28 * K1)
        lam_in = sb("lam_in", [P, 4, LAYERS * 64], f32, sh + 29 * K1)
        lam_pr = sb("lam_pr", [P, 2, LAYERS, 64], f32, sh + 31 * K1)
        lam_s = sb("lam_s", [P, 2, LAYERS], f32, sh + 32 * K1)
        pos_i = sb("pos_i", [ST, P], i32, sh + 33 * K1)
        pos_f = sb("pos_f", [ST, P], f32, sh + 34 * K1)
        pos_t = sb("pos_t", [P, ST], f32, sh + 35 * K1)
        invf = sb("invf", [P, HALF], f32, sh + 36 * K1)
        ang = sb("ang", [P, 5, ST, HALF], f32, sh + 37 * K1)
        o_sb = sb("o_sb", [P, ST, D], f32, sh + 16 * K1)

        FIN_BANK = (0, 2, 6, 4)
        ps = ctx.enter_context(nc.psum_tensor("ps", [P, 8, 512], f32))

        x_loaded = [sem(f"x_loaded{t}") for t in range(ST)]
        ffn1_gain_loaded = sem("ffn1_gain_loaded")
        gains_loaded = sem("gains_loaded")
        half_rounded = sem("half_rounded")
        pos_loaded = sem("pos_loaded")
        lam_loaded = sem("lam_loaded")
        mem_loaded = sem("mem_loaded")
        setup_pool = sem("setup_pool")
        setup_dve = sem("setup_dve")
        setup_act = sem("setup_act")
        setup_pe = sem("setup_pe")
        w_loaded = [sem("w_loaded0"), sem("w_loaded1")]
        w_rounded = sem("w_rounded")
        w_split = sem("w_split")
        w_used = sem("w_used")
        x_turned = sem("x_turned")
        mem_sq_ready = sem("mem_sq_ready")
        mem_ms_ready = sem("mem_ms_ready")
        mem_r_ready = sem("mem_r_ready")
        lam_sums_ready = sem("lam_sums_ready")
        angles_ready = sem("angles_ready")
        mem_normed = sem("mem_normed")
        mem_turned = sem("mem_turned")
        h_ready = sem("h_ready")
        hn_rounded = sem("hn_rounded")
        hn_ready = sem("hn_ready")
        sq_ready = sem("sq_ready")
        sum_ready = sem("sum_ready")
        stat_done = sem("stat_done")
        ms_ready = sem("ms_ready")
        r_ready = sem("r_ready")
        rb_done = sem("rb_done")
        rb_ready = sem("rb_ready")
        gate_ready = sem("gate_ready")
        up_read = sem("up_read")
        silu_ready = sem("silu_ready")
        prod_ready = sem("prod_ready")
        hid_rounded = sem("hid_rounded")
        hid_ready = sem("hid_ready")
        small_loaded = sem("small_loaded")
        ws_masked = sem("ws_masked")
        gelu_ready = sem("gelu_ready")
        var_ready = sem("var_ready")
        rstd_ready = sem("rstd_ready")
        vn_final = sem("vn_final")
        vn_rounded = sem("vn_rounded")
        vn_ready = sem("vn_ready")
        qk_copied = sem("qk_copied")
        qk_roped = sem("qk_roped")
        qk_turned = sem("qk_turned")
        qkT_rounded = sem("qkT_rounded")
        qkT_ready = sem("qkT_ready")
        ws_turned = sem("ws_turned")
        wsT_rounded = sem("wsT_rounded")
        wsT_ready = sem("wsT_ready")
        gu_scaled = sem("gu_scaled")
        gu_ready = sem("gu_ready")
        mix_done = sem("mix_done")
        gm_final = sem("gm_final")
        gm_rounded = sem("gm_rounded")
        gm_ready = sem("gm_ready")
        v_rounded = sem("v_rounded")
        v_ready = sem("v_ready")
        mg_rounded = sem("mg_rounded")
        mg_ready = sem("mg_ready")
        sc_done = sem("sc_done")
        nb_ready = sem("nb_ready")
        exp_done = sem("exp_done")
        attn_w_ready = sem("attn_w_ready")
        attn_w_turned = sem("attn_w_turned")
        wT_rounded = sem("wT_rounded")
        wT_ready = sem("wT_ready")
        pv_done = sem("pv_done")
        osq_ready = sem("osq_ready")
        ostat_done = sem("ostat_done")
        oms_ready = sem("oms_ready")
        rh_powered = sem("rh_powered")
        rh_ready = sem("rh_ready")
        orb_done = sem("orb_done")
        orb_ready = sem("orb_ready")
        attn_final = sem("attn_final")
        attn_rounded = sem("attn_rounded")
        attn_ready = sem("attn_ready")
        kv_rounded = sem("kv_rounded")
        kv_ready = sem("kv_ready")
        qc_rounded = sem("qc_rounded")
        qc_ready = sem("qc_ready")
        csc_done = sem("csc_done")
        cnb_ready = sem("cnb_ready")
        cexp_done = sem("cexp_done")
        cw_ready = sem("cw_ready")
        cw_turned = sem("cw_turned")
        wc_rounded = sem("wc_rounded")
        wc_ready = sem("wc_ready")
        cpv_done = sem("cpv_done")
        o_rounded = sem("o_rounded")
        o_ready = sem("o_ready")
        dve_chain = sem("dve_chain")
        fin_turned = sem("fin_turned")
        fin_ready = sem("fin_ready")
        fin_ready_v = sem("fin_ready_v")
        out_stored = sem("out_stored")

        CHAIN = ST * 4 + 2 * ST + ST + 16 * 3 + HEADS * 2 + 1 + 2 * HEADS

        def unit_no(L, u, i=0, per=2):
            return L * UNITS + u + per * i

        def used(L, u, i=0, per=2):
            return unit_no(L, u, i, per) + 3

        def tile_no(L, stage, m):
            return KT + (L * STAGES + stage) * KT + m + 1

        def hn_no(L, stage, t):
            return (L * STAGES + stage) * KT + t + 1

        def sum_no(L, stage, m):
            return 9 + (L * STAGES + stage) * 9 + m + 2

        def ffn_no(L, f, j):
            return (L * 2 + f) * HT + j + 1

        def wait_apart(eng, signal, value):
            eng.compute_val(value)
            eng.wait_ge(setup_pool, 1)
            eng.wait_ge(signal, value)

        def down_loop(eng, body):
            with eng.Fori(0, KT // 2 - 1) as i:
                body(i, False)
            body(KT // 2 - 1, True)

        def up_loop(eng, body):
            body(0, "first")
            with eng.Fori(1, HT // 2 - 1) as i:
                body(i, "")
            body(HT // 2 - 1, "last")

        block = ctx.enter_context(nc.Block())

        @block.sync
        def _(sp):
            def load(L, u, i, per, parts):
                assert len(parts) == 2
                wait_apart(sp, w_split, unit_no(L, u, i, per) + 1)
                for (a, k, c, src) in parts:
                    dst = raw[:, u % 2, a:a + k * c].rearrange("p (k c) -> p k c", c=c)
                    sp.dma_start(dst, src.rearrange("o (k p) c -> (o p) k c", p=P))\
                      .then_inc(w_loaded[u % 2], 16)

            def ffn_loads(L, up, dn, wgu, wd):
                with sp.Fori(0, HT // 2) as i:
                    for s in range(2):
                        col = i * (2 * P) + s * P
                        load(L, up + s, i, 2, [(0, KT, P, wgu[ds(L, 1), :, ds(col, P)]),
                                               (1024, KT, P, wgu[ds(L, 1), :, ds(col + FF, P)])])
                with sp.Fori(0, KT) as m:
                    for s in range(2):
                        k0 = s * HK
                        load(L, dn + s, m, 2,
                             [(0, 6, P, wd[ds(L, 1), k0 * P:(k0 + 6) * P, ds(m * P, P)]),
                              (768, HK - 6, P, wd[ds(L, 1), (k0 + 6) * P:(k0 + HK) * P, ds(m * P, P)])])

            def token_loads(L, u, w, col):
                for s in range(2):
                    load(L, u + s, 0, 2,
                         [(n * 1024, 2, 512, w[ds(L, 1), (4 * s + 2 * n) * P:(4 * s + 2 * n + 2) * P, col:col + 512])
                          for n in range(2)])

            def feature_loads(L, u, w, col, n_units):
                for t in range(n_units):
                    c0 = col + t * 256
                    load(L, u + t, 0, 2,
                         [(n * 1024, 4, 256, w[ds(L, 1), n * 512:(n + 1) * 512, c0:c0 + 256]) for n in range(2)])

            for t in range(ST):
                sp.dma_start(x_in[:, t, :], x[0, t * P:(t + 1) * P, :]).then_inc(x_loaded[t], 16)
            with sp.Fori(0, LAYERS) as L:
                ffn_loads(L, UP1, DN1, ffn1_wgu, ffn1_wd)
                token_loads(L, GV, w_in, 2048)
                token_loads(L, QQ, w_in, 0)
                token_loads(L, KK, w_in, 512)
                feature_loads(L, GU, w_in, 1536, 2)
                token_loads(L, VV, w_in, 1024)
                feature_loads(L, CK, cross_wkv, 0, 8)
                feature_loads(L, WO, w_out, 0, 4)
                feature_loads(L, WQ, cross_wq, 0, 4)
                feature_loads(L, CO, cross_wo, 0, 4)
                ffn_loads(L, UP2, DN2, ffn2_wgu, ffn2_wd)
            for s in range(2):
                load(LAYERS, s, 0, 2, [(g * 1024, KT, P, ffn1_wgu[0:1, :, g * FF + s * P:g * FF + (s + 1) * P])
                                       for g in range(2)])
            for t in range(ST):
                sp.wait_ge(fin_ready if t % 2 == 0 else fin_ready_v, t // 2 + 1)
                sp.dma_start(out[0, t * P:(t + 1) * P, :], o_sb[:, t, :]).then_inc(out_stored, 16)
            sp.wait_ge(out_stored, 16 * ST)

        @block.gpsimd
        def _(pool):
            pool.memset(ident[:, :], 0.0).then_inc(setup_pool, 1)
            pool.memset(ones[:, :], 1.0).then_inc(setup_pool, 1)
            pool.memset(rb[:, 0:P], 0.0).then_inc(setup_pool, 1)
            pool.memset(m_half[:, :], -0.5).then_inc(setup_pool, 1)
            pool.wait_ge(setup_pool, 4)
            pool.affine_select(out=ident[:, :], in_=ident[:, :], compare_op=ALU.not_equal, fill=1.0,
                               base=0, pattern=[[-1, P]], channel_multiplier=1).then_inc(setup_pool, 1)
            pool.affine_select(out=rb[:, 0:P], in_=rb[:, 0:P], compare_op=ALU.is_ge, fill=NEG,
                               base=0, pattern=[[-1, P]], channel_multiplier=1).then_inc(setup_pool, 1)

            def clear_sum(first_sum):
                pool.memset(sumsq[:, :], 0.0).then_inc(sum_ready, 1)

            def add_square(sq_no, before, m2):
                pool.wait_ge(sq_ready, sq_no)
                pool.wait_ge(sum_ready, before)
                pool.tensor_tensor(out=sumsq[:, :], in0=sumsq[:, :], in1=tmp[:, m2, :], op=ALU.add)\
                    .then_inc(sum_ready, 1)

            def inverse_rms(n):
                pool.wait_ge(ms_ready, n)
                pool.tensor_tensor(out=rtok[:, :], in0=msq[:, :], in1=m_half[:, 0:ST], op=ALU.pow)\
                    .then_inc(r_ready, 1)

            clear_sum(0)
            for m in range(KT):
                add_square(m + 1, m + 1, m % 2)

            def stage_sums(L, stage, stats_before):
                wait_apart(pool, stat_done, L * 4 + stats_before)
                clear_sum(0)
                if stage in (0, 3):
                    def body(i, last):
                        for b in range(2):
                            m = 2 * i + b
                            add_square(tile_no(L, stage, m), sum_no(L, stage, m) - 1, b)
                    down_loop(pool, body)
                else:
                    for m in range(KT):
                        add_square(tile_no(L, stage, m), sum_no(L, stage, m) - 1, m % 2)

            with pool.Fori(0, LAYERS) as L:
                inverse_rms(L * 4 + 1)
                stage_sums(L, 0, 1)
                inverse_rms(L * 4 + 2)
                wait_apart(pool, small_loaded, L * 64 + 64)
                pool.affine_select(out=wsr[:, :, :], in_=wsr[:, :, :], compare_op=ALU.is_ge, fill=0.0,
                                   base=0, pattern=[[0, HEADS], [-1, P]], channel_multiplier=1)\
                    .then_inc(ws_masked, 1)
                pool.wait_ge(var_ready, L + 1)
                pool.tensor_tensor(out=rstd[:, :, :], in0=vareps[:, :, :],
                                   in1=m_half[:, :].rearrange("p (a b) -> p a b", b=HEADS), op=ALU.pow)\
                    .then_inc(rstd_ready, 1)
                pool.wait_ge(mem_ms_ready, L + 1)
                pool.tensor_tensor(out=mss[:, 2, :], in0=mss[:, 1, :], in1=m_half[:, 0:MT], op=ALU.pow)\
                    .then_inc(mem_r_ready, 1)
                for hd in range(HEADS):
                    pool.wait_ge(oms_ready, L * 4 + hd + 1)
                    pool.tensor_tensor(out=rh[:, :], in0=msh[:, :], in1=m_half[:, 0:ST], op=ALU.pow)\
                        .then_inc(rh_powered, 1)
                    pool.wait_ge(rh_powered, L * 4 + hd + 1)
                    pool.tensor_tensor(out=rh[:, :], in0=rh[:, :], in1=rs[:, hd, 0, :], op=ALU.mult)\
                        .then_inc(rh_ready, 1)
                stage_sums(L, 1, 2)
                inverse_rms(L * 4 + 3)
                stage_sums(L, 2, 3)
                inverse_rms(L * 4 + 4)
                stage_sums(L, 3, 4)
            inverse_rms(LAYERS * 4 + 1)

        @block.scalar
        def _(act):
            def load_gains(dst, src):
                act.dma_start(dst, src).then_inc(gains_loaded, 16)

            act.dma_start(rows[G_FFN1:G_FFN1 + LAYERS * KT, :], ffn1_norm.rearrange("l (t p) -> (l t) p", p=P))\
               .then_inc(ffn1_gain_loaded, 16)
            for col, g in ((G_MIX, mix_norm), (G_CROSS, cross_norm), (G_FFN2, ffn2_norm),
                           (G_MEM, mem_norm)):
                load_gains(rows[col:col + LAYERS * KT, :], g.rearrange("l (t p) -> (l t) p", p=P))
            load_gains(rows[G_FINAL:G_FINAL + KT, :], final_norm.rearrange("(t p) -> t p", p=P))
            load_gains(rows[G_SUBLN:G_SUBLN + LAYERS, :], subln)
            act.dma_start(pos_i[:, :], positions[0].rearrange("(t p) -> t p", p=P)).then_inc(pos_loaded, 16)
            for n, v in enumerate([lam_q1, lam_k1, lam_q2, lam_k2]):
                act.dma_start(lam_in[:, n, :], v.rearrange("l d -> (l d)").unsqueeze(0).to_broadcast([P, LAYERS * 64]))\
                   .then_inc(lam_loaded, 16)

            act.wait_ge(setup_pool, 6)
            act.activation(ident_r[:, :], ident[:, :], ACT.Copy).then_inc(setup_act, 1)
            act.activation(mask_r[:, :], rb[:, 0:P], ACT.Copy).then_inc(setup_act, 1)

            def round_unit(L, u, i=0, per=2):
                n = unit_no(L, u, i, per)
                s = u % 2
                act.wait_ge(w_loaded[s], 32 * (L * (UNITS // 2) + u // 2 + (per // 2) * i + 1))
                act.wait_ge(w_used, n + 1)
                z = unit_size(u)
                act.activation(w_hi[:, s, 0:z], raw[:, s, 0:z], ACT.Copy).then_inc(w_rounded, 1)

            def round_tile(no, m, gcol):
                wait_apart(act, h_ready, no)
                act.activation(hn_hi[:, ds(m, 1), :], h[:, ds(m, 1), :], ACT.Copy,
                               scale=gains[:, ds(gcol, 1)]).then_inc(hn_rounded, 1)

            def square_tile(m, b, sum_before):
                if sum_before is not None:
                    wait_apart(act, sum_ready, sum_before)
                act.activation(tmp[:, b:b + 1, :], h[:, ds(m, 1), :], ACT.Square).then_inc(sq_ready, 1)

            def copy_rb(n, bank):
                act.wait_ge(rb_done, n)
                act.activation(rb[:, :], ps[:, bank, :], ACT.Copy).then_inc(rb_ready, 1)

            def first_unit():
                act.wait_ge(w_loaded[0], 32)
                act.activation(w_hi[:, 0, 0:1024], raw[:, 0, 0:1024], ACT.Copy).then_inc(half_rounded, 1)
                act.activation(w_hi[:, 0, 1024:2048], raw[:, 0, 1024:2048], ACT.Copy).then_inc(w_rounded, 1)

            act.wait_ge(setup_dve, HALF + 1)
            for m in range(KT):
                round_tile(KT, m, m)
                if m == 2:
                    first_unit()
                if m == KT - 1:
                    round_unit(0, 1)
                if m >= 1:
                    square_tile(m - 1, (m - 1) % 2, m - 1 if m >= 3 else None)
            square_tile(KT - 1, 1, KT - 1)
            act.wait_ge(lam_sums_ready, 1)
            act.activation(lam_s[:, :, :], lam_s[:, :, :], ACT.Exp).then_inc(setup_act, 1)
            act.wait_ge(angles_ready, 1)
            act.activation(ang[:, 3, :, :], ang[:, 1, :, :], ACT.Sin).then_inc(setup_act, 1)
            act.activation(ang[:, 4, :, :], ang[:, 2, :, :], ACT.Sin).then_inc(setup_act, 1)

            def ffn(L, f, up, dn, stage, rb_no, next_gain, next_unit):
                def up_body(i, where):
                    if where == "first":
                        copy_rb(rb_no, 7)
                    for s in range(2):
                        u = up + s
                        if where == "last":
                            round_unit(L, dn + s)
                        else:
                            round_unit(L, u + 2, i)
                        n = ffn_no(L, f, 2 * i + s)
                        act.wait_ge(gate_ready, n)
                        act.activation(tmp[:, 1, :], tmp[:, 0, :], ACT.Silu).then_inc(silu_ready, 1)
                        wait_apart(act, prod_ready, n)
                        act.activation(hid_hi[:, ds(2 * i + s, 1), :], tmp[:, 1:2, :], ACT.Copy)\
                           .then_inc(hid_rounded, 1)
                up_loop(act, up_body)

                def down_body(i, last):
                    for b in range(2):
                        m = 2 * i + b
                        no = tile_no(L, stage, m)
                        at_end = last and b == 1
                        for s in range(2):
                            if s == 1:
                                round_tile(no, m, L * KT + next_gain + m)
                                if at_end:
                                    square_tile(m, b, sum_no(L, stage, m) - 2)
                            if not at_end:
                                round_unit(L, dn + 2 * b + 2 + s, i, 4)
                            else:
                                round_unit(L, next_unit + s)
                        if not at_end:
                            square_tile(m, b, sum_no(L, stage, m) - 2)
                down_loop(act, down_body)

            with act.Fori(0, LAYERS) as L:
                ffn(L, 0, UP1, DN1, 0, L * 3 + 1, G_MIX, GV)

                act.wait_ge(hn_ready, hn_no(L, 1, KT - 1))
                for t in range(MT):
                    act.dma_start(mem_in[:, t, :], mem[0, t * P:(t + 1) * P, :]).then_inc(mem_loaded, 16)
                act.dma_start(wsr[:, :, :], gmlp_ws[ds(L, 1)].rearrange("o g t s -> (o t) g s")).then_inc(small_loaded, 16)

                def load_vector(dst, src):
                    act.dma_start(dst[:, :], src[ds(L, 1)].rearrange("o g c -> o (g c)").to_broadcast([P, HEADS * P]))\
                       .then_inc(small_loaded, 16)

                load_vector(ln_g, gmlp_ln_g)
                load_vector(ln_b, gmlp_ln_b)
                round_unit(L, QQ)
                act.wait_ge(stat_done, L * 4 + 2)
                load_vector(bs_b, gmlp_bs)
                round_unit(L, QQ + 1)
                act.wait_ge(w_used, used(L, GV + 1))
                act.wait_ge(r_ready, L * 4 + 2)
                for t in range(ST):
                    act.activation(k_tok[:, t, :], ps[:, t, :], ACT.Gelu, scale=rtok[:, t:t + 1])\
                       .then_inc(gelu_ready, 1)
                for t in range(MT):
                    if t:
                        act.wait_ge(mem_sq_ready, L * 2 + t)
                    else:
                        act.wait_ge(mem_loaded, L * 32 + 32)
                    act.activation(tmp[:, 0:2, :], mem_in[:, t, :].rearrange("p (a c) -> p a c", c=S), ACT.Square,
                                   accum_out=mss[:, 0, t:t + 1]).then_inc(mem_sq_ready, 1)
                round_unit(L, KK)
                for t in range(ST):
                    act.wait_ge(vn_final, L * 4 + t + 1)
                    act.activation(gm_hi[:, :, t * P:(t + 1) * P],
                                   k_tok[:, t, :].rearrange("p (g c) -> p g c", c=P), ACT.Copy)\
                       .then_inc(vn_rounded, 1)
                round_unit(L, KK + 1)
                act.wait_ge(w_used, used(L, QQ + 1))
                for t in range(ST):
                    act.activation(q_tok[:, t, :], ps[:, 4 + t, :], ACT.Copy, scale=rtok[:, t:t + 1])\
                       .then_inc(qk_copied, 1)
                round_unit(L, GU)
                copy_rb(L * 3 + 2, 4)
                act.wait_ge(ws_turned, L + 1)
                act.activation(wsT_hi[:, :, :], ps[:, 5, :].rearrange("p (g c) -> p g c", c=P), ACT.Copy)\
                   .then_inc(wsT_rounded, 1)
                round_unit(L, GU + 1)
                act.wait_ge(w_used, used(L, KK + 1))
                act.wait_ge(vn_ready, L * 4 + 4)
                for t in range(ST):
                    act.activation(k_tok[:, t, :], ps[:, t, :], ACT.Copy, scale=rtok[:, t:t + 1])\
                       .then_inc(qk_copied, 1)

                def gelu_gu(half):
                    act.wait_ge(gu_scaled, L * 2 + half + 1)
                    act.activation(gu[:, 2 * half:2 * half + 2, :], gu[:, 2 * half:2 * half + 2, :], ACT.Gelu)\
                       .then_inc(gu_ready, 1)

                def round_turned(n, dst):
                    act.wait_ge(qk_turned, L * 8 + n + 1)
                    t = n % ST
                    act.activation(dst[:, :, t * P:(t + 1) * P],
                                   ps[:, t, :].rearrange("p (g c) -> p g c", c=P), ACT.Copy)\
                       .then_inc(qkT_rounded, 1)

                round_unit(L, VV)
                gelu_gu(0)
                for t in range(ST):
                    round_turned(t, qT_hi)
                round_unit(L, VV + 1)
                gelu_gu(1)
                for t in range(ST):
                    round_turned(ST + t, kT_hi)
                def round_gm(t):
                    act.wait_ge(gm_final, L * 4 + t + 1)
                    act.activation(gm_hi[:, :, t * P:(t + 1) * P],
                                   tmp[:, t % 2, :].rearrange("p (g c) -> p g c", c=P), ACT.Copy)\
                       .then_inc(gm_rounded, 1)

                def round_mg(half):
                    wait_apart(act, mem_turned, L * 2 + half + 1)
                    for n in range(4):
                        m = 4 * half + n
                        act.activation(mg_hi[:, m, :], ps[:, 4 + n // 2, (n % 2) * M:(n % 2 + 1) * M], ACT.Copy,
                                       scale=gains[:, ds(L * KT + G_MEM + m, 1)]).then_inc(mg_rounded, 1)

                round_gm(0)
                round_gm(1)
                round_mg(0)
                round_unit(L, CK)
                round_gm(2)
                round_mg(1)
                act.wait_ge(w_used, used(L, VV + 1))
                for t in range(ST):
                    act.activation(v_hi[:, t, :], ps[:, t, :], ACT.Copy, scale=rtok[:, t:t + 1])\
                       .then_inc(v_rounded, 1)
                round_unit(L, CK + 1)

                def turned_high(s):
                    n = s - 1
                    qb = n % 4
                    act.wait_ge(attn_w_turned, L * 16 + n + 1)
                    if qb == 0 and n:
                        act.wait_ge(pv_done, L * 4 + n // 4)
                    act.activation(wT_hi[:, 0:qb + 1, qb * P:(qb + 1) * P],
                                   ps[:, 0, 0:(qb + 1) * P].rearrange("p (k c) -> p k c", c=P), ACT.Copy)\
                       .then_inc(wT_rounded, 1)

                def exponentials(s):
                    qb, b = s % 4, s % 2
                    N = (qb + 1) * P
                    act.wait_ge(nb_ready, L * 16 + s + 1)
                    if s >= 2:
                        act.wait_ge(attn_w_turned, L * 16 + s - 1)
                    for br in range(2):
                        last = act.activation(ex[:, b, br, 0:N], ps[:, 4 + 2 * b + br, 0:N], ACT.Exp,
                                              bias=nb[:, b, br:br + 1], scale=QK_SCALE,
                                              accum_out=sm[:, b, br:br + 1])
                    last.then_inc(exp_done, 1)

                def kv_high(s):
                    n = s // 2
                    act.wait_ge(w_used, used(L, CK + n))
                    act.activation(kc_hi[:, 2 * n:2 * n + 2, :] if n < 4 else vc_hi[n - 4][:, :, :],
                                   ps[:, 2, :].rearrange("p (k c) -> p k c", c=M), ACT.Copy)\
                       .then_inc(kv_rounded, 1)

                for s in range(22):
                    late = s % 4 == 1 and s > 1
                    if 1 <= s < 17 and not late:
                        turned_high(s)
                    if s < 16:
                        exponentials(s)
                    if s == 0:
                        round_gm(3)
                    if s % 2 and s < 16:
                        kv_high(s)
                    if s < 17 and late:
                        turned_high(s)
                    if s % 2 and s < 16:
                        round_unit(L, CK + s // 2 + 2)
                    if s >= 5:
                        hd, part = divmod(s - 5, 4)
                        if part == 0 and hd < 4:
                            act.wait_ge(pv_done, L * 4 + hd + 1)
                            if hd:
                                act.wait_ge(attn_ready, L * 4 + hd)
                            act.activation(tmp[:, 0, :], ps[:, 1, :], ACT.Square).then_inc(osq_ready, 1)
                        if part == 2:
                            act.wait_ge(orb_done, L * 4 + hd + 1)
                            act.activation(tmp[:, 1, :], ps[:, 3, :], ACT.Copy).then_inc(orb_ready, 1)
                        if part == 3:
                            act.wait_ge(attn_final, L * 4 + hd + 1)
                            act.activation(qT_hi[:, hd, :], tmp[:, 0, :], ACT.Copy).then_inc(attn_rounded, 1)

                def projected(stage, u, gcol):
                    for t in range(4):
                        if t < 3:
                            round_unit(L, u + t + 2)
                        for b in range(2):
                            round_tile(tile_no(L, stage, 2 * t + b), 2 * t + b, L * KT + gcol + 2 * t + b)
                        if t == 3:
                            round_unit(L, u + t + 2)
                        for b in range(2):
                            m = 2 * t + b
                            square_tile(m, b, sum_no(L, stage, m) - 2)

                projected(1, WO, G_CROSS)

                def round_qc(hd):
                    b = hd % 2
                    act.wait_ge(w_used, used(L, WQ + hd))
                    act.activation(qc_hi[:, b, :, :], ps[:, 4 + 2 * b:6 + 2 * b, :], ACT.Copy).then_inc(qc_rounded, 1)

                def cross_exp(hd):
                    act.wait_ge(cnb_ready, L * 4 + hd + 1)
                    if hd:
                        act.wait_ge(cw_turned, L * 4 + hd)
                    for qb in range(ST):
                        last = act.activation(tmp[:, qb // 2, (qb % 2) * M:(qb % 2 + 1) * M],
                                              ps[:, qb // 2, (qb % 2) * M:(qb % 2 + 1) * M], ACT.Exp,
                                              bias=cnb[:, qb:qb + 1], scale=crs[:, qb:qb + 1],
                                              accum_out=csm[:, qb:qb + 1])
                    last.then_inc(cexp_done, 1)

                round_qc(0)
                round_unit(L, WQ + 2)
                round_qc(1)
                round_unit(L, WQ + 3)
                cross_exp(0)
                round_qc(2)
                for hd in range(HEADS):
                    act.wait_ge(cw_turned, L * 4 + hd + 1)
                    if hd:
                        act.wait_ge(cpv_done, L * 4 + hd)
                    act.activation(wc_hi[:, :, :], ps[:, 2:4, :], ACT.Copy).then_inc(wc_rounded, 1)
                    if hd == 1:
                        round_unit(L, CO + 1)
                    if hd < 3:
                        cross_exp(hd + 1)
                    if hd == 0:
                        round_unit(L, CO)
                    act.wait_ge(cpv_done, L * 4 + hd + 1)
                    act.activation(o_hi[:, 2 * hd:2 * hd + 2, :], ps[:, 2:4, :], ACT.Copy).then_inc(o_rounded, 1)
                    if hd == 0:
                        round_qc(3)

                projected(2, CO, G_FFN2)
                ffn(L, 1, UP2, DN2, 3, L * 3 + 3, G_FFN1 + KT, UNITS)

            act.wait_ge(stat_done, LAYERS * 4 + 1)
            act.activation(msq[:, :], ps[:, 4, 0:ST], ACT.Copy, scale=1.0 / D, bias=EPS).then_inc(ms_ready, 1)
            act.wait_ge(r_ready, LAYERS * 4 + 1)
            for t in (0, 2):
                act.wait_ge(fin_turned, 1 if t == 0 else 2)
                act.activation(o_sb[:, t, :].rearrange("p (a c) -> p a c", c=512), ps[:, FIN_BANK[t]:FIN_BANK[t] + 2, :],
                               ACT.Copy, scale=rtok[:, t:t + 1]).then_inc(fin_ready, 1)

        @block.vector
        def _(dve):
            def split_unit(L, u, i=0, per=2):
                s = u % 2
                dve.wait_ge(w_rounded, unit_no(L, u, i, per) + 1)
                z = unit_size(u)
                dve.tensor_tensor(out=w_lo[:, s, 0:z], in0=raw[:, s, 0:z], in1=w_hi[:, s, 0:z].bitcast(f32),
                                  op=ALU.subtract).then_inc(w_split, 1)

            def split_half(L, u, half):
                s = u % 2
                if half == 0:
                    dve.wait_ge(w_rounded, unit_no(L, u) + 1)
                z = unit_size(u) // 2
                c = slice(half * z, (half + 1) * z)
                last = dve.tensor_tensor(out=w_lo[:, s, c], in0=raw[:, s, c], in1=w_hi[:, s, c].bitcast(f32),
                                         op=ALU.subtract)
                if half == 1:
                    last.then_inc(w_split, 1)

            def add_tile(products, m, bank, factor):
                dve.wait_ge(w_used, products)
                dve.scalar_tensor_tensor(out=h[:, ds(m, 1), :], in0=ps[:, bank:bank + 1, :], scalar=factor,
                                         in1=h[:, ds(m, 1), :], op0=ALU.mult, op1=ALU.add).then_inc(h_ready, 1)

            def low_tile(no, m, gcol):
                dve.wait_ge(hn_rounded, no)
                dve.scalar_tensor_tensor(out=hn_lo[:, ds(m, 1), :], in0=h[:, ds(m, 1), :],
                                         scalar=gains[:, ds(gcol, 1)],
                                         in1=hn_hi[:, ds(m, 1), :].bitcast(f32),
                                         op0=ALU.mult, op1=ALU.subtract).then_inc(hn_ready, 1)

            def mean_square(n, bank):
                dve.wait_ge(stat_done, n)
                dve.tensor_scalar(msq[:, :], ps[:, bank, 0:ST], 1.0 / D, EPS, ALU.mult, ALU.add)\
                   .then_inc(ms_ready, 1)

            done = [0]

            def setup(ins):
                done[0] += 1
                ins.then_inc(setup_dve, 1)
                dve.wait_ge(setup_dve, done[0])

            dve.memset(msh[:, :], 0.0).then_inc(w_split, 2)
            dve.memset(rh[:, :], 0.0).then_inc(w_used, 2)
            inv = (1.0 / np.power(np.float32(500000.0), np.arange(0, 16, 2, dtype=np.float32) / np.float32(16))).astype(np.float32)
            for j in range(HALF):
                setup(dve.memset(invf[:, j:j + 1], float(inv[j])))
            for n in range(2 * ST):
                t, c = divmod(n, 2)
                if n == 2:
                    dve.wait_ge(setup_pe, 1)
                    dve.tensor_copy(gains[:, 0:LAYERS * KT], ps[:, 7, 0:LAYERS * KT]).then_inc(setup_dve, 1)
                dve.wait_ge(x_turned, n + 1)
                dve.tensor_copy(h[:, 4 * c:4 * c + 4, t * P:(t + 1) * P],
                                ps[:, n % 6, :].rearrange("p (k c) -> p k c", c=P)).then_inc(h_ready, 1)
            done[0] += 1
            low_tile(1, 0, 0)
            dve.wait_ge(pos_loaded, 16)
            setup(dve.tensor_copy(pos_f[:, :], pos_i[:, :]))
            low_tile(2, 1, 1)
            dve.wait_ge(setup_pe, 2)
            setup(dve.tensor_copy(gains[:, LAYERS * KT:], ps[:, 6, LAYERS * KT:90]))
            dve.wait_ge(half_rounded, 1)
            dve.tensor_tensor(out=w_lo[:, 0, 0:1024], in0=raw[:, 0, 0:1024], in1=w_hi[:, 0, 0:1024].bitcast(f32),
                              op=ALU.subtract)
            dve.wait_ge(w_rounded, 1)
            dve.tensor_tensor(out=w_lo[:, 0, 1024:2048], in0=raw[:, 0, 1024:2048],
                              in1=w_hi[:, 0, 1024:2048].bitcast(f32), op=ALU.subtract).then_inc(w_split, 1)
            for m in range(2, KT):
                low_tile(m + 1, m, m)
            dve.wait_ge(setup_pe, 3)
            setup(dve.tensor_copy(pos_t[:, :], ps[:, 7, LAYERS * KT:LAYERS * KT + ST]))
            for t in range(ST):
                setup(dve.tensor_scalar(ang[:, 0, t, :], invf[:, :], pos_t[:, t:t + 1], None, ALU.mult))
            magic = float(1.5 * 2 ** 23)
            setup(dve.tensor_scalar(ang[:, 1, :, :], ang[:, 0, :, :], 1.0 / (2 * math.pi), None, ALU.mult))
            setup(dve.tensor_scalar(ang[:, 1, :, :], ang[:, 1, :, :], magic, None, ALU.add))
            setup(dve.tensor_scalar(ang[:, 1, :, :], ang[:, 1, :, :], -magic, None, ALU.add))
            c1 = 6.28125
            c2 = float(round((2 * math.pi - c1) * 2 ** 20) / 2 ** 20)
            c3 = 2 * math.pi - c1 - c2
            for c in (c1, c2, c3):
                setup(dve.scalar_tensor_tensor(out=ang[:, 0, :, :], in0=ang[:, 1, :, :], scalar=-c,
                                               in1=ang[:, 0, :, :], op0=ALU.mult, op1=ALU.add))
            setup(dve.tensor_scalar(ang[:, 1, :, :], ang[:, 0, :, :], 3.1415925, -3.1415925, ALU.min, ALU.max))
            setup(dve.tensor_scalar(ang[:, 2, :, :], ang[:, 1, :, :], -1.0, None, ALU.mult))
            setup(dve.tensor_tensor(out=ang[:, 2, :, :], in0=ang[:, 2, :, :], in1=ang[:, 1, :, :], op=ALU.max))
            dve.tensor_scalar(ang[:, 2, :, :], ang[:, 2, :, :], -1.0, math.pi / 2, ALU.mult, ALU.add).then_inc(angles_ready, 1)
            split_unit(0, 1)
            dve.wait_ge(lam_loaded, 16 * 4)
            for n in range(2):
                setup(dve.tensor_tensor(out=lam_pr[:, n, :, :],
                                        in0=lam_in[:, 2 * n, :].rearrange("p (l d) -> p l d", d=64),
                                        in1=lam_in[:, 2 * n + 1, :].rearrange("p (l d) -> p l d", d=64), op=ALU.mult))
            dve.tensor_reduce(lam_s[:, :, :], lam_pr[:, :, :, :], AX.X, ALU.add).then_inc(lam_sums_ready, 1)
            for l in range(LAYERS):
                setup(dve.tensor_scalar(gsub[:, l:l + 1], gains[:, G_SUBLN + l:G_SUBLN + l + 1],
                                        1.0 - (0.8 - 0.6 * math.exp(-0.3 * l)), None, ALU.mult))
            dve.wait_ge(setup_act, 3)
            setup(dve.tensor_tensor(out=neg_lam[:, :], in0=lam_s[:, 1, :], in1=lam_s[:, 0, :], op=ALU.subtract))
            for l in range(LAYERS):
                setup(dve.tensor_scalar(neg_lam[:, l:l + 1], neg_lam[:, l:l + 1], -(0.8 - 0.6 * math.exp(-0.3 * l)), None, ALU.add))
            dve.wait_ge(setup_act, 5)
            for a, src in ((0, 4), (1, 3)):
                for b in range(2):
                    setup(dve.tensor_copy(rope[:, :, a, b * HALF:(b + 1) * HALF], ang[:, src, :, :]))

            def ffn(L, f, up, dn, stage, stat_no, next_gain, next_unit):
                def up_body(i, where):
                    if where == "first":
                        mean_square(stat_no, 6)
                        dve.wait_ge(rb_ready, L * 3 + (1 if f == 0 else 3))
                    for s in range(2):
                        n = ffn_no(L, f, 2 * i + s)
                        dve.wait_ge(w_used, used(L, up + s, i))
                        dve.tensor_tensor(out=tmp[:, 0, :], in0=ps[:, 2 * s, :], in1=rb[:, :], op=ALU.mult)\
                           .then_inc(gate_ready, 1)
                        dve.tensor_tensor(out=tmp[:, 2, :], in0=ps[:, 2 * s + 1, :], in1=rb[:, :], op=ALU.mult)\
                           .then_inc(up_read, 1)
                        if where == "last":
                            split_unit(L, dn + s)
                        else:
                            split_unit(L, up + s + 2, i)
                        dve.wait_ge(silu_ready, n)
                        dve.wait_ge(up_read, n)
                        dve.tensor_tensor(out=tmp[:, 1, :], in0=tmp[:, 1, :], in1=tmp[:, 2, :], op=ALU.mult)\
                           .then_inc(prod_ready, 1)
                        dve.wait_ge(hid_rounded, n)
                        dve.tensor_tensor(out=hid_lo[:, ds(2 * i + s, 1), :], in0=tmp[:, 1:2, :],
                                          in1=hid_hi[:, ds(2 * i + s, 1), :].bitcast(f32), op=ALU.subtract)\
                           .then_inc(hid_ready, 1)
                up_loop(dve, up_body)

                def down_body(i, last):
                    for b in range(2):
                        m = 2 * i + b
                        no = tile_no(L, stage, m)
                        at_end = last and b == 1
                        for s in range(2):
                            if s == 1:
                                add_tile(used(L, dn + 2 * b + 1, i, 4), m, 4 + b, 0.5)
                                low_tile(no, m, L * KT + next_gain + m)
                            if not at_end:
                                split_unit(L, dn + 2 * b + 2 + s, i, 4)
                            else:
                                split_unit(L, next_unit + s)
                down_loop(dve, down_body)

            with dve.Fori(0, LAYERS) as L:
                count = [0]

                def link(ins):
                    count[0] += 1
                    ins.then_inc(dve_chain, 1)
                    dve.wait_ge(dve_chain, L * CHAIN + count[0])

                ffn(L, 0, UP1, DN1, 0, L * 4 + 1, G_MIX, GV)

                split_unit(L, QQ)
                mean_square(L * 4 + 2, 7)
                split_unit(L, QQ + 1)
                dve.wait_ge(small_loaded, L * 64 + 64)
                for t in range(ST):
                    dve.wait_ge(gelu_ready, L * 4 + t + 1)
                    for g in range(HEADS):
                        last = dve.bn_stats(bst[:, t, g, :], k_tok[:, t, g * P:(g + 1) * P])
                    count[0] += 1
                    last.then_inc(dve_chain, 1)
                    wait_apart(dve, dve_chain, L * CHAIN + count[0])
                    for g in range(HEADS):
                        last = dve.bn_aggr(mv[:, t, g, :], bst[:, t, g, :])
                    link(last)
                dve.tensor_scalar(vareps[:, :, :], mv[:, :, :, 1], EPS, None, ALU.add).then_inc(var_ready, 1)
                dve.wait_ge(mem_sq_ready, L * 2 + 2)
                dve.tensor_scalar(mss[:, 1, :], mss[:, 0, :], 1.0 / D, EPS, ALU.mult, ALU.add).then_inc(mem_ms_ready, 1)
                split_unit(L, KK)
                dve.wait_ge(rstd_ready, L + 1)
                for t in range(ST):
                    for g in range(HEADS):
                        last = dve.tensor_scalar(k_tok[:, t, g * P:(g + 1) * P], k_tok[:, t, g * P:(g + 1) * P],
                                                 mv[:, t, g, 0:1], rstd[:, t, g:g + 1], ALU.subtract, ALU.mult)
                    link(last)
                    link(dve.tensor_tensor(out=k_tok[:, t, :], in0=k_tok[:, t, :], in1=ln_g[:, :], op=ALU.mult))
                    dve.tensor_tensor(out=k_tok[:, t, :], in0=k_tok[:, t, :], in1=ln_b[:, :], op=ALU.add)\
                       .then_inc(vn_final, 1)
                for t in range(ST):
                    dve.wait_ge(vn_rounded, L * 4 + t + 1)
                    dve.tensor_tensor(out=gm_lo[:, :, t * P:(t + 1) * P],
                                      in0=k_tok[:, t, :].rearrange("p (g c) -> p g c", c=P),
                                      in1=gm_hi[:, :, t * P:(t + 1) * P].bitcast(f32), op=ALU.subtract)\
                       .then_inc(vn_ready, 1)
                dve.wait_ge(mem_r_ready, L + 1)
                for t in range(MT):
                    last = dve.tensor_scalar(mem_in[:, t, :], mem_in[:, t, :], mss[:, 2, t:t + 1], None, ALU.mult)
                last.then_inc(mem_normed, 1)
                split_unit(L, KK + 1)

                def rotate(n, tok):
                    t = n % ST
                    dve.wait_ge(qk_copied, L * 8 + n + 1)
                    part = tok[:, t, :].rearrange("p (h d) -> p h d", d=64)[:, :, 0:2 * HALF]
                    a = tmp[:, 0, 0:P].rearrange("p (h d) -> p h d", d=2 * HALF)
                    b = tmp[:, 1, 0:P].rearrange("p (h d) -> p h d", d=2 * HALF)
                    cos, sin = (rope[:, t, i:i + 1, :].to_broadcast([P, 8, 2 * HALF]) for i in range(2))
                    dve.tensor_tensor(out=a, in0=part, in1=cos, op=ALU.mult)
                    link(dve.tensor_tensor(out=b, in0=part, in1=sin, op=ALU.mult))
                    dve.tensor_tensor(out=part[:, :, 0:HALF], in0=a[:, :, 0:HALF], in1=b[:, :, HALF:], op=ALU.subtract)
                    dve.tensor_tensor(out=part[:, :, HALF:], in0=a[:, :, HALF:], in1=b[:, :, 0:HALF], op=ALU.add)\
                       .then_inc(qk_roped, 1)
                    dve.wait_ge(qk_roped, L * 8 + n + 1)

                for t in range(ST):
                    rotate(t, q_tok)
                split_unit(L, GU)
                dve.wait_ge(wsT_rounded, L + 1)
                dve.tensor_tensor(out=wsT_lo[:, :, :], in0=ps[:, 5, :].rearrange("p (g c) -> p g c", c=P),
                                  in1=wsT_hi[:, :, :].bitcast(f32), op=ALU.subtract).then_inc(wsT_ready, 1)
                split_unit(L, GU + 1)
                for t in range(ST):
                    rotate(ST + t, k_tok)

                def scale_gu(half, bank):
                    dve.wait_ge(w_used, used(L, GU + half))
                    if half == 0:
                        dve.wait_ge(rb_ready, L * 3 + 2)
                    for b in range(2):
                        last = dve.tensor_tensor(out=gu[:, 2 * half + b, :], in0=ps[:, bank + b, :], in1=rb[:, :],
                                                 op=ALU.mult)
                    last.then_inc(gu_scaled, 1)

                def low_turned(n, hi, lo):
                    dve.wait_ge(qkT_rounded, L * 8 + n + 1)
                    t = n % ST
                    dve.tensor_tensor(out=lo[:, :, t * P:(t + 1) * P],
                                      in0=ps[:, t, :].rearrange("p (g c) -> p g c", c=P),
                                      in1=hi[:, :, t * P:(t + 1) * P].bitcast(f32), op=ALU.subtract)\
                       .then_inc(qkT_ready, 1)

                def gate_chunk(t):
                    dve.wait_ge(mix_done, L * 4 + t + 1)
                    if t == 0:
                        dve.wait_ge(gu_ready, L * 2 + 2)
                    if t >= 2:
                        dve.wait_ge(gm_ready, L * 4 + t - 1)
                    link(dve.tensor_tensor(out=tmp[:, t % 2, :], in0=ps[:, 6 + t % 2, :], in1=bs_b[:, :], op=ALU.add))
                    dve.tensor_tensor(out=tmp[:, t % 2, :].rearrange("p (g c) -> p g c", c=P),
                                      in0=tmp[:, t % 2, :].rearrange("p (g c) -> p g c", c=P),
                                      in1=gu[:, :, t * P:(t + 1) * P], op=ALU.mult).then_inc(gm_final, 1)

                def low_gm(t):
                    dve.wait_ge(gm_rounded, L * 4 + t + 1)
                    dve.tensor_tensor(out=gm_lo[:, :, t * P:(t + 1) * P],
                                      in0=tmp[:, t % 2, :].rearrange("p (g c) -> p g c", c=P),
                                      in1=gm_hi[:, :, t * P:(t + 1) * P].bitcast(f32), op=ALU.subtract)\
                       .then_inc(gm_ready, 1)

                def low_mg(half):
                    for n in range(4):
                        m = 4 * half + n
                        if n % 2 == 0:
                            dve.wait_ge(mg_rounded, L * 8 + m + 2)
                        dve.scalar_tensor_tensor(out=mg_lo[:, m, :], in0=ps[:, 4 + n // 2, (n % 2) * M:(n % 2 + 1) * M],
                                                 scalar=gains[:, ds(L * KT + G_MEM + m, 1)],
                                                 in1=mg_hi[:, m, :].bitcast(f32), op0=ALU.mult, op1=ALU.subtract)\
                           .then_inc(mg_ready, 1)

                scale_gu(0, 6)
                split_unit(L, VV)
                for t in range(ST):
                    low_turned(t, qT_hi, qT_lo)
                scale_gu(1, 4)
                split_unit(L, VV + 1)
                for t in range(ST):
                    low_turned(ST + t, kT_hi, kT_lo)
                gate_chunk(0)
                gate_chunk(1)
                low_gm(0)
                low_gm(1)
                low_mg(0)
                split_unit(L, CK)
                gate_chunk(2)
                low_gm(2)
                low_mg(1)
                for t in range(ST):
                    dve.wait_ge(v_rounded, L * 4 + t + 1)
                    dve.scalar_tensor_tensor(out=v_lo[:, t, :], in0=ps[:, t, :], scalar=rtok[:, t:t + 1],
                                             in1=v_hi[:, t, :].bitcast(f32), op0=ALU.mult, op1=ALU.subtract)\
                       .then_inc(v_ready, 1)

                def maxima(s):
                    qb, b = s % 4, s % 2
                    N = (qb + 1) * P
                    dve.wait_ge(sc_done, L * 16 + s + 1)
                    link(dve.tensor_reduce(mx[:, b, :], ps[:, 4 + 2 * b:6 + 2 * b, 0:N], AX.X, ALU.max))
                    dve.tensor_scalar(nb[:, b, :], mx[:, b, :], -QK_SCALE, None, ALU.mult).then_inc(nb_ready, 1)

                def turned_low(s):
                    n = s - 1
                    qb = n % 4
                    dve.wait_ge(wT_rounded, L * 16 + n + 1)
                    dve.tensor_tensor(out=wT_lo[:, 0:qb + 1, qb * P:(qb + 1) * P],
                                      in0=ps[:, 0, 0:(qb + 1) * P].rearrange("p (k c) -> p k c", c=P),
                                      in1=wT_hi[:, 0:qb + 1, qb * P:(qb + 1) * P].bitcast(f32),
                                      op=ALU.subtract).then_inc(wT_ready, 1)

                def attn_weights(s):
                    hd, qb, b = s // 4, s % 4, s % 2
                    N = (qb + 1) * P
                    dve.wait_ge(exp_done, L * 16 + s + 1)
                    link(dve.reciprocal(rs[:, hd, :, qb], sm[:, b, :]))
                    link(dve.scalar_tensor_tensor(out=ratio[:, b:b + 1], in0=rs[:, hd, 1, qb:qb + 1],
                                                  scalar=sm[:, b, 0:1], in1=neg_lam[:, ds(L, 1)],
                                                  op0=ALU.mult, op1=ALU.mult))
                    dve.scalar_tensor_tensor(out=ex[:, b, 0, 0:N], in0=ex[:, b, 1, 0:N], scalar=ratio[:, b:b + 1],
                                             in1=ex[:, b, 0, 0:N], op0=ALU.mult, op1=ALU.add)\
                       .then_inc(attn_w_ready, 1)

                def kv_low(s):
                    n = s // 2
                    dve.wait_ge(kv_rounded, L * 8 + n + 1)
                    hi, lo = ((kc_hi[:, 2 * n:2 * n + 2, :], kc_lo[:, 2 * n:2 * n + 2, :]) if n < 4
                              else (vc_hi[n - 4][:, :, :], vc_lo[n - 4][:, :, :]))
                    dve.tensor_tensor(out=lo, in0=ps[:, 2, :].rearrange("p (k c) -> p k c", c=M),
                                      in1=hi.bitcast(f32), op=ALU.subtract).then_inc(kv_ready, 1)

                for s in range(22):
                    if s >= 5:
                        hd, part = divmod(s - 5, 4)
                        if part == 0 and hd >= 1:
                            dve.wait_ge(attn_rounded, L * 4 + hd)
                            dve.tensor_tensor(out=qT_lo[:, hd - 1, :], in0=tmp[:, 0, :],
                                              in1=qT_hi[:, hd - 1, :].bitcast(f32), op=ALU.subtract)\
                               .then_inc(attn_ready, 1)
                    late = s % 4 == 1 and s > 1
                    if s < 16:
                        maxima(s)
                    if s == 0:
                        gate_chunk(3)
                    if s % 2 and s <= 17:
                        split_half(L, CK + s // 2 + 1, 1)
                    if 1 <= s < 17 and not late:
                        turned_low(s)
                    if s < 16:
                        attn_weights(s)
                    if s == 0:
                        low_gm(3)
                    if s % 2 and s < 16:
                        kv_low(s)
                    if s < 17 and late:
                        turned_low(s)
                    if s % 2 == 0 and s <= 16:
                        split_half(L, CK + s // 2 + 1, 0)
                    if s >= 5:
                        hd, part = divmod(s - 5, 4)
                        if part == 1:
                            dve.wait_ge(ostat_done, L * 4 + hd + 1)
                            link(dve.scalar_tensor_tensor(out=msh[:, :], in0=ps[:, 3, 0:ST], scalar=1.0 / P,
                                                          in1=rs[:, hd, 0, :], op0=ALU.mult, op1=ALU.mult))
                            link(dve.tensor_tensor(out=msh[:, :], in0=msh[:, :], in1=rs[:, hd, 0, :], op=ALU.mult))
                            dve.tensor_scalar(msh[:, :], msh[:, :], EPS, None, ALU.add)\
                               .then_inc(oms_ready, 1)
                        if part == 3:
                            dve.wait_ge(orb_ready, L * 4 + hd + 1)
                            dve.scalar_tensor_tensor(out=tmp[:, 0, :], in0=ps[:, 1, :], scalar=gsub[:, ds(L, 1)],
                                                     in1=tmp[:, 1, :], op0=ALU.mult, op1=ALU.mult)\
                               .then_inc(attn_final, 1)

                def projected(stage, u, gcol):
                    for t in range(4):
                        for b in range(2):
                            add_tile(used(L, u + t), 2 * t + b, 4 + 2 * (t % 2) + b, 1.0)
                        if t < 3:
                            split_unit(L, u + t + 2)
                        for b in range(2):
                            low_tile(tile_no(L, stage, 2 * t + b), 2 * t + b, L * KT + gcol + 2 * t + b)
                        if t == 3:
                            split_unit(L, u + t + 2)

                projected(1, WO, G_CROSS)
                mean_square(L * 4 + 3, 0)
                dve.wait_ge(r_ready, L * 4 + 3)
                link(dve.tensor_scalar(crs[:, :], rtok[:, :], CROSS_SCALE, None, ALU.mult))

                def low_qc(hd):
                    b = hd % 2
                    dve.wait_ge(qc_rounded, L * 4 + hd + 1)
                    dve.tensor_tensor(out=qc_lo[:, b, :, :], in0=ps[:, 4 + 2 * b:6 + 2 * b, :],
                                      in1=qc_hi[:, b, :, :].bitcast(f32), op=ALU.subtract).then_inc(qc_ready, 1)

                def cross_max(hd):
                    dve.wait_ge(csc_done, L * 4 + hd + 1)
                    link(dve.tensor_reduce(cmx[:, :], ps[:, 0:2, :].rearrange("p a (b m) -> p (a b) m", m=M),
                                           AX.X, ALU.max))
                    dve.scalar_tensor_tensor(out=cnb[:, :], in0=cmx[:, :], scalar=-1.0, in1=crs[:, :],
                                             op0=ALU.mult, op1=ALU.mult).then_inc(cnb_ready, 1)

                def cross_norm_w(hd):
                    dve.wait_ge(cexp_done, L * 4 + hd + 1)
                    link(dve.reciprocal(crc[:, :], csm[:, :]))
                    for qb in range(ST):
                        part = tmp[:, qb // 2, (qb % 2) * M:(qb % 2 + 1) * M]
                        last = dve.tensor_scalar(part, part, crc[:, qb:qb + 1], None, ALU.mult)
                    last.then_inc(cw_ready, 1)

                low_qc(0)
                split_unit(L, WQ + 2)
                low_qc(1)
                split_unit(L, WQ + 3)
                cross_max(0)
                cross_norm_w(0)
                low_qc(2)
                for hd in range(HEADS):
                    dve.wait_ge(wc_rounded, L * 4 + hd + 1)
                    dve.tensor_tensor(out=wc_lo[:, :, :], in0=ps[:, 2:4, :], in1=wc_hi[:, :, :].bitcast(f32),
                                      op=ALU.subtract).then_inc(wc_ready, 1)
                    if hd < 3:
                        cross_max(hd + 1)
                        if hd == 1:
                            split_unit(L, CO + 1)
                        cross_norm_w(hd + 1)
                    if hd == 0:
                        split_unit(L, CO)
                    dve.wait_ge(o_rounded, L * 4 + hd + 1)
                    dve.tensor_tensor(out=o_lo[:, 2 * hd:2 * hd + 2, :], in0=ps[:, 2:4, :],
                                      in1=o_hi[:, 2 * hd:2 * hd + 2, :].bitcast(f32), op=ALU.subtract)\
                       .then_inc(o_ready, 1)
                    if hd == 0:
                        low_qc(3)

                projected(2, CO, G_FFN2)
                ffn(L, 1, UP2, DN2, 3, L * 4 + 4, G_FFN1 + KT, UNITS)
                assert count[0] == CHAIN, count[0]

            dve.wait_ge(r_ready, LAYERS * 4 + 1)
            for t in (1, 3):
                dve.wait_ge(fin_turned, 1 if t == 1 else 3)
                dve.tensor_scalar(o_sb[:, t, :].rearrange("p (a c) -> p a c", c=512),
                                  ps[:, FIN_BANK[t]:FIN_BANK[t] + 2, :], rtok[:, t:t + 1], None, ALU.mult)\
                   .then_inc(fin_ready_v, 1)

        @block.tensor
        def _(pe):
            def product(dst, a_hi, a_lo, b_hi, b_lo, start, stop, extra=None):
                pe.matmul(dst, a_hi, b_hi, start=start, stop=False)
                if extra:
                    extra()
                pe.matmul(dst, a_hi, b_lo, start=False, stop=False)
                return pe.matmul(dst, a_lo, b_hi, start=False, stop=stop)

            def wait_unit(L, u, i=0, per=2):
                pe.wait_ge(w_split, unit_no(L, u, i, per) + 3)

            def wtile(u, a, n=P):
                return w_hi[:, u % 2, a:a + n], w_lo[:, u % 2, a:a + n]

            def token_sums(sum_no_, bank):
                pe.wait_ge(sum_ready, sum_no_)
                for t in range(ST):
                    last = pe.matmul(ps[:, bank, t:t + 1], sumsq[:, t * P:(t + 1) * P], ones[:, 0:1],
                                     start=True, stop=True)
                last.then_inc(stat_done, 1)

            def broadcast(values, bank, done_sem):
                for t in range(ST):
                    last = pe.transpose(ps[:, bank, t * P:(t + 1) * P], values[:, t:t + 1].to_broadcast([P, P]),
                                        ident[:, :])
                last.then_inc(done_sem, 1)

            pe.wait_ge(setup_pool, 6)
            for n in range(2 * ST):
                t, c = divmod(n, 2)
                if c == 0:
                    pe.wait_ge(x_loaded[t], 16)
                if n >= 6:
                    pe.wait_ge(h_ready, n - 5)
                if n == 2:
                    pe.wait_ge(ffn1_gain_loaded, 16)
                    g = LAYERS * KT
                    pe.transpose(ps[:, 7, 0:g], rows[0:g, :], ident[0:g, 0:g]).then_inc(setup_pe, 1)
                for m in range(4):
                    last = pe.transpose(ps[:, n % 6, m * P:(m + 1) * P],
                                        x_in[:, t, (4 * c + m) * P:(4 * c + m + 1) * P], ident[:, :])
                last.then_inc(x_turned, 1)

            pe.wait_ge(gains_loaded, 16 * 6)
            pe.transpose(ps[:, 6, 0:90], rows[:, :], ident[0:90, 0:90]).then_inc(setup_pe, 1)
            pe.wait_ge(setup_dve, HALF + 2)
            pe.transpose(ps[:, 7, LAYERS * KT:LAYERS * KT + ST], pos_f[:, :], ident[0:ST, 0:ST]).then_inc(setup_pe, 1)

            def ffn(L, f, up, dn, stage):
                def up_unit(i, s, hook=None, waits=False):
                    u = up + s
                    wait_unit(L, u, i)
                    if not waits:
                        pe.wait_ge(up_read, ffn_no(L, f, 2 * i + s) - 2)
                    for k in range(KT):
                        if waits:
                            pe.wait_ge(hn_ready, hn_no(L, stage, k))
                        if hook and k == 4:
                            hook()
                        for g in range(2):
                            a_hi, a_lo = wtile(u, g * 1024 + k * P)
                            last = product(ps[:, 2 * s + g, :], a_hi, a_lo, hn_hi[:, k, :], hn_lo[:, k, :],
                                           k == 0, k == KT - 1)
                    last.then_inc(w_used, 1)
                    return last

                def send_rb():
                    pe.wait_ge(r_ready, L * 4 + (1 if f == 0 else 4))
                    broadcast(rtok, 7, rb_done)

                def body(i, where):
                    first = where == "first"
                    up_unit(i, 0, None, first)
                    if first:
                        token_sums(9 + (L * STAGES + stage) * 9, 6)
                    up_unit(i, 1, send_rb if first else None, first)
                up_loop(pe, body)

                def down_body(i, last_two):
                    for b in range(2):
                        m = 2 * i + b
                        pe.wait_ge(h_ready, tile_no(L, stage, m) - 2)
                        for s in range(2):
                            u = dn + 2 * b + s
                            wait_unit(L, u, i, 4)
                            pe.wait_ge(hid_ready, ffn_no(L, f, HK * (s + 1) - 1))
                            for k in range(HK):
                                a_hi, a_lo = wtile(u, k * P)
                                kk = s * HK + k
                                last = product(ps[:, 4 + b, :], a_hi, a_lo, hid_hi[:, kk, :], hid_lo[:, kk, :],
                                               kk == 0, kk == HT - 1)
                            last.then_inc(w_used, 1)
                down_loop(pe, down_body)

            def head_norm(L, hd, part):
                if part == 1:
                    pe.wait_ge(osq_ready, L * 4 + hd + 1)
                    for t in range(ST):
                        last = pe.matmul(ps[:, 3, t:t + 1], tmp[:, 0, t * P:(t + 1) * P], ones[:, 0:1],
                                         start=True, stop=True)
                    last.then_inc(ostat_done, 1)
                if part == 2:
                    pe.wait_ge(rh_ready, L * 4 + hd + 1)
                    broadcast(rh, 3, orb_done)

            def token_unit(L, u, s, bank, n_tok, src_hi, src_lo, stage=None, wait=None):
                wait_unit(L, u)
                for k4 in range(4):
                    k = 4 * s + k4
                    if stage is not None:
                        pe.wait_ge(hn_ready, hn_no(L, stage, k))
                    w1, w2 = wtile(u, k4 * 512, 512)
                    for t in range(n_tok):
                        if wait and k == 0:
                            wait(t)
                        last = product(ps[:, bank + t, :], src_hi[:, k, t * P:(t + 1) * P],
                                       src_lo[:, k, t * P:(t + 1) * P], w1, w2, k == 0, k == KT - 1)
                return last.then_inc(w_used, 1)

            def feature_unit(L, u, bank, ks, src, first=True, last_part=True, before=None):
                for k in ks:
                    if before:
                        before(k)
                    s_hi, s_lo = src(k)
                    for b in range(2):
                        a_hi, a_lo = wtile(u, k * 256 + b * P)
                        last = product(ps[:, bank + b, :], a_hi, a_lo, s_hi, s_lo,
                                       first and k == ks[0], last_part and k == ks[-1])
                return last

            with pe.Fori(0, LAYERS) as L:
                ffn(L, 0, UP1, DN1, 0)

                for s in range(2):
                    token_unit(L, GV + s, s, 0, ST, hn_hi, hn_lo, stage=1)
                token_sums(9 + (L * STAGES + 1) * 9, 7)
                def after_ms(t):
                    if t == 3:
                        pe.wait_ge(ms_ready, L * 4 + 2)
                for s in range(2):
                    token_unit(L, QQ + s, s, 4, ST, hn_hi, hn_lo, wait=after_ms)
                for s in range(2):
                    token_unit(L, KK + s, s, 0, ST, hn_hi, hn_lo,
                               wait=lambda t: pe.wait_ge(gelu_ready, L * 4 + t + 1))
                pe.wait_ge(qk_copied, L * 8 + 4)
                pe.wait_ge(r_ready, L * 4 + 2)
                broadcast(rtok, 4, rb_done)
                pe.wait_ge(ws_masked, L + 1)
                for g in range(HEADS):
                    last = pe.transpose(ps[:, 5, g * P:(g + 1) * P], wsr[:, g, :], ident[:, :])
                last.then_inc(ws_turned, 1)
                hn_tile = lambda k: (hn_hi[:, k, :], hn_lo[:, k, :])
                wait_unit(L, GU)
                last = feature_unit(L, GU, 6, range(KT), hn_tile)
                last.then_inc(w_used, 1)

                def turn(n, tok):
                    t = n % ST
                    pe.wait_ge(qk_roped, L * 8 + n + 1)
                    if n < ST:
                        pe.wait_ge(qk_copied, L * 8 + ST + t + 1)
                    else:
                        pe.wait_ge(qkT_ready, L * 8 + t + 1)
                    for hd in range(HEADS):
                        last = pe.transpose(ps[:, t, hd * P:(hd + 1) * P], tok[:, t, hd * P:(hd + 1) * P], ident[:, :])
                    last.then_inc(qk_turned, 1)

                for t in range(ST):
                    turn(t, q_tok)
                wait_unit(L, GU + 1)
                pe.wait_ge(rb_ready, L * 3 + 2)
                pe.wait_ge(wsT_ready, L + 1)
                last = feature_unit(L, GU + 1, 4, range(KT), hn_tile)
                last.then_inc(w_used, 1)
                for t in range(ST):
                    turn(ST + t, k_tok)
                def mix_chunk(t):
                    pe.wait_ge(vn_ready, L * 4 + t + 1)
                    if t == 0:
                        pe.wait_ge(gu_scaled, L * 2 + 1)
                    if t >= 2:
                        pe.wait_ge(gm_final, L * 4 + t - 1)
                    for g in range(HEADS):
                        c = slice(t * P, (t + 1) * P)
                        last = product(ps[:, 6 + t % 2, g * P:(g + 1) * P], gm_hi[:, g, c], gm_lo[:, g, c],
                                       wsT_hi[:, g, :], wsT_lo[:, g, :], True, True)
                    last.then_inc(mix_done, 1)

                def turn_memory(half):
                    if half == 0:
                        pe.wait_ge(mem_normed, L + 1)
                        pe.wait_ge(gu_scaled, L * 2 + 2)
                    else:
                        pe.wait_ge(mg_ready, L * 8 + 4)
                    for n in range(4):
                        for t in range(MT):
                            c = (n % 2) * M + t * P
                            m = 4 * half + n
                            last = pe.transpose(ps[:, 4 + n // 2, c:c + P], mem_in[:, t, m * P:(m + 1) * P], ident[:, :])
                    last.then_inc(mem_turned, 1)

                mix_chunk(0)
                mix_chunk(1)
                turn_memory(0)
                for s in range(2):
                    token_unit(L, VV + s, s, 0, ST, hn_hi, hn_lo,
                               wait=lambda t: pe.wait_ge(qkT_ready, L * 8 + 4 + t + 1))
                    mix_chunk(2 + s)
                    if s == 0:
                        turn_memory(1)

                def cat_tile(k):
                    return (gm_hi[:, k - 4, :], gm_lo[:, k - 4, :]) if k >= 4 else (qT_hi[:, k, :], qT_lo[:, k, :])

                def attn_out(t, ks):
                    last = feature_unit(L, WO + t, 4 + 2 * t, ks, cat_tile, first=ks[0] == 4, last_part=ks[-1] == 3,
                                        before=lambda k: pe.wait_ge(attn_ready, L * 4 + k + 1) if k < 4 else None)
                    if ks[-1] == 3:
                        last.then_inc(w_used, 1)

                def head_values(hd):
                    pe.wait_ge(wT_ready, L * 16 + 4 * hd + 4)
                    if hd:
                        pe.wait_ge(attn_final, L * 4 + hd)
                    for kb in range(ST):
                        c = slice(hd * P, (hd + 1) * P)
                        last = product(ps[:, 1, kb * P:512], v_hi[:, kb, c], v_lo[:, kb, c],
                                       wT_hi[:, kb, kb * P:512], wT_lo[:, kb, kb * P:512], kb == 0, kb == 3)
                    last.then_inc(pv_done, 1)

                def turn_weights(s):
                    n = s - 1
                    qb, b = n % 4, n % 2
                    pe.wait_ge(attn_w_ready, L * 16 + n + 1)
                    if n:
                        pe.wait_ge(wT_ready, L * 16 + n)
                    for kb in range(qb + 1):
                        last = pe.transpose(ps[:, 0, kb * P:(kb + 1) * P], ex[:, b, 0, kb * P:(kb + 1) * P],
                                            ident[:, :])
                    last.then_inc(attn_w_turned, 1)

                def cross_kv(s):
                    n, c = s // 2, s % 2
                    if c == 0:
                        wait_unit(L, CK + n)
                        if n:
                            pe.wait_ge(kv_ready, L * 8 + n)
                        else:
                            pe.wait_ge(v_ready, L * 4 + 3)
                    for k in range(KT):
                        dst = ps[:, 2, c * M:(c + 1) * M]
                        if n < 4:
                            a_hi, a_lo = wtile(CK + n, k * 256 + c * P)
                            last = product(dst, a_hi, a_lo, mg_hi[:, k, :], mg_lo[:, k, :], k == 0, k == KT - 1)
                        else:
                            b_hi, b_lo = wtile(CK + n, k * 256, 256)
                            m = slice(c * P, (c + 1) * P)
                            last = product(dst, mg_hi[:, k, m], mg_lo[:, k, m], b_hi, b_lo, k == 0, k == KT - 1)
                    if c == 1:
                        last.then_inc(w_used, 1)

                for s in range(19):
                    late = s % 4 == 1 and s > 1
                    if s < 16:
                        hd, qb, b = s // 4, s % 4, s % 2
                        N = (qb + 1) * P
                        if s == 0:
                            pe.wait_ge(mg_ready, L * 8 + 8)
                        if s == 1:
                            pe.wait_ge(gm_final, L * 4 + 4)
                        if s >= 2:
                            pe.wait_ge(exp_done, L * 16 + s - 1)
                        for br in range(2):
                            r = slice(64 * br, 64 * br + 64)
                            bank = 4 + 2 * b + br
                            q = slice(qb * P, (qb + 1) * P)

                            def mask():
                                pe.matmul(ps[:, bank, N - P:N], ident_r[:, :], mask_r[:, :], start=False, stop=False)
                            last = product(ps[:, bank, 0:N], qT_hi[r, hd, q], qT_lo[r, hd, q],
                                           kT_hi[r, hd, 0:N], kT_lo[r, hd, 0:N], True, True, extra=mask)
                        last.then_inc(sc_done, 1)
                    if 1 <= s < 17 and not late:
                        turn_weights(s)
                    if s < 16:
                        cross_kv(s)
                    if late:
                        head_values((s - 5) // 4)
                    if s < 17 and late:
                        turn_weights(s)
                    if s == 16:
                        wait_unit(L, WO)
                        attn_out(0, [4, 5, 6, 7])
                    if s == 17:
                        attn_out(0, [0, 1])
                    if s >= 5:
                        head_norm(L, *divmod(s - 5, 4))

                wait_unit(L, WO + 1)
                attn_out(1, [4, 5])
                head_norm(L, 3, 2)
                attn_out(1, [6, 7])
                attn_out(0, [2, 3])
                attn_out(1, [0, 1, 2, 3])
                for t in range(2, 4):
                    wait_unit(L, WO + t)
                    pe.wait_ge(h_ready, tile_no(L, 1, 2 * t - 3))
                    feature_unit(L, WO + t, 4 + 2 * (t % 2), range(KT), cat_tile).then_inc(w_used, 1)

                def queries(hd, ks=range(KT)):
                    if ks[0] == 0:
                        wait_unit(L, WQ + hd)
                        if hd >= 2:
                            pe.wait_ge(qc_ready, L * 4 + hd - 1)
                    last = feature_unit(L, WQ + hd, 4 + 2 * (hd % 2), ks, hn_tile,
                                        first=ks[0] == 0, last_part=ks[-1] == KT - 1,
                                        before=(lambda k: pe.wait_ge(hn_ready, hn_no(L, 2, k))) if hd == 0 else None)
                    if ks[-1] == KT - 1:
                        last.then_inc(w_used, 1)

                def cross_scores(hd):
                    pe.wait_ge(qc_ready, L * 4 + hd + 1)
                    if hd:
                        pe.wait_ge(cexp_done, L * 4 + hd)
                    else:
                        pe.wait_ge(ms_ready, L * 4 + 3)
                    for qb in range(ST):
                        for d in range(2):
                            q = slice(qb * P, (qb + 1) * P)
                            last = product(ps[:, qb // 2, (qb % 2) * M:(qb % 2 + 1) * M],
                                           qc_hi[:, hd % 2, d, q], qc_lo[:, hd % 2, d, q],
                                           kc_hi[:, 2 * hd + d, :], kc_lo[:, 2 * hd + d, :], d == 0, d == 1)
                    last.then_inc(csc_done, 1)

                def cross_turn(hd):
                    pe.wait_ge(cw_ready, L * 4 + hd + 1)
                    if hd:
                        pe.wait_ge(o_ready, L * 4 + hd)
                    for t in range(MT):
                        for qb in range(ST):
                            c0 = (qb % 2) * M + t * P
                            last = pe.transpose(ps[:, 2 + t, qb * P:(qb + 1) * P], tmp[:, qb // 2, c0:c0 + P], ident[:, :])
                    last.then_inc(cw_turned, 1)

                def cross_values(hd):
                    pe.wait_ge(wc_ready, L * 4 + hd + 1)
                    for d in range(2):
                        for t in range(MT):
                            c = slice(d * P, (d + 1) * P)
                            last = product(ps[:, 2 + d, :], vc_hi[hd][:, t, c], vc_lo[hd][:, t, c],
                                           wc_hi[:, t, :], wc_lo[:, t, :], t == 0, t == 1)
                    last.then_inc(cpv_done, 1)

                def cross_out(t, ks):
                    if ks[0] == 0:
                        wait_unit(L, CO + t)
                        pe.wait_ge(qc_ready, L * 4 + 3 + t)
                    last = feature_unit(L, CO + t, 4 + 2 * t, ks, lambda k: (o_hi[:, k, :], o_lo[:, k, :]),
                                        first=ks[0] == 0, last_part=ks[-1] == 7,
                                        before=lambda k: pe.wait_ge(o_ready, L * 4 + k // 2 + 1))
                    if ks[-1] == 7:
                        last.then_inc(w_used, 1)

                queries(0)
                token_sums(9 + (L * STAGES + 2) * 9, 0)
                queries(1)
                cross_scores(0)
                queries(2)
                cross_turn(0)
                cross_scores(1)
                queries(3, range(4))
                cross_values(0)
                queries(3, range(4, KT))
                cross_turn(1)
                cross_scores(2)
                cross_values(1)
                cross_out(0, [0, 1])
                cross_out(1, [0])
                cross_turn(2)
                cross_scores(3)
                cross_values(2)
                cross_out(1, [1])
                cross_out(0, [2, 3])
                cross_turn(3)
                cross_out(1, [2, 3])
                cross_values(3)
                cross_out(0, [4, 5])
                cross_out(0, [6, 7])
                cross_out(1, [4, 5, 6, 7])
                for t in range(2, 4):
                    wait_unit(L, CO + t)
                    pe.wait_ge(h_ready, tile_no(L, 2, 2 * t - 3))
                    feature_unit(L, CO + t, 4 + 2 * (t % 2), range(KT), lambda k: (o_hi[:, k, :], o_lo[:, k, :]))\
                        .then_inc(w_used, 1)

                ffn(L, 1, UP2, DN2, 3)

            def fin_turn(t, m):
                c = slice(t * P, (t + 1) * P)
                dst = ps[:, FIN_BANK[t] + m // 4, (m % 4) * P:(m % 4 + 1) * P]
                pe.matmul(dst, hn_hi[:, m, c], ident_r[:, :], start=True, stop=False)
                return pe.matmul(dst, hn_lo[:, m, c], ident_r[:, :], start=False, stop=True)

            for m in range(KT):
                pe.wait_ge(hn_ready, hn_no(LAYERS, 0, m))
                for t in range(2):
                    last = fin_turn(t, m)
            last.then_inc(fin_turned, 1)
            token_sums(9 + LAYERS * STAGES * 9, 4)
            for t in (2, 3):
                if t == 3:
                    pe.wait_ge(ms_ready, LAYERS * 4 + 1)
                for m in range(KT):
                    last = fin_turn(t, m)
                last.then_inc(fin_turned, 1)


_INS = ['x', 'mem', 'positions', 'ffn1_norm', 'ffn1_wgu', 'ffn1_wd', 'mix_norm', 'w_in', 'lam_q1', 'lam_k1',
        'lam_q2', 'lam_k2', 'subln', 'gmlp_ln_g', 'gmlp_ln_b', 'gmlp_ws', 'gmlp_bs', 'w_out', 'cross_norm',
        'mem_norm', 'cross_wq', 'cross_wkv', 'cross_wo', 'ffn2_norm', 'ffn2_wgu', 'ffn2_wd', 'final_norm']


def kernel(**inputs):
    import numpy as _np
    import concourse.bacc as _bacc
    from concourse import mybir as _mybir
    from concourse.bass_utils import run_bass_kernel_spmd as _run

    nc = _bacc.Bacc("TRN2", target_bir_lowering=False, num_devices=1)
    arrays, args = {}, []
    for name in _INS:
        a = _np.ascontiguousarray(inputs[name])
        arrays[f"in_{name}_dram"] = a
        args.append(nc.dram_tensor(f"in_{name}_dram", a.shape, _mybir.dt.from_np(a.dtype), kind="ExternalInput").ap())
    args.append(nc.dram_tensor("out_dram", (1, S, D), _mybir.dt.float32, kind="ExternalOutput").ap())
    macaron_kernel(nc, *args)
    r = _run(nc, [arrays], core_ids=[0])
    return r.results[0]["out_dram"]
```
